# Optimizing a Trainium2 kernel written in Bass

```python
import jax
import jax.numpy as jnp
from jax import lax
import numpy as np

D_MODEL = 1024
BATCH = 1
SEQ = 1024
DEPTH = 2

GRID_W = 64
CTX_LEN = 256
SSD_D_INNER = D_MODEL
SSD_HEAD_DIM = 64
SSD_HEADS = SSD_D_INNER // SSD_HEAD_DIM
SSD_GROUPS = 2
SSD_STATE = 128
SSD_CONV = 5
SSD_CHUNK = 128
SSD_XBC = SSD_D_INNER + 2 * SSD_GROUPS * SSD_STATE
SG_WIDTH = D_MODEL
SG_CHUNK = 128
SG_GROUP_DIM = 128
SG_GROUPS = SG_WIDTH // SG_GROUP_DIM
ROWS_PER_CHUNK = SG_CHUNK // GRID_W
MIX_WIDTH = SSD_D_INNER + SG_WIDTH
IN_PROJ = SSD_D_INNER + SSD_XBC + 2 * SSD_HEADS + 2 * SG_WIDTH
CONF_WIDTH = D_MODEL
CONF_CONV_WIDTH = 31
MLP_HIDDEN = 4 * D_MODEL
EPS = 1e-6

kernel_name = "hybrid_ssd_gmlp_conformer_dit"

def rmsnorm(x, g):
    xf = x.astype(jnp.float32)
    y = xf * lax.rsqrt(jnp.mean(xf * xf, axis=-1, keepdims=True) + EPS)
    return (y * g.astype(jnp.float32)).astype(x.dtype)

def layernorm(x, g, b):
    xf = x.astype(jnp.float32)
    mu = jnp.mean(xf, axis=-1, keepdims=True)
    xc = xf - mu
    y = xc * lax.rsqrt(jnp.mean(xc * xc, axis=-1, keepdims=True) + EPS)
    return (y * g.astype(jnp.float32) + b.astype(jnp.float32)).astype(x.dtype)

def modulate(x, g, shift, scale):
    return rmsnorm(x, g) * (1 + scale) + shift

def dwconv_centred(x, w, b):
    k = w.shape[0]
    y = lax.conv_general_dilated(
        x, w[:, None, :].astype(x.dtype), window_strides=(1,),
        padding=[(k // 2, k // 2)], dimension_numbers=('NWC', 'WIO', 'NWC'),
        feature_group_count=x.shape[-1])
    return y + b.astype(x.dtype)

def ssd_chunked(x, dt, a, bm, cm, h0):
    f32 = jnp.float32
    bsz, seq_len, n_heads, p_dim = x.shape
    n_groups, n_state = bm.shape[-2], bm.shape[-1]
    r = n_heads // n_groups
    nc = seq_len // SSD_CHUNK
    xc = x.astype(f32).reshape(bsz, nc, SSD_CHUNK, n_groups, r, p_dim)
    dtc = dt.reshape(bsz, nc, SSD_CHUNK, n_groups, r)
    bc = bm.astype(f32).reshape(bsz, nc, SSD_CHUNK, n_groups, n_state)
    cc = cm.astype(f32).reshape(bsz, nc, SSD_CHUNK, n_groups, n_state)
    acs = jnp.cumsum(dtc * a.astype(f32).reshape(n_groups, r), axis=2)
    lower = jnp.tril(jnp.ones((SSD_CHUNK, SSD_CHUNK), dtype=bool))[:, :, None, None]
    seg = acs[:, :, :, None] - acs[:, :, None, :]
    decay = jnp.exp(jnp.where(lower, seg, -jnp.inf))
    scores = jnp.einsum('bcign,bcjgn->bcijg', cc, bc)
    w = scores[..., None] * decay * dtc[:, :, None]
    y_diag = jnp.einsum('bcijgr,bcjgrp->bcigrp', w, xc)
    to_end = jnp.exp(acs[:, :, -1:] - acs) * dtc
    states = jnp.einsum('bcjgn,bcjgrp->bcgrpn', bc, xc * to_end[..., None])
    chunk_decay = jnp.exp(acs[:, :, -1])

    def step(h, inp):
        s, d = inp
        return h * d[..., None, None] + s, h

    h_last, h_in = lax.scan(step, h0, (jnp.moveaxis(states, 1, 0),
                                       jnp.moveaxis(chunk_decay, 1, 0)))
    h_in = jnp.moveaxis(h_in, 0, 1)
    y_off = jnp.einsum('bcign,bcgrpn->bcigrp', cc, h_in) * jnp.exp(acs)[..., None]
    y = (y_diag + y_off).reshape(bsz, seq_len, n_heads, p_dim).astype(x.dtype)
    return y, h_last

def ssd_bidirectional(xs, dt_f, dt_b, a_f, a_b, bm, cm, h0_f, h0_b):
    flip = lambda t: jnp.flip(t, axis=1)
    y_f, h_f = ssd_chunked(xs, dt_f, a_f, bm, cm, h0_f)
    y_b, h_b = ssd_chunked(flip(xs), flip(dt_b), a_b, flip(bm), flip(cm), h0_b)
    return y_f + flip(y_b), h_f, h_b

def hybrid_mixer(u, n_chunks, h0_f, h0_b, w_in, conv_w, conv_b, dt_bias, a_log, d_skip,
                 ssd_norm_g, sg_ln_g, sg_ln_b, sg_w, sg_b, w_out):
    bsz, seq_len, _ = u.shape
    proj = u @ w_in
    o1 = SSD_D_INNER
    o2 = o1 + SSD_XBC
    o3 = o2 + 2 * SSD_HEADS
    z, xbc, dt_raw, uv = jnp.split(proj, [o1, o2, o3], axis=-1)
    xbc = jax.nn.silu(dwconv_centred(xbc, conv_w, conv_b))
    xs, bm, cm = jnp.split(xbc, [SSD_D_INNER, SSD_D_INNER + SSD_GROUPS * SSD_STATE], axis=-1)
    xs = xs.reshape(bsz, seq_len, SSD_HEADS, SSD_HEAD_DIM)
    bm = bm.reshape(bsz, seq_len, SSD_GROUPS, SSD_STATE)
    cm = cm.reshape(bsz, seq_len, SSD_GROUPS, SSD_STATE)
    dt = jax.nn.softplus(dt_raw.astype(jnp.float32).reshape(bsz, seq_len, 2, SSD_HEADS)
                         + dt_bias.astype(jnp.float32))
    a = -jnp.exp(a_log.astype(jnp.float32))
    y, h_f, h_b = ssd_bidirectional(xs, dt[:, :, 0], dt[:, :, 1], a[0], a[1], bm, cm, h0_f, h0_b)
    y = y + d_skip[:, None].astype(y.dtype) * xs
    y = y.reshape(bsz, seq_len, SSD_D_INNER) * jax.nn.silu(z)
    y_ssd = rmsnorm(y.reshape(bsz, seq_len, SSD_GROUPS, -1),
                    ssd_norm_g.reshape(SSD_GROUPS, -1)).reshape(bsz, seq_len, SSD_D_INNER)
    gate_u, v = jnp.split(jax.nn.gelu(uv), 2, axis=-1)
    v = layernorm(v, sg_ln_g, sg_ln_b).reshape(bsz, n_chunks, SG_CHUNK, SG_GROUPS, SG_GROUP_DIM)
    s = jnp.einsum('gqk,bnkgc->bnqgc', sg_w, v) + sg_b.T[:, :, None]
    y_sg = gate_u * s.reshape(bsz, seq_len, SG_WIDTH)
    out = jnp.concatenate([y_ssd, y_sg], axis=-1) @ w_out
    return out, h_f, h_b

def conformer_conv(u, w_pw1, b_pw1, w_dw, b_dw, ln_g, ln_b, w_pw2, b_pw2):
    a = u @ w_pw1 + b_pw1
    a = a[..., :CONF_WIDTH] * jax.nn.sigmoid(a[..., CONF_WIDTH:])
    a = dwconv_centred(a, w_dw, b_dw)
    a = jax.nn.silu(layernorm(a, ln_g, ln_b))
    return a @ w_pw2 + b_pw2

def sq_relu_mlp(u, w1, w2):
    return jnp.square(jax.nn.relu(u @ w1)) @ w2

def setup_inputs(seed: int = 0) -> dict:
    key = jax.random.key(seed)
    ks = jax.random.split(key, 40)
    n_even = (DEPTH + 1) // 2
    n_odd = DEPTH // 2
    nrm = lambda k, shape, s: jax.random.normal(k, shape, jnp.float32) * s
    gain = lambda k, shape: 1.0 + 0.05 * jax.random.normal(k, shape, jnp.float32)
    dt0 = jnp.exp(jax.random.uniform(ks[13], (n_even, 2, SSD_HEADS), jnp.float32,
                                     np.log(1e-3), np.log(1e-1)))
    return {
        "x": nrm(ks[0], (BATCH, SEQ, D_MODEL), 1.0),
        "c": nrm(ks[1], (BATCH, D_MODEL), 1.0),
        "ctx": nrm(ks[2], (BATCH, CTX_LEN, D_MODEL), 1.0),
        "c_ctx": nrm(ks[3], (D_MODEL,), 1.0),
        "ada_w": nrm(ks[4], (DEPTH, D_MODEL, 6 * D_MODEL), 0.5 * D_MODEL ** -0.5),
        "ada_b": nrm(ks[5], (DEPTH, 6 * D_MODEL), 0.02),
        "norm_mix_g": gain(ks[6], (DEPTH, D_MODEL)),
        "norm_mlp_g": gain(ks[7], (DEPTH, D_MODEL)),
        "mlp_w1": nrm(ks[8], (DEPTH, D_MODEL, MLP_HIDDEN), D_MODEL ** -0.5),
        "mlp_w2": nrm(ks[9], (DEPTH, MLP_HIDDEN, D_MODEL), MLP_HIDDEN ** -0.5),
        "hy_w_in": nrm(ks[10], (n_even, D_MODEL, IN_PROJ), D_MODEL ** -0.5),
        "ssd_conv_w": nrm(ks[11], (n_even, SSD_CONV, SSD_XBC), SSD_CONV ** -0.5),
        "ssd_conv_b": nrm(ks[12], (n_even, SSD_XBC), 0.02),
        "ssd_dt_bias": dt0 + jnp.log(-jnp.expm1(-dt0)),
        "ssd_a_log": jnp.log(jax.random.uniform(ks[14], (n_even, 2, SSD_HEADS), jnp.float32, 1.0, 16.0)),
        "ssd_d": 1.0 + 0.1 * jax.random.normal(ks[15], (n_even, SSD_HEADS), jnp.float32),
        "ssd_norm_g": gain(ks[16], (n_even, SSD_D_INNER)),
        "sg_ln_g": gain(ks[17], (n_even, SG_WIDTH)),
        "sg_ln_b": nrm(ks[18], (n_even, SG_WIDTH), 0.02),
        "sg_w": nrm(ks[19], (n_even, SG_GROUPS, SG_CHUNK, SG_CHUNK), 0.5 * SG_CHUNK ** -0.5),
        "sg_b": gain(ks[20], (n_even, SG_GROUPS, SG_CHUNK)),
        "hy_w_out": nrm(ks[21], (n_even, MIX_WIDTH, D_MODEL), MIX_WIDTH ** -0.5),
        "cf_w_pw1": nrm(ks[22], (n_odd, D_MODEL, 2 * CONF_WIDTH), D_MODEL ** -0.5),
        "cf_b_pw1": nrm(ks[23], (n_odd, 2 * CONF_WIDTH), 0.02),
        "cf_w_dw": nrm(ks[24], (n_odd, CONF_CONV_WIDTH, CONF_WIDTH), CONF_CONV_WIDTH ** -0.5),
        "cf_b_dw": nrm(ks[25], (n_odd, CONF_WIDTH), 0.02),
        "cf_ln_g": gain(ks[26], (n_odd, CONF_WIDTH)),
        "cf_ln_b": nrm(ks[27], (n_odd, CONF_WIDTH), 0.02),
        "cf_w_pw2": nrm(ks[28], (n_odd, CONF_WIDTH, D_MODEL), CONF_WIDTH ** -0.5),
        "cf_b_pw2": nrm(ks[29], (n_odd, D_MODEL), 0.02),
        "final_norm_g": gain(ks[30], (D_MODEL,)),
    }

def reference(x, c, ctx, c_ctx, ada_w, ada_b, norm_mix_g, norm_mlp_g, mlp_w1, mlp_w2,
              hy_w_in, ssd_conv_w, ssd_conv_b, ssd_dt_bias, ssd_a_log, ssd_d, ssd_norm_g,
              sg_ln_g, sg_ln_b, sg_w, sg_b, hy_w_out, cf_w_pw1, cf_b_pw1, cf_w_dw, cf_b_dw,
              cf_ln_g, cf_ln_b, cf_w_pw2, cf_b_pw2, final_norm_g):
    bsz = x.shape[0]
    rows = x.shape[1] // GRID_W
    lat_chunks = rows // ROWS_PER_CHUNK
    ctx_chunks = ctx.shape[1] // SG_CHUNK
    silu_c = jax.nn.silu(c)[:, None, :]
    silu_cc = jax.nn.silu(c_ctx)[None, None, :]
    h, hc = x, ctx
    for i in range(DEPTH):
        ctx_needed = i < DEPTH - 1
        sh1, sc1, g1, sh2, sc2, g2 = jnp.split(silu_c @ ada_w[i] + ada_b[i], 6, axis=-1)
        csh1, csc1, cg1, csh2, csc2, cg2 = jnp.split(silu_cc @ ada_w[i] + ada_b[i], 6, axis=-1)
        j = i // 2
        if i % 2 == 0:
            p = (hy_w_in[j], ssd_conv_w[j], ssd_conv_b[j], ssd_dt_bias[j], ssd_a_log[j], ssd_d[j],
                 ssd_norm_g[j], sg_ln_g[j], sg_ln_b[j], sg_w[j], sg_b[j], hy_w_out[j])
            zeros = jnp.zeros((bsz, SSD_GROUPS, SSD_HEADS // SSD_GROUPS, SSD_HEAD_DIM, SSD_STATE),
                              jnp.float32)
            ctx_mix, h0_f, h0_b = hybrid_mixer(modulate(hc, norm_mix_g[i], csh1, csc1),
                                               ctx_chunks, zeros, zeros, *p)
            lat_mix, _, _ = hybrid_mixer(modulate(h, norm_mix_g[i], sh1, sc1),
                                         lat_chunks, h0_f, h0_b, *p)
            h = h + g1 * lat_mix
            if ctx_needed:
                hc = hc + cg1 * ctx_mix
        else:
            p = (cf_w_pw1[j], cf_b_pw1[j], cf_w_dw[j], cf_b_dw[j], cf_ln_g[j], cf_ln_b[j],
                 cf_w_pw2[j], cf_b_pw2[j])
            h = h + g1 * conformer_conv(modulate(h, norm_mix_g[i], sh1, sc1), *p)
            if ctx_needed:
                hc = hc + cg1 * conformer_conv(modulate(hc, norm_mix_g[i], csh1, csc1), *p)
        h = h + g2 * sq_relu_mlp(modulate(h, norm_mlp_g[i], sh2, sc2), mlp_w1[i], mlp_w2[i])
        if ctx_needed:
            hc = hc + cg2 * sq_relu_mlp(modulate(hc, norm_mlp_g[i], csh2, csc2), mlp_w1[i], mlp_w2[i])
    return rmsnorm(h, final_norm_g)


_drawn_inputs = setup_inputs


def setup_inputs(seed=0):
    import zlib

    import numpy as np

    out = dict(_drawn_inputs(seed))
    spreads = {}
    factors = {'ctx': 7.752,
     'c_ctx': 7.99,
     'norm_mix_g': 2.707,
     'ssd_conv_b': 22.959,
     'ssd_d': 176.421,
     'ssd_norm_g': 21.092,
     'sg_ln_g': 25.574,
     'sg_ln_b': 52.484,
     'sg_b': 7.448,
     'cf_b_pw1': 21.417,
     'cf_b_dw': 8.0,
     'cf_ln_g': 104.636,
     'cf_ln_b': 200.0,
     'cf_b_pw2': 191.16,
     'norm_mlp_g': 6.595}
    for name, (base, spread) in spreads.items():
        noise = np.random.default_rng([zlib.crc32(name.encode()), seed]).standard_normal(out[name].shape)
        drawn = base * np.exp(spread * noise) if base else spread * noise
        out[name] = jnp.asarray(drawn.astype(out[name].dtype))
    for name, factor in factors.items():
        out[name] = (out[name] * factor).astype(out[name].dtype)
    return out
```

```python
from contextlib import ExitStack, contextmanager

import concourse.bass as bass
from concourse import mybir

P = 128
F32 = mybir.dt.float32
F32R = mybir.dt.float32r
ALU = mybir.AluOpType
ACT = mybir.ActivationFunctionType

D = 1024
TOK = 1024
CTX = 256
ALL = TOK + CTX
KT = D // P
HALF = 512
SEGS = [(0, HALF), (HALF, HALF), (TOK, CTX)]
NCH = TOK // P
NCX = CTX // P
NALL = NCH + NCX
XBC = 1536
XBT = XBC // P
HEADS = 16
HD = 64
HID = 4096
EPS = 1e-6
BIG = 1e30
UNIT = 2048
CONV = 5
CW = 31
PADW = 1288
CONF_PAD = 1056


class Lin:

    def __init__(self, c, step=0, i=None):
        self.c, self.step, self.i = c, step, i

    def plus(self, k):
        return Lin(self.c + k, self.step, self.i)

    def value(self, mul=1, add=0):
        v = self.c * mul + add
        return self.i * (self.step * mul) + v if self.step else v


class Program:

    def __init__(self, eng, names, start):
        self.e, self.step = eng, names
        self.cnt = {n: Lin(start.get(n, 0)) for n in names}

    def begun(self, name, k=0):
        v = self.cnt[name].plus(k)
        return v.step != 0 or v.c > 0

    def so_far(self, name, k=0):
        assert self.begun(name, k), name
        return self.cnt[name].plus(k).value(self.step[name])

    def skip(self, name, k=1):
        self.cnt[name] = self.cnt[name].plus(k)

    def after(self, name, k=1):
        self.skip(name, k)
        return self.so_far(name)

    def counted(self, name):
        self.skip(name)
        return self.step[name]

    @contextmanager
    def loop(self, n, per):
        start = {k: v.c for k, v in self.cnt.items()}
        with self.e.Fori(0, n) as i:
            for k, step in per.items():
                self.cnt[k] = Lin(start[k], step, i)
            yield i
        moved = {k: v.c - start[k] for k, v in self.cnt.items() if v.c != start[k]}
        assert moved == {k: v for k, v in per.items() if v}, f"signals in a turn: {moved}"
        for k in self.cnt:
            self.cnt[k] = Lin(start[k] + n * per.get(k, 0))


def build(nc, a, out):
    dram = lambda n, s: nc.dram_tensor(n, s, F32, kind="Internal").ap()
    xbcT = dram("scr_xbcT", [XBC, ALL])
    xtokD = dram("scr_xtok", [ALL, XBC])
    zT = dram("scr_zT", [D, TOK])
    guT = dram("scr_guT", [D, TOK])
    vtok = dram("scr_vtok", [TOK, D])
    acsD = dram("scr_acs", [2 * HEADS, ALL])

    stack = ExitStack()
    with stack:
        def sb(name, shape, dt=F32, at=stack):
            return at.enter_context(nc.sbuf_tensor(name, shape, dt))

        hT = sb("hT", [P, KT, TOK])
        raw = [sb(f"raw{i}", [P, UNIT]) for i in range(2)]
        wh = [sb(f"wh{i}", [P, UNIT], F32R) for i in range(2)]
        wl = [sb(f"wl{i}", [P, UNIT], F32R) for i in range(2)]
        ident = sb("ident", [P, P])
        ones = sb("ones", [P, P])
        maskF = sb("maskF", [P, P])
        maskB = sb("maskB", [P, P])
        mod = sb("mod", [P, 2, 48, 2])
        gsc = sb("gsc", [P, 6, KT])
        csil = sb("csil", [P, 16])
        G = ExitStack()
        adaw = [sb(f"adaw{i}", [P, D], at=G) for i in range(2)]
        G.close()
        sacc = sb("sacc", [P, HALF])
        rs = [sb("rs0", [P, HALF])]
        tm = [sb(f"tm{i}", [P, HALF]) for i in range(2)]
        sq = [sb(f"sq{i}", [P, HALF]) for i in range(2)]
        uf = [sb(f"uf{i}", [P, HALF]) for i in range(2)]
        PG = stack.enter_context(nc.psum_tensor("PG", [P, 4, 512], F32))
        PM = stack.enter_context(nc.psum_tensor("PM", [P, 4, 512], F32))

        rows = {}
        place = []
        n_rows = 0

        def add_rows(name, ap, r):
            nonlocal n_rows
            rows[name] = n_rows
            s = 0
            while s < r:
                k = min(r - s, P - n_rows % P)
                place.append((n_rows // P, n_rows % P, k, ap, s))
                n_rows += k
                s += k

        vec = lambda ap: ap.rearrange("(r p) -> r p", p=P)
        add_rows("c", vec(a["c"].rearrange("a d -> (a d)")), KT)
        add_rows("c_ctx", vec(a["c_ctx"]), KT)
        add_rows("ada_b", vec(a["ada_b"].rearrange("a d -> (a d)")), 96)
        add_rows("mix_g", vec(a["norm_mix_g"].rearrange("a d -> (a d)")), 2 * KT)
        add_rows("mlp_g", vec(a["norm_mlp_g"].rearrange("a d -> (a d)")), 2 * KT)
        add_rows("ssd_g", vec(a["ssd_norm_g"].rearrange("a d -> (a d)")), KT)
        add_rows("ln_g", vec(a["cf_ln_g"].rearrange("a d -> (a d)")), KT)
        add_rows("ln_b", vec(a["cf_ln_b"].rearrange("a d -> (a d)")), KT)
        add_rows("b_dw", vec(a["cf_b_dw"].rearrange("a d -> (a d)")), KT)
        add_rows("b_pw1", vec(a["cf_b_pw1"].rearrange("a d -> (a d)")), 2 * KT)
        add_rows("b_pw2", vec(a["cf_b_pw2"].rearrange("a d -> (a d)")), KT)
        add_rows("conv_b", vec(a["ssd_conv_b"].rearrange("a d -> (a d)")), XBT)
        add_rows("conv_w", vec(a["ssd_conv_w"].rearrange("a t d -> (a t d)")), CONV * XBT)
        add_rows("w_dw", vec(a["cf_w_dw"].rearrange("a t d -> (a t d)")), CW * KT)
        NB = (n_rows + P - 1) // P
        par = sb("par", [P, NB, P])

        def col(name, k=0, n=1):
            return par[:, :, :].rearrange("p b q -> p (b q)")[:, rows[name] + k:rows[name] + k + n]

        def cold(name, k):
            return par[:, :, :].rearrange("p b q -> p (b q)")[:, bass.ds(k + rows[name], 1)]

        R32 = 2 * HEADS
        alog = sb("alog", [R32, 1])
        dtb = sb("dtb", [R32, 1])
        a_bc = sb("a_bc", [P, R32])
        d_bc = sb("d_bc", [P, HEADS])
        dsk = sb("dsk", [P, KT])

        A = ExitStack()
        uh = sb("uh", [P, KT, ALL], F32R, A)
        ul = sb("ul", [P, KT, ALL], F32R, A)
        A1 = ExitStack()
        hcT = sb("hcT", [P, KT, CTX], at=A1)
        xin = [sb(f"xin{i}", [P, D], at=A1) for i in range(2)]
        prow = sb("prow", [P, NB, P], at=A1)
        A1.close()
        zo = sq + uf
        A2 = ExitStack()
        xp = [sb(f"xp{i}", [P, PADW], at=A2) for i in range(2)]
        cv = sb("cv", [P, PADW], at=A2)
        xs = sb("xs", [P, ALL], at=A2)
        xtk = sb("xtk", [P, NALL, P], at=A2)
        A2.close()
        A3 = ExitStack()
        rwx, rwe, rwq, rwp, rwdt = [sb(f"row_{n}", [R32, ALL], at=A3) for n in ("x", "e", "q", "p", "dt")]
        A3.close()
        A.close()

        B = ExitStack()
        yT = sb("yT", [P, KT, TOK], at=B)
        B1 = ExitStack()
        tab = sb("tab", [P, NALL, 2, 4, HEADS], at=B1)
        B2 = ExitStack()
        dAt = sb("dAt", [P, NALL, R32], at=B2)
        te = sb("te", [P, NALL, R32], at=B2)
        B2.close()
        bcT = [sb(f"bcT{i}", [P, 4, P], at=B1) for i in range(2)]
        xtb = [sb(f"xtb{i}", [P, D + 2 * P], at=B1) for i in range(2)]
        Abc = [sb(f"Abc{i}", [P, HEADS, P], at=B1) for i in range(2)]
        Eb = [sb(f"Eb{i}", [P, HEADS, P], at=B1) for i in range(2)]
        Wb = sb("Wb", [P, HEADS, P], at=B1)
        xte = sb("xte", [P, D], at=B1)
        st = [sb(f"st{i}", [P, D], at=B1) for i in range(2)]
        scal = sb("scal", [P, 4, HEADS], at=B1)
        B1.close()
        yh = sb("yh", [P, KT, TOK], F32R, B)
        yl = sb("yl", [P, KT, TOK], F32R, B)
        ld = [sb(f"ld{i}", [P, TOK], at=B) for i in range(2)]
        B.close()

        C = ExitStack()
        vln = sb("vln", [P, NCH, D], at=C)
        yh2 = sb("yh2", [P, KT, TOK], F32R, C)
        yl2 = sb("yl2", [P, KT, TOK], F32R, C)
        gu = sq
        lnrow = sb("lnrow", [P, D], at=C)
        sgwT = sb("sgwT", [P, KT, P], at=C)
        bst = sb("bst", [P, 2, 6], at=C)
        mv = sb("mv", [P, NCH, 2], at=C)
        rstd = sb("rstd", [P, NCH, 1], at=C)
        sgb = lambda g: (sacc, rs[0])[g // 4][0:1, (g % 4) * P:(g % 4 + 1) * P]
        C.close()

        Dx = ExitStack()
        vh = sb("vh", [P, KT, TOK], F32R, Dx)
        vl = sb("vl", [P, KT, TOK], F32R, Dx)
        D1 = ExitStack()
        hh = sb("hh", [P, 4, TOK], F32R, D1)
        hl = sb("hl", [P, 4, TOK], F32R, D1)
        D1.close()
        D2 = ExitStack()
        cT = sb("cT", [P, KT, TOK], at=D2)
        apad = [sb(f"apad{i}", [P, CONF_PAD], at=D2) for i in range(2)]
        gb = sb("gb", [P, KT], at=D2)
        D2.close()
        D3 = ExitStack()
        fg = sb("fg", [P, D], at=D3)
        fo = [sb(f"fo{i}", [P, D], at=D3) for i in range(2)]
        fs = sb("fs", [P, D], at=D3)
        fm = sb("fm", [P, NCH, 1], at=D3)
        D3.close()
        Dx.close()

        names = {}
        for n in ("const_ready", "group_done", "read_by_act", "read_by_dve", "split_begun", "split_hi",
                  "par_turned", "par_ready", "skip_ready", "silu_c", "mod_ready",
                  "sq_ready", "sq_added", "stat_done", "ln_done", "rstd_ready", "norm_mul", "uf_ready", "u_hi", "u_lo",
                  "pads_ready", "conv_step", "conv_done", "xs_ready", "xt_turned", "xt_copied",
                  "row_act", "row_dve", "tab_turned", "tot_done", "tab_dve", "tab_act",
                  "scal_ready", "seg_ready", "E_ready", "D_exp", "CE_ready", "xdt_ready", "xte_ready", "scores_done",
                  "W_ready", "S_done", "state_mul", "state_ready", "y_done", "step_done",
                  "fin_dve", "v_dve", "v_act", "v_ready", "sg_hi", "sg_lo",
                  "relu_sq", "hid_hi", "hid_lo", "glu_done", "dw_step", "dw_done", "mean_done", "ln_dve", "bias_added",
                  "out_dve", "out_act"):
            names[n] = 1
        for i in range(2):
            names[f"raw_empty{i}"] = 1
            names[f"ada_empty{i}"] = 1
            names[f"split_full{i}"] = 1
            for n in ("raw_full", "ada_full", "xin_full", "step_full", "gu_full"):
                names[f"{n}{i}"] = 16
        for i in range(4):
            names[f"zo_stored{i}"] = 16
            names[f"ld_full{i}"] = 16
        for n in ("par_loaded", "rec_loaded", "xs_stored", "xt_stored", "acs_stored", "acs_loaded", "v_loaded", "sg_loaded",
                  "fg_loaded", "out_stored0", "out_stored1"):
            names[n] = 16
        sem = {n: stack.enter_context(nc.semaphore(n)) for n in names}
        credit = {"read_by_act": 4, "read_by_dve": 4, "raw_empty0": 1, "raw_empty1": 1,
                  "ada_empty0": 1, "ada_empty1": 1, "step_done": 2, "W_ready": 2,
                  "relu_sq": 2, "zo_stored0": 1, "zo_stored1": 1, "zo_stored2": 1, "zo_stored3": 1}
        mirrored = {n: k for n, k in credit.items() if "_empty" not in n}
        marks = {}
        SHARED = ("group_done", "read_by_act", "read_by_dve")

        block = stack.enter_context(nc.Block())

        w_ada = [a["ada_w"][l].rearrange("(k p) n -> p k n", p=P) for l in range(2)]
        w_in = a["hy_w_in"][0].rearrange("(k p) n -> p k n", p=P)
        w_out = a["hy_w_out"][0].rearrange("(k p) n -> p k n", p=P)
        w_m1 = [a["mlp_w1"][l].rearrange("(k p) n -> p k n", p=P) for l in range(2)]
        w_m2 = [a["mlp_w2"][l].rearrange("(k p) n -> p k n", p=P) for l in range(2)]
        w_p1 = a["cf_w_pw1"][0].rearrange("(k p) n -> p k n", p=P)
        w_p2 = a["cf_w_pw2"][0].rearrange("(k p) n -> p k n", p=P)
        Z0, X0, T0, U0 = 0, D, D + XBC, D + XBC + 2 * HEADS
        V0 = U0 + D

        N_ADA0 = 2 * D // 256
        N_XBC = XBC // 256

        class Stream:

            def __init__(self):
                self.raw = self.split = 0

            @contextmanager
            def loop(self, p, n, gemms, per):
                raw0, split0 = self.raw, self.split
                with p.loop(n, per) as i:
                    yield i
                assert self.raw - raw0 == gemms and self.split - split0 == gemms
                self.raw, self.split = raw0 + n * gemms, split0 + n * gemms

        def walk(p, S, per, gemm, ada, later_ada, after_v, stage=lambda name: None):
            for u in range(N_ADA0):
                ada(w_ada[0], u * 256, 256)
            stage("xbc")
            for u in range(N_XBC):
                gemm(w_in, 0, 8, X0 + u * 256, 256, 6)
            gemm(w_in, 0, 8, T0, P, 3)
            for c0, m0 in ((Z0, 2048), (U0, 4096)):
                with S.loop(p, 2, 2, per(2, 8)) as i:
                    for j in range(2):
                        gemm(w_in, 0, 8, i * 512 + (c0 + j * 256), 256, 4)
                    for q in range(8):
                        later_ada(w_ada[0], i * 1024 + (m0 + q * P), q, 3 * KT)
            with S.loop(p, 2, 2, per(2, 0)) as i:
                for j in range(2):
                    gemm(w_in, 0, 8, i * 512 + (V0 + j * 256), 256, 4)
            after_v()
            for k0 in (0, 8):
                stage("out" if k0 == 0 else "out2")
                with S.loop(p, 2, 2, per(2, 0)) as i:
                    for j in range(2):
                        gemm(w_out, k0, 8, i * 512 + j * 256, 256, 4)
            for l in range(2):
                adas = 6 if l == 0 else 0
                with S.loop(p, 8, 4, per(4, adas)) as i:
                    for j in range(2):
                        gemm(w_m1[l], 0, 8, i * 512 + j * 256, 256, 4)
                    for q in range(adas):
                        later_ada(w_ada[1], i * 768 + q * P, q, 7 * KT)
                    for j in range(2):
                        gemm(w_m2[l], i * 4, 4, j * 512, 512, 8)
                if l == 0:
                    with S.loop(p, 4, 2, per(2, 0, 2)) as i:
                        for j in range(2):
                            gemm(w_p1, 0, 8, (i * 256 + j * P,), 256, 4)
                    with S.loop(p, 2, 2, per(2, 0)) as i:
                        for j in range(2):
                            gemm(w_p2, 0, 8, i * 512 + j * 256, 256, 4)

        ADA_FREED = [1 + 16, 1 + 16 + 24]

        @block.sync
        def _(sp):
            p = Program(sp, names, {})
            S = Stream()

            def load(w, k0, kn, c0, cn):
                s = S.raw % 2
                S.raw += 1
                sp.wait_ge(sem[f"raw_empty{s}"], p.after(f"raw_empty{s}"))
                if isinstance(c0, tuple):
                    dst = raw[s][:, :].rearrange("p (k b c) -> p b k c", b=2, c=P)
                    for b in range(2):
                        sp.dma_start(dst[:, b], w[:, :, bass.ds(c0[0] + b * D, P)]).then_inc(sem[f"raw_full{s}"], 16)
                else:
                    dst = raw[s][:, 0:kn * cn].rearrange("p (k c) -> p k c", c=cn)
                    ks = slice(k0, k0 + kn) if isinstance(k0, int) else bass.ds(k0, kn)
                    cs = slice(c0, c0 + cn) if isinstance(c0, int) else bass.ds(c0, cn)
                    sp.dma_start(dst, w[:, ks, cs]).then_inc(sem[f"raw_full{s}"], 16)

            def gemm(w, k0, kn, c0, cn, groups):
                load(w, k0, kn, c0, cn)
                S.split += 1

            def later_ada(w, c0, q, n_norm):
                sp.wait_ge(sem["u_lo"], n_norm)
                sp.wait_ge(sem[f"ada_empty{q % 2}"], p.after(f"ada_empty{q % 2}"))
                sp.dma_start(adaw[q % 2][:, :].rearrange("p (k c) -> p k c", c=P),
                             w[:, :, bass.ds(c0, P)]).then_inc(sem[f"ada_full{q % 2}"], 16)

            def per(gemms, adas, loads=1):
                return {**{f"raw_empty{s}": gemms // 2 for s in range(2)}, **{f"ada_empty{s}": adas // 2 for s in range(2)}}

            def step(s, c, d, lat):
                sp.wait_ge(sem["step_done"], p.after("step_done"))
                toks = slice(c * P, c * P + P) if isinstance(c, int) else bass.ds(c * P, P)
                full = sem[f"step_full{s}"]
                sp.dma_start(xtb[s][:, :], xtokD[toks, 0:D + 2 * P]).then_inc(full, 16)
                if lat:
                    sp.dma_start(bcT[s][:, :, :], xbcT[D:XBC, toks].rearrange("(b p) t -> p b t", p=P)).then_inc(full, 16)
                    sp.dma_start(Abc[s][:, :, :], acsD[d * HEADS:(d + 1) * HEADS, toks].partition_broadcast(P)).then_inc(full, 16)

            def scan_loads():
                sp.wait_ge(sem["xs_stored"], 16 * XBT)
                sp.wait_ge(sem["xt_stored"], 16 * XBT)
                sp.wait_ge(sem["acs_loaded"], 16)
                sp.wait_ge(sem["tab_dve"], 6)
                for d in range(2):
                    for j in range(NCX):
                        step(j, NCH + (j if d == 0 else NCX - 1 - j), d, False)
                    with p.loop(NCH // 2, {"step_done": 2}) as i:
                        for j in range(2):
                            step(j, i * 2 + j if d == 0 else i * -2 + (NCH - 1 - j), d, True)

            walk(p, S, per, gemm, lambda w, c0, cn: load(w, 0, 8, c0, cn), later_ada, scan_loads)

        @block.gpsimd
        def _(pool):
            p = Program(pool, names, {})
            S = Stream()
            for n, k in credit.items():
                pool.sem_inc(sem[n], k * names[n])
            pool.memset(ident[:, :], 0.0).then_inc(sem["const_ready"], p.counted("const_ready"))
            pool.memset(ones[:, :], 1.0).then_inc(sem["const_ready"], p.counted("const_ready"))
            pool.memset(maskF[:, :], BIG).then_inc(sem["const_ready"], p.counted("const_ready"))
            pool.memset(maskB[:, :], BIG).then_inc(sem["const_ready"], p.counted("const_ready"))
            pool.wait_ge(sem["const_ready"], p.so_far("const_ready"))
            pool.affine_select(out=ident[:, :], in_=ident[:, :], compare_op=ALU.not_equal, fill=1.0, base=0,
                                      pattern=[[-1, P]], channel_multiplier=1).then_inc(sem["const_ready"], p.counted("const_ready"))
            pool.affine_select(out=maskF[:, :], in_=maskF[:, :], compare_op=ALU.is_ge, fill=-BIG, base=0,
                                      pattern=[[1, P]], channel_multiplier=-1).then_inc(sem["const_ready"], p.counted("const_ready"))
            pool.affine_select(out=maskB[:, :], in_=maskB[:, :], compare_op=ALU.is_ge, fill=-BIG, base=0,
                                      pattern=[[-1, P]], channel_multiplier=1).then_inc(sem["const_ready"], p.counted("const_ready"))
            pool.wait_ge(sem["const_ready"], p.so_far("const_ready"))

            ends = [None, None]

            def loop_ended():
                if in_loop[0] is not None:
                    c = p.cnt["group_done"].c
                    ends[:] = [c - in_loop[0], c]
                    in_loop[0] = None

            def enter():
                loop_ended()
                pool.wait_ge(sem["group_done"], ends[0])

            def gemm(w, k0, kn, c0, cn, groups):
                s, t = S.raw % 2, S.split % 2
                S.raw += 1
                S.split += 1
                n = kn * cn
                pool.wait_ge(sem[f"raw_full{s}"], p.after(f"raw_full{s}", 2 if isinstance(c0, tuple) else 1))
                if in_loop[0] is not None:
                    pool.wait_ge(sem["group_done"], p.so_far("group_done", -in_loop[0]))
                    in_loop[0] = groups
                elif ends[0] is not None:
                    pool.wait_ge(sem["group_done"], ends[0])
                p.skip("group_done", groups)
                if in_loop[0] is None:
                    ends[:] = [ends[1], p.cnt["group_done"].c]
                pool.sem_inc(sem["split_begun"], 1)
                pool.tensor_scalar(wh[t][:, 0:n], raw[s][:, 0:n], 1.0, None, ALU.mult).then_inc(sem["split_hi"], p.counted("split_hi"))
                pool.wait_ge(sem["split_hi"], p.so_far("split_hi"))
                pool.tensor_tensor(wl[t][:, 0:n], raw[s][:, 0:n], wh[t][:, 0:n].bitcast(F32), ALU.subtract).then_inc(sem[f"split_full{t}"], p.counted(f"split_full{t}"))
                pool.wait_ge(sem[f"split_full{t}"], p.so_far(f"split_full{t}"))
                pool.sem_inc(sem[f"raw_empty{s}"], 1)

            def ada(w, c0, cn):
                p.skip(f"raw_full{S.raw % 2}")
                S.raw += 1

            def per(gemms, adas, loads=1):
                d = {f"raw_full{s}": gemms // 2 * loads for s in range(2)}
                for s in range(2):
                    d[f"split_full{s}"] = gemms // 2
                enter()
                in_loop[0] = 8 if gemms == 4 else 4
                return {**d, "split_hi": gemms, "group_done": 24 if gemms == 4 else 8}

            def scan_gates():
                for d in range(2):
                    for j in range(NCX):
                        p.skip(f"step_full{j}")
                    with p.loop(NCH // 2, {"step_full0": 3, "step_full1": 3, "E_ready": 2, "CE_ready": 4}) as i:
                        for s in range(2):
                            pool.wait_ge(sem[f"step_full{s}"], p.after(f"step_full{s}", 3))
                            pool.wait_ge(sem["E_ready"], p.after("E_ready"))
                            for g in range(2):
                                v = Eb[s][:, g * 8:(g + 1) * 8, :]
                                cT_ = bcT[s][:, 2 + g, :].unsqueeze(1).to_broadcast([P, 8, P])
                                pool.tensor_tensor(v, v, cT_, ALU.mult).then_inc(sem["CE_ready"], p.counted("CE_ready"))

            def stage(name):
                loop_ended()
                p.cnt["group_done"] = Lin({"xbc": 2 * NALL, "out": p.cnt["group_done"].c,
                                           "out2": p.cnt["group_done"].c + 2 + 2 * KT}[name])

            in_loop = [None]
            walk(p, S, per, gemm, ada, lambda w, c0, q, n_norm: None, scan_gates, stage)

        @block.tensor
        def _(pe):
            p = Program(pe, names, mirrored)
            S = Stream()
            prev = [None]
            bank = [0]

            def next_bank(evac, j):
                if j < 4 and prev[0] is not None and prev[0] != evac:
                    pe.wait_ge(sem[prev[0]], p.so_far(prev[0], j - 3))
                else:
                    pe.wait_ge(sem[evac], p.so_far(evac, -3))
                p.skip(evac)
                b = bank[0]
                bank[0] = (b + 1) % 4
                return b

            def mark(name):
                marks[name] = {n: p.cnt[n].c for n in SHARED}, bank[0]

            def drained(evac):
                if prev[0] is not None:
                    pe.wait_ge(sem[prev[0]], p.so_far(prev[0]))
                prev[0] = evac

            def unit(width, kn, tiles, segs, rhs, evac, j0, ready=None, loads=1, between=lambda n: None):
                t_ = S.split % 2
                S.raw += 1
                S.split += 1
                p.skip(f"raw_full{(S.raw - 1) % 2}", loads)
                pe.wait_ge(sem[f"split_full{t_}"], p.after(f"split_full{t_}"))
                order = [(t, s) for s in segs for t in range(tiles)]
                for n, (t, s) in enumerate(order):
                    b = next_bank(evac, j0 + n)
                    w = SEGS[s][1]
                    for k in range(kn):
                        if ready:
                            ready(n, t, s, k)
                        o = k * width + t * P
                        H, L = wh[t_][:, o:o + P], wl[t_][:, o:o + P]
                        xh, xl = rhs(k, s)
                        pe.matmul(PG[:, b, 0:w], H, xh, start=(k == 0), stop=False)
                        pe.matmul(PG[:, b, 0:w], H, xl, start=False, stop=False)
                        ins = pe.matmul(PG[:, b, 0:w], L, xh, start=False, stop=(k == kn - 1))
                    ins.then_inc(sem["group_done"], p.counted("group_done"))
                    between(n)

            def later_ada(q, out_col):
                s = q % 2
                pe.wait_ge(sem[f"ada_full{s}"], p.after(f"ada_full{s}"))
                for k in range(KT):
                    ins = pe.matmul(PM[:, 3, bass.ds(out_col, 2)], adaw[s][:, k * P:(k + 1) * P], csil[:, k:k + 9:8],
                                    start=(k == 0), stop=(k == KT - 1))
                ins.then_inc(sem[f"ada_empty{s}"], 1)

            def ada_unit(cols, out_col):
                s = S.raw % 2
                S.raw += 1
                pe.wait_ge(sem[f"raw_full{s}"], p.after(f"raw_full{s}"))
                for t in range(cols // P):
                    for k in range(KT):
                        o = out_col + 2 * t
                        dst = PM[:, 3, o:o + 2] if isinstance(o, int) else PM[:, 3, bass.ds(o, 2)]
                        ins = pe.matmul(dst, raw[s][:, k * cols + t * P:k * cols + (t + 1) * P],
                                        csil[:, k:k + 9:8], start=(k == 0), stop=(k == KT - 1))
                ins.then_inc(sem[f"raw_empty{s}"], 1)

            def per(gemms, adas, **more):
                d = {f"raw_full{s}": gemms // 2 for s in range(2)}
                for s in range(2):
                    d[f"split_full{s}"] = gemms // 2
                    d[f"ada_full{s}"] = adas // 2
                return {**d, **more}

            pe.wait_ge(sem["const_ready"], 7)
            pe.wait_ge(sem["par_loaded"], 16 * (len(place)))
            for b in range(NB):
                n = min(P, n_rows - b * P)
                ins = pe.transpose(PM[:, b // 4, (b % 4) * P:(b % 4) * P + n], prow[0:n, b, :], ident[0:n, 0:n])
            ins.then_inc(sem["par_turned"], p.counted("par_turned"))
            prev[0] = "read_by_act"
            for c in range(NALL):
                pe.wait_ge(sem[f"xin_full{c % 2}"], p.after(f"xin_full{c % 2}"))
                for hf in range(2):
                    b = next_bank("read_by_act", 4)
                    for q in range(4):
                        ins = pe.transpose(PG[:, b, q * P:(q + 1) * P], xin[c % 2][:, (4 * hf + q) * P:(4 * hf + q + 1) * P],
                                           ident[:, :])
                    ins.then_inc(sem["group_done"], p.counted("group_done"))
            pe.wait_ge(sem["silu_c"], 1)
            for u in range(N_ADA0):
                ada_unit(256, 4 * u)

            def stats(n, width=HALF):
                pe.wait_ge(sem["sq_added"], p.after("sq_added", n))
                if p.cnt["stat_done"].c >= 1:
                    pe.wait_ge(sem["ln_done"], p.cnt["stat_done"].c)
                pe.matmul(PM[:, 0, 0:width], ones[:, :], sacc[:, 0:width], start=True, stop=True).then_inc(sem["stat_done"], p.counted("stat_done"))

            for s in range(3):
                stats(KT - 1, SEGS[s][1])
            u_base = {"n": 0}

            def u_ready(n, t, s, k):
                if t == 0:
                    pe.wait_ge(sem["u_lo"], u_base["n"] + s * KT + k + 1)

            def u_rhs(k, s):
                o, w = SEGS[s]
                return uh[:, k, o:o + w], ul[:, k, o:o + w]

            drained("read_by_act")
            mark("xbc")

            def turn(tt):
                pe.wait_ge(sem["xs_ready"], 2 * (tt + 1))
                if tt:
                    pe.wait_ge(sem["xt_copied"], tt)
                for c in range(NALL):
                    dst = PM[:, c // 4, (c % 4) * P:(c % 4 + 1) * P]
                    ins = pe.transpose(dst, xs[:, c * P:(c + 1) * P], ident[:, :])
                ins.then_inc(sem["xt_turned"], p.counted("xt_turned"))

            for u in range(N_XBC):
                t_ = S.split % 2
                S.raw += 1
                S.split += 1
                p.skip(f"raw_full{(S.raw - 1) % 2}")
                pe.wait_ge(sem[f"split_full{t_}"], p.after(f"split_full{t_}"))
                for t in range(2):
                    for s in range(3):
                        b = next_bank("read_by_act", 4)
                        w = SEGS[s][1]
                        for k in range(KT):
                            if u == 0 and t == 0:
                                u_ready(0, 0, s, k)
                            o = k * 256 + t * P
                            H, L = wh[t_][:, o:o + P], wl[t_][:, o:o + P]
                            xh, xl = u_rhs(k, s)
                            pe.matmul(PG[:, b, 0:w], H, xh, start=(k == 0), stop=False)
                            pe.matmul(PG[:, b, 0:w], H, xl, start=False, stop=False)
                            ins = pe.matmul(PG[:, b, 0:w], L, xh, start=False, stop=(k == KT - 1))
                        ins.then_inc(sem["group_done"], p.counted("group_done"))
                    if 2 * u + t >= 1:
                        turn(2 * u + t - 1)
            unit(P, 8, 1, range(3), u_rhs, "read_by_act", 4)
            turn(XBT - 1)
            lat = range(2)
            mark("zg")
            for m0 in (16, 32):
                with S.loop(p, 2, 2, per(2, 8, group_done=8, read_by_act=8)) as i:
                    for j in range(2):
                        unit(256, 8, 2, lat, u_rhs, "read_by_act", 4,
                             between=lambda n: later_ada(4 * j + n, i * 16 + (2 * m0 + 2 * (4 * j + n))))
            mark("v")
            with S.loop(p, 2, 2, per(2, 0, group_done=8, read_by_act=8)) as i:
                for j in range(2):
                    t_ = S.split % 2
                    S.raw += 1
                    S.split += 1
                    p.skip(f"raw_full{(S.raw - 1) % 2}")
                    pe.wait_ge(sem[f"split_full{t_}"], p.after(f"split_full{t_}"))
                    for cc in range(NCH // 2):
                        b = next_bank("read_by_act", 4)
                        for c2 in range(2):
                            c = 2 * cc + c2
                            dst = PG[:, b, c2 * 256:(c2 + 1) * 256]
                            for k in range(KT):
                                H, L = wh[t_][:, k * 256:(k + 1) * 256], wl[t_][:, k * 256:(k + 1) * 256]
                                xh, xl = uh[:, k, c * P:(c + 1) * P], ul[:, k, c * P:(c + 1) * P]
                                pe.matmul(dst, xh, H, start=(k == 0), stop=False)
                                pe.matmul(dst, xl, H, start=False, stop=False)
                                ins = pe.matmul(dst, xh, L, start=False, stop=(k == KT - 1))
                        ins.then_inc(sem["group_done"], p.counted("group_done"))

            pe.wait_ge(sem["acs_loaded"], 16)
            pe.wait_ge(sem["xt_copied"], XBT)
            for c in range(NALL):
                pe.transpose(PM[:, 0, c * 32:(c + 1) * 32], rwq[:, c * P:(c + 1) * P], ident[0:32, 0:32])
                ins = pe.transpose(PM[:, 1, c * 32:(c + 1) * 32], rwdt[:, c * P:(c + 1) * P], ident[0:32, 0:32])
            ins.then_inc(sem["tab_turned"], p.counted("tab_turned"))
            pe.wait_ge(sem["tab_dve"], 3)
            pe.matmul(PM[:, 2, 0:NALL * 32], ones[:, :], dAt[:, :, :].rearrange("p c h -> p (c h)"),
                             start=True, stop=True).then_inc(sem["tot_done"], p.counted("tot_done"))

            def states(s, d):
                for g in range(2):
                    if p.begun("state_ready"):
                        pe.wait_ge(sem["state_ready"], p.so_far("state_ready"))
                    p.skip("state_ready")
                    pe.matmul(PM[:, 1, :], xtb[s][:, D + g * P:D + (g + 1) * P], xte[:, g * 512:(g + 1) * 512],
                                     start=True, stop=True).then_inc(sem["S_done"], p.counted("S_done"))

            pe.wait_ge(sem["tab_dve"], 6)
            pe.wait_ge(sem["tab_act"], 2)
            for d in range(2):
                for s in range(NCX):
                    pe.wait_ge(sem[f"step_full{s}"], p.after(f"step_full{s}"))
                    pe.wait_ge(sem["xte_ready"], p.after("xte_ready"))
                    states(s, d)
                    p.skip("step_done")
                with p.loop(NCH // 2, {"step_full0": 3, "step_full1": 3, "xte_ready": 2, "xdt_ready": 4, "W_ready": 4,
                                       "CE_ready": 4, "scores_done": 2, "S_done": 4, "state_ready": 4, "y_done": 2,
                                       "step_done": 2}) as i:
                    for s in range(2):
                        pe.wait_ge(sem[f"step_full{s}"], p.after(f"step_full{s}", 3))
                        pe.wait_ge(sem["W_ready"], p.so_far("W_ready"))
                        for g in range(2):
                            ins = pe.matmul(PM[:, 0, g * P:(g + 1) * P], bcT[s][:, g, :], bcT[s][:, 2 + g, :],
                                            start=True, stop=True)
                        ins.then_inc(sem["scores_done"], p.counted("scores_done"))
                        pe.wait_ge(sem["xte_ready"], p.after("xte_ready"))
                        states(s, d)
                        pe.wait_ge(sem["xdt_ready"], p.after("xdt_ready", 2))
                        pe.wait_ge(sem["CE_ready"], p.after("CE_ready", 2))
                        pe.wait_ge(sem["W_ready"], p.after("W_ready", 2))
                        pe.wait_ge(sem["step_done"], p.so_far("step_done"))
                        p.skip("step_done")
                        for h in range(HEADS):
                            t, q = h // 2, (h % 2) * HD
                            dst = PM[q:q + HD, 2 + t // 4, (t % 4) * P:(t % 4 + 1) * P]
                            pe.matmul(dst, tm[h // 8][:, (h % 8) * HD:(h % 8 + 1) * HD], Wb[:, h, :], start=True, stop=False)
                            ins = pe.matmul(dst, st[s][:, h * HD:(h + 1) * HD], Eb[s][:, h, :], start=False, stop=True)
                        ins.then_inc(sem["y_done"], p.counted("y_done"))

            for g in range(2):
                for s in lat:
                    stats(3)

            def y_ready(n, t, s, k):
                if t == 0:
                    pe.wait_ge(sem["u_lo"], u_base["n"] + (k // 4) * 8 + s * 4 + k % 4 + 1)

            u_base["n"] = 3 * KT
            drained("read_by_dve")
            mark("out")
            with S.loop(p, 2, 2, per(2, 0, group_done=8, read_by_dve=8)) as i:
                for j in range(2):
                    unit(256, 8, 2, lat, lambda k, s: (yh[:, k, SEGS[s][0]:SEGS[s][0] + HALF], yl[:, k, SEGS[s][0]:SEGS[s][0] + HALF]),
                         "read_by_dve", 4, ready=y_ready if j == 0 else None)
            pe.wait_ge(sem["sg_loaded"], 80)
            drained("read_by_dve")
            mark("sg")
            for g2 in range(2):
                b = next_bank("read_by_dve", 4)
                for q in range(4):
                    ins = pe.transpose(PG[:, b, q * P:(q + 1) * P], uf[g2][:, q * P:(q + 1) * P], ident[:, :])
                ins.then_inc(sem["group_done"], p.counted("group_done"))
            pe.wait_ge(sem["v_ready"], NCH)
            pe.wait_ge(sem["read_by_dve"], p.so_far("read_by_dve"))
            for g in range(KT):
                for s in lat:
                    b = next_bank("read_by_dve", 4)
                    for q in range(4):
                        dst = PG[:, b, q * P:(q + 1) * P]
                        pe.matmul(dst, vln[:, 4 * s + q, g * P:(g + 1) * P], sgwT[:, g, :], start=True, stop=False)
                        ins = pe.matmul(dst, ones[0:1, :], sgb(g), start=False, stop=True)
                    ins.then_inc(sem["group_done"], p.counted("group_done"))
            with S.loop(p, 2, 2, per(2, 0, group_done=8, read_by_dve=8)) as i:
                for j in range(2):
                    unit(256, 8, 2, lat, lambda k, s: (yh2[:, k, SEGS[s][0]:SEGS[s][0] + HALF], yl2[:, k, SEGS[s][0]:SEGS[s][0] + HALF]),
                         "read_by_dve", 4,
                         ready=(lambda n, t, s, k: t == 0 and pe.wait_ge(sem["sg_lo"], 2 * k + s + 1)) if j == 0 else None)
            u_base["n"] += 16

            def v_rhs(k, s):
                o, w = SEGS[s]
                return vh[:, k, o:o + w], vl[:, k, o:o + w]

            def h_rhs(j):
                return lambda k, s: (hh[:, k, SEGS[s][0]:SEGS[s][0] + HALF], hl[:, k, SEGS[s][0]:SEGS[s][0] + HALF])

            def mlp(l):
                for s in lat:
                    stats(KT - 1)
                adas = 6 if l == 0 else 0
                drained("read_by_dve")
                mark(f"mlp{l}")
                with S.loop(p, 8, 4, per(4, adas, group_done=24, read_by_act=8, read_by_dve=16, hid_lo=8)) as i:
                    prev[0] = "read_by_dve"
                    for j in range(2):
                        unit(256, 8, 2, lat, v_rhs, "read_by_act", 4 * j, ready=u_ready if j == 0 else None,
                             between=lambda n: 4 * j + n < adas and later_ada(4 * j + n, i * 12 + 2 * (4 * j + n)))
                    prev[0] = "read_by_act"
                    base = p.cnt["hid_lo"]

                    def hid_ready(n, t, s, k):
                        if t == 0:
                            p.cnt["hid_lo"] = base.plus((k // 2) * 4 + s * 2 + k % 2 + 1)
                            pe.wait_ge(sem["hid_lo"], p.so_far("hid_lo"))

                    for j in range(2):
                        unit(512, 4, 4, lat, h_rhs(j), "read_by_dve", 8 * j, ready=hid_ready if j == 0 else None)
                    p.cnt["hid_lo"] = base.plus(8)
                prev[0] = "read_by_dve"
                u_base["n"] += 16

            mlp(0)
            for s in lat:
                stats(KT - 1)
            drained("read_by_act")
            mark("pw1")
            with S.loop(p, 4, 2, {**per(2, 0, group_done=8, read_by_act=8), "raw_full0": 2, "raw_full1": 2}) as i:
                for j in range(2):
                    unit(256, 8, 2, lat, v_rhs, "read_by_act", 4, ready=u_ready if j == 0 else None, loads=2)
            for s in lat:
                pe.wait_ge(sem["ln_dve"], 15 * s + 7)
                if s:
                    pe.wait_ge(sem["mean_done"], 1)
                pe.matmul(PM[:, 1, :], ones[:, :], sacc[:, :], start=True, stop=True).then_inc(sem["mean_done"], p.counted("mean_done"))
                stats(KT - 1)
            u_base["n"] += 16
            drained("read_by_dve")
            mark("pw2")
            with S.loop(p, 2, 2, per(2, 0, group_done=8, read_by_dve=8)) as i:
                for j in range(2):
                    unit(256, 8, 2, lat, v_rhs, "read_by_dve", 4, ready=u_ready if j == 0 else None)
            u_base["n"] += 16
            mlp(1)
            drained("read_by_act")
            mark("final")
            for c in range(NCH):
                for hf in range(2):
                    b = next_bank("read_by_act", 4)
                    for q in range(4):
                        ins = pe.transpose(PG[:, b, q * P:(q + 1) * P], hT[:, 4 * hf + q, c * P:(c + 1) * P], ident[:, :])
                    ins.then_inc(sem["group_done"], p.counted("group_done"))
        def part(w, items):
            return w, items

        def h_parts(g, l, shift, segs, dh, dl):
            got = []
            for s in segs:
                o, w = SEGS[s]
                j = 1 if s == 2 else 0
                src = (lambda k: hcT[:, k, :]) if s == 2 else (lambda k, o=o, w=w: hT[:, k, o:o + w])
                got.append(part(w, [(src(k), gsc[:, g + j, k:k + 1], mod[:, l, shift + k, j:j + 1],
                                     dh[:, k, o:o + w], dl[:, k, o:o + w]) for k in range(KT)]))
            return got

        def y_parts():
            return [part(HALF, [(yT[:, k, s * HALF:(s + 1) * HALF], col("ssd_g", k), None,
                                 yh[:, k, s * HALF:(s + 1) * HALF], yl[:, k, s * HALF:(s + 1) * HALF])
                                for k in range(4 * g, 4 * g + 4)]) for g in range(2) for s in range(2)]

        def c_parts(s):
            return [part(HALF, [(cT[:, k, s * HALF:(s + 1) * HALF], col("ln_g", k), col("ln_b", k),
                                 vh[:, k, s * HALF:(s + 1) * HALF], vl[:, k, s * HALF:(s + 1) * HALF]) for k in range(KT)])]

        def norm_act(p, act, parts, dim, func=ACT.Identity):
            for w, items in parts:
                for k, it in enumerate(items):
                    if k:
                        if p.begun("sq_added", -1):
                            act.wait_ge(sem["sq_added"], p.so_far("sq_added", -1))
                        p.skip("sq_added")
                    dst = sq[k % 2] if k else sacc
                    act.activation(dst[:, 0:w], it[0], ACT.Square).then_inc(sem["sq_ready"], p.counted("sq_ready"))
                act.wait_ge(sem["stat_done"], p.after("stat_done"))
                r = rs[0]
                if p.begun("norm_mul"):
                    act.wait_ge(sem["norm_mul"], p.so_far("norm_mul"))
                act.activation(r[:, 0:w], PM[:, 0, 0:w], ACT.Ln, bias=EPS, scale=1.0 / dim).then_inc(sem["ln_done"], p.counted("ln_done"))
                act.wait_ge(sem["ln_done"], p.so_far("ln_done"))
                act.activation(r[:, 0:w], r[:, 0:w], ACT.Exp, scale=-0.5).then_inc(sem["rstd_ready"], p.counted("rstd_ready"))
                for k, (src, g, b, hi, lo) in enumerate(items):
                    act.wait_ge(sem["norm_mul"], p.after("norm_mul"))
                    if p.begun("u_lo", -1):
                        act.wait_ge(sem["u_lo"], p.so_far("u_lo", -1))
                    p.skip("u_lo")
                    if b is None:
                        act.activation(uf[k % 2][:, 0:w], tm[k % 2][:, 0:w], func, scale=g).then_inc(sem["uf_ready"], p.counted("uf_ready"))
                    else:
                        act.activation(uf[k % 2][:, 0:w], tm[k % 2][:, 0:w], func, scale=g, bias=b).then_inc(sem["uf_ready"], p.counted("uf_ready"))
                    act.wait_ge(sem["uf_ready"], p.so_far("uf_ready"))
                    act.activation(hi, uf[k % 2][:, 0:w], ACT.Copy).then_inc(sem["u_hi"], p.counted("u_hi"))

        def norm_dve(p, dve, parts):
            for w, items in parts:
                dve.wait_ge(sem["sq_ready"], p.after("sq_ready"))
                for k in range(1, len(items)):
                    dve.wait_ge(sem["sq_ready"], p.after("sq_ready"))
                    if k > 1:
                        dve.wait_ge(sem["sq_added"], p.so_far("sq_added"))
                    dve.tensor_tensor(sacc[:, 0:w], sacc[:, 0:w], sq[k % 2][:, 0:w], ALU.add).then_inc(sem["sq_added"], p.counted("sq_added"))
                dve.wait_ge(sem["rstd_ready"], p.after("rstd_ready"))

                def lo_part(k):
                    dve.wait_ge(sem["u_hi"], p.after("u_hi"))
                    hi, lo = items[k][3], items[k][4]
                    dve.tensor_tensor(lo, uf[k % 2][:, 0:w], hi.bitcast(F32), ALU.subtract).then_inc(sem["u_lo"], p.counted("u_lo"))

                for k, it in enumerate(items):
                    if p.begun("uf_ready", -1):
                        dve.wait_ge(sem["uf_ready"], p.so_far("uf_ready", -1))
                    p.skip("uf_ready")
                    dve.tensor_tensor(tm[k % 2][:, 0:w], it[0], rs[0][:, 0:w], ALU.mult).then_inc(sem["norm_mul"], p.counted("norm_mul"))
                    if k:
                        lo_part(k - 1)
                lo_part(len(items) - 1)

        def at(p, name):
            counts, p.bank = marks[name]
            for n, c in counts.items():
                p.cnt[n] = Lin(c)

        @block.scalar
        def _(act):
            p = Program(act, names, mirrored)
            p.bank = 0

            def group(fn, evac=True):
                b = p.bank
                p.bank = (b + 1) % 4
                act.wait_ge(sem["group_done"], p.after("group_done"))
                return fn(b).then_inc(sem["read_by_act"], p.counted("read_by_act"))

            for blk, q0, k, ap, s0 in place:
                act.dma_start(prow[q0:q0 + k, blk, :], ap[s0:s0 + k]).then_inc(sem["par_loaded"], p.counted("par_loaded"))
            x2, c2 = a["x"][0], a["ctx"][0]
            tok_rows = lambda c: x2[c * P:(c + 1) * P, :] if c < NCH else c2[(c - NCH) * P:(c - NCH + 1) * P, :]
            for c in range(2):
                act.dma_start(xin[c][:, :], tok_rows(c)).then_inc(sem[f"xin_full{c}"], 16)
            rec = a["ssd_a_log"].rearrange("a b h -> (a b h)")
            act.dma_start(alog[:, :], rec.unsqueeze(1)).then_inc(sem["rec_loaded"], p.counted("rec_loaded"))
            act.dma_start(a_bc[:, :], rec.partition_broadcast(P)).then_inc(sem["rec_loaded"], p.counted("rec_loaded"))
            act.dma_start(dtb[:, :], a["ssd_dt_bias"].rearrange("a b h -> (a b h)").unsqueeze(1)).then_inc(sem["rec_loaded"], p.counted("rec_loaded"))
            act.dma_start(d_bc[:, :], a["ssd_d"].rearrange("a h -> (a h)").partition_broadcast(P)).then_inc(sem["rec_loaded"], p.counted("rec_loaded"))
            act.wait_ge(sem["par_turned"], 1)
            flat = par[:, :, :].rearrange("p b q -> p (b q)")
            act.activation(flat[:, 0:512], PM[:, 0, :], ACT.Copy).then_inc(sem["par_ready"], p.counted("par_ready"))
            act.activation(flat[:, 512:n_rows], PM[:, 1, 0:n_rows - 512], ACT.Copy).then_inc(sem["par_ready"], p.counted("par_ready"))
            act.wait_ge(sem["par_ready"], p.so_far("par_ready"))
            act.activation(csil[:, :], col("c", 0, 16), ACT.Silu).then_inc(sem["silu_c"], p.counted("silu_c"))
            for c in range(NALL):
                for hf in range(2):
                    dst = hT[:, 4 * hf:4 * hf + 4, c * P:(c + 1) * P] if c < NCH else \
                        hcT[:, 4 * hf:4 * hf + 4, (c - NCH) * P:(c - NCH + 1) * P]
                    group(lambda b: act.activation(dst, PG[:, b, :].rearrange("p (q t) -> p q t", t=P), ACT.Copy))
                if c + 2 < NALL:
                    act.dma_start(xin[c % 2][:, :], tok_rows(c + 2)).then_inc(sem[f"xin_full{c % 2}"], 16)
            act.wait_ge(sem["read_by_act"], p.so_far("read_by_act"))
            act.wait_ge(sem["mod_ready"], 3)
            norm_act(p, act, h_parts(0, 0, 0, range(3), uh, ul), D)

            at(p, "xbc")
            act.wait_ge(sem["pads_ready"], 2)

            def silu(tt):
                act.wait_ge(sem["conv_done"], tt + 1)
                act.wait_ge(sem["xt_turned"], tt)
                act.wait_ge(sem["xs_stored"], 16 * tt)
                act.activation(xs[:, 0:TOK], cv[:, 0:TOK], ACT.Silu).then_inc(sem["xs_ready"], p.counted("xs_ready"))
                act.activation(xs[:, TOK:ALL], cv[:, TOK + 4:TOK + 4 + CTX], ACT.Silu).then_inc(sem["xs_ready"], p.counted("xs_ready"))
                act.wait_ge(sem["xs_ready"], p.so_far("xs_ready"))
                act.dma_start(xbcT[tt * P:(tt + 1) * P, :], xs[:, :]).then_inc(sem["xs_stored"], p.counted("xs_stored"))

            def store_turned(tt):
                act.wait_ge(sem["xt_copied"], tt + 1)
                act.dma_start(xtokD.rearrange("(c p) n -> p c n", p=P)[:, :, tt * P:(tt + 1) * P], xtk[:, :, :]).then_inc(sem["xt_stored"], p.counted("xt_stored"))

            for tt in range(XBT):
                for s in range(3):
                    o, w = SEGS[s]
                    q = 2 + o + (4 if s == 2 else 0)
                    if s == 0 and tt >= 2:
                        act.wait_ge(sem["conv_done"], tt - 1)
                    group(lambda b: act.activation(xp[tt % 2][:, q:q + w], PG[:, b, 0:w], ACT.Copy))
                    if s == 0 and tt >= 1:
                        silu(tt - 1)
                        if tt >= 2:
                            store_turned(tt - 2)
            silu(XBT - 1)
            store_turned(XBT - 2)
            store_turned(XBT - 1)
            act.wait_ge(sem["xs_stored"], 16 * XBT)
            act.wait_ge(sem["xt_stored"], 16 * XBT)
            act.wait_ge(sem["rec_loaded"], 64)
            for s in range(3):
                o, w = SEGS[s]
                group(lambda b: act.activation(rwx[:, o:o + w], PG[0:R32, b, 0:w], ACT.Identity, bias=dtb[:, 0:1]))
            act.wait_ge(sem["read_by_act"], p.so_far("read_by_act"))
            act.activation(rwe[:, :], rwx[:, :], ACT.Abs).then_inc(sem["row_act"], p.counted("row_act"))
            act.wait_ge(sem["row_act"], p.so_far("row_act"))
            act.activation(rwe[:, :], rwe[:, :], ACT.Exp, scale=-1.0).then_inc(sem["row_act"], p.counted("row_act"))
            act.activation(alog[:, :], alog[:, :], ACT.Exp).then_inc(sem["row_act"], p.counted("row_act"))
            act.activation(a_bc[:, :], a_bc[:, :], ACT.Exp).then_inc(sem["row_act"], p.counted("row_act"))

            def zo_loop(n_units, func, dst):
                per = {"group_done": 8, "read_by_act": 8, **{f"zo_stored{b}": 2 for b in range(4)}}
                with p.loop(2, per) as i:
                    for j in range(2):
                        for n in range(4):
                            b = p.bank
                            act.wait_ge(sem[f"zo_stored{b}"], p.so_far(f"zo_stored{b}"))
                            group(lambda b: act.activation(zo[b][:, :], PG[:, b, :], func))
                            act.wait_ge(sem["read_by_act"], p.so_far("read_by_act"))
                            act.dma_start(*dst(i, j, n, b)).then_inc(sem[f"zo_stored{b}"], p.counted(f"zo_stored{b}"))

            def by_feature(t):
                def dst(i, j, n, b):
                    s, q = n // 2, n % 2
                    return t[bass.ds(i * 512 + (j * 256 + q * P), P), s * HALF:(s + 1) * HALF], zo[b][:, :]
                return dst

            zo_loop(4, ACT.Silu, by_feature(zT))
            act.wait_ge(sem["row_dve"], 3 + 12 + 2 * NALL)
            act.dma_start(acsD[0:HEADS, :], rwx[0:HEADS, :]).then_inc(sem["acs_stored"], p.counted("acs_stored"))
            act.dma_start(acsD[HEADS:2 * HEADS, :], rwe[HEADS:2 * HEADS, :]).then_inc(sem["acs_stored"], p.counted("acs_stored"))
            zo_loop(4, ACT.Gelu_apprx_tanh, by_feature(guT))
            act.wait_ge(sem["acs_stored"], 32)
            act.dma_start(rwq[:, :], acsD[:, :]).then_inc(sem["acs_loaded"], p.counted("acs_loaded"))
            v3 = vtok.rearrange("(c p) n -> p c n", p=P)
            zo_loop(4, ACT.Gelu_apprx_tanh,
                    lambda i, j, n, b: (v3[:, 2 * n:2 * n + 2, bass.ds(i * 512 + j * 256, 256)],
                                        zo[b][:, :].rearrange("p (c n) -> p c n", c=2)))

            act.wait_ge(sem["tab_dve"], 5)
            act.activation(te[:, :, :], te[:, :, :], ACT.Exp).then_inc(sem["tab_act"], p.counted("tab_act"))
            act.activation(tab[:, :, :, 3, :], PM[:, 2, 0:NALL * R32].rearrange("p (c d h) -> p c d h", d=2, h=HEADS),
                                  ACT.Exp).then_inc(sem["tab_act"], p.counted("tab_act"))
            for d in range(2):
                for s in range(NCX):
                    p.skip(f"step_full{s}")
                with p.loop(NCH // 2, {"step_full0": 3, "step_full1": 3, "seg_ready": 2, "E_ready": 2, "D_exp": 2}) as i:
                    for s in range(2):
                        act.wait_ge(sem[f"step_full{s}"], p.after(f"step_full{s}", 3))
                        act.activation(Eb[s][:, :, :], Abc[s][:, :, :], ACT.Exp).then_inc(sem["E_ready"], p.counted("E_ready"))
                        act.wait_ge(sem["seg_ready"], p.after("seg_ready"))
                        act.activation(Wb[:, :, :], Wb[:, :, :], ACT.Exp).then_inc(sem["D_exp"], p.counted("D_exp"))
            act.wait_ge(sem["step_done"], 2 + 2 * NALL)
            for b in range(4):
                act.wait_ge(sem[f"zo_stored{b}"], p.so_far(f"zo_stored{b}"))
            for k in range(KT):
                for q, t in ((0, xbcT), (1, zT)):
                    b = q
                    if k >= 1:
                        act.wait_ge(sem["fin_dve"], 2 * (k - 1) + q + 1)
                    act.dma_start(ld[b][:, :], t[k * P:(k + 1) * P, 0:TOK]).then_inc(sem[f"ld_full{b}"], 16)
            act.wait_ge(sem["fin_dve"], 2 * KT)
            norm_act(p, act, y_parts(), D // 2)

            act.wait_ge(sem["u_lo"], p.so_far("u_lo"))
            for q in range(2):
                act.dma_start(uf[q][:, :].rearrange("p (g k) -> p g k", k=P),
                                     a["sg_w"][0, 4 * q:4 * q + 4].rearrange("g q k -> q g k")).then_inc(sem["sg_loaded"], p.counted("sg_loaded"))
                act.dma_start((sacc, rs[0])[q][0:1, :], a["sg_b"][0, 4 * q:4 * q + 4].rearrange("g q -> (g q)").unsqueeze(0)).then_inc(sem["sg_loaded"], p.counted("sg_loaded"))
            act.dma_start(lnrow[:, :], a["sg_ln_g"].rearrange("a d -> (a d)").partition_broadcast(P)).then_inc(sem["sg_loaded"], p.counted("sg_loaded"))
            act.dma_start(vln[:, :, :], v3).then_inc(sem["v_loaded"], p.counted("v_loaded"))
            at(p, "out")
            p.skip("group_done", 16)
            act.wait_ge(sem["v_dve"], 3 * NCH)
            act.activation(rstd[:, :, :], mv[:, :, 1:2], ACT.Ln, bias=EPS).then_inc(sem["v_act"], p.counted("v_act"))
            act.wait_ge(sem["v_act"], p.so_far("v_act"))
            act.activation(rstd[:, :, :], rstd[:, :, :], ACT.Exp, scale=-0.5).then_inc(sem["v_act"], p.counted("v_act"))
            act.wait_ge(sem["v_dve"], 5 * NCH)
            act.dma_start(lnrow[:, :], a["sg_ln_b"].rearrange("a d -> (a d)").partition_broadcast(P)).then_inc(sem["sg_loaded"], p.counted("sg_loaded"))
            at(p, "sg")
            p.skip("read_by_dve", 2)
            act.wait_ge(sem["read_by_dve"], p.so_far("read_by_dve"))
            for g in range(KT):
                for s in range(2):
                    if g:
                        act.wait_ge(sem["sg_lo"], 2 * (g - 1) + s + 1)
                    act.dma_start(gu[s][:, :], guT[g * P:(g + 1) * P, s * HALF:(s + 1) * HALF]).then_inc(sem[f"gu_full{s}"], 16)
                for s in range(2):
                    act.wait_ge(sem["read_by_dve"], p.after("read_by_dve"))
                    act.activation(yh2[:, g, s * HALF:(s + 1) * HALF], tm[s][:, :], ACT.Copy).then_inc(sem["sg_hi"], p.counted("sg_hi"))

            def mlp(l):
                norm_act(p, act, h_parts(2 if l == 0 else 4, l, 24, range(2), vh, vl), D)
                at(p, f"mlp{l}")
                with p.loop(8, {"group_done": 24, "read_by_act": 8, "relu_sq": 8}) as i:
                    for m in range(8):
                        act.wait_ge(sem["relu_sq"], p.so_far("relu_sq", -1))
                        p.skip("relu_sq")
                        group(lambda b: act.activation(sq[m % 2][:, :], PG[:, b, :], ACT.Relu))
                    p.skip("group_done", 16)
                act.wait_ge(sem["read_by_act"], p.so_far("read_by_act"))

            at(p, "mlp0")
            act.wait_ge(sem["read_by_dve"], p.so_far("read_by_dve"))
            act.wait_ge(sem["mod_ready"], 5)
            mlp(0)
            at(p, "pw1")
            act.wait_ge(sem["read_by_dve"], p.so_far("read_by_dve"))
            act.wait_ge(sem["mod_ready"], 9)
            norm_act(p, act, h_parts(3, 1, 0, range(2), vh, vl), D)
            for k in range(KT):
                for s in range(2):
                    m = 2 * k + s
                    if m >= 1:
                        act.wait_ge(sem["glu_done"], m)
                    group(lambda b: act.activation(tm[0][:, :], PG[:, b, :], ACT.Identity, bias=col("b_pw1", k)))
                    group(lambda b: act.activation(tm[1][:, :], PG[:, b, :], ACT.Sigmoid, bias=col("b_pw1", KT + k)))
            for s in range(2):
                act.wait_ge(sem["ln_dve"], 15 * (s + 1))
                norm_act(p, act, c_parts(s), D, ACT.Silu)
            at(p, "mlp1")
            act.wait_ge(sem["read_by_dve"], p.so_far("read_by_dve"))
            mlp(1)
            at(p, "final")
            act.wait_ge(sem["group_done"], p.so_far("group_done", 1))
            act.dma_start(fg[:, :], a["final_norm_g"].partition_broadcast(P)).then_inc(sem["fg_loaded"], p.counted("fg_loaded"))
            for c in range(NCH):
                if p.begun(f"out_stored{c % 2}"):
                    act.wait_ge(sem[f"out_stored{c % 2}"], p.so_far(f"out_stored{c % 2}"))
                for hf in range(2):
                    group(lambda b: act.activation(fo[c % 2][:, hf * 512:(hf + 1) * 512], PG[:, b, :], ACT.Copy))
                act.wait_ge(sem["read_by_act"], p.so_far("read_by_act"))
                act.activation(fs[:, :], fo[c % 2][:, :], ACT.Square, accum_out=fm[:, c, :]).then_inc(sem["out_act"], p.counted("out_act"))
                act.wait_ge(sem["out_act"], p.so_far("out_act"))
                act.activation(fm[:, c, :], fm[:, c, :], ACT.Ln, bias=EPS, scale=1.0 / D).then_inc(sem["out_act"], p.counted("out_act"))
                act.wait_ge(sem["out_act"], p.so_far("out_act"))
                act.activation(fm[:, c, :], fm[:, c, :], ACT.Exp, scale=-0.5).then_inc(sem["out_act"], p.counted("out_act"))
                act.wait_ge(sem["out_dve"], c + 1)
                act.dma_start(out[0, c * P:(c + 1) * P, :], fo[c % 2][:, :]).then_inc(sem[f"out_stored{c % 2}"], p.counted(f"out_stored{c % 2}"))
            for q in range(2):
                act.wait_ge(sem[f"out_stored{q}"], p.so_far(f"out_stored{q}"))

        @block.vector
        def _(dve):
            p = Program(dve, names, mirrored)
            p.bank = 0

            def group(fn):
                b = p.bank
                p.bank = (b + 1) % 4
                dve.wait_ge(sem["group_done"], p.after("group_done"))
                return fn(b).then_inc(sem["read_by_dve"], p.counted("read_by_dve"))

            def add_ada(l, t0, n):
                src = PM[:, 3, 2 * t0:2 * (t0 + n)].rearrange("p (t j) -> p t j", j=2)
                b = col("ada_b", l * 48 + t0, n).unsqueeze(2).to_broadcast([P, n, 2])
                dve.tensor_tensor(mod[:, l, t0:t0 + n, :], src, b, ALU.add).then_inc(sem["mod_ready"], p.counted("mod_ready"))
                dve.wait_ge(sem["mod_ready"], p.so_far("mod_ready"))

            def gain(idx, l, t0, j, g):
                dve.scalar_tensor_tensor(out=gsc[:, idx, :], in0=mod[:, l, t0:t0 + KT, j], scalar=1.0, in1=g,
                                                op0=ALU.add, op1=ALU.mult).then_inc(sem["mod_ready"], p.counted("mod_ready"))

            dve.wait_ge(sem["par_ready"], 2)
            for s in range(2):
                dve.wait_ge(sem[f"raw_empty{s}"], 1 + N_ADA0 // 2)
            add_ada(0, 0, 16)
            gain(0, 0, 8, 0, col("mix_g", 0, KT))
            gain(1, 0, 8, 1, col("mix_g", 0, KT))
            dve.wait_ge(sem["rec_loaded"], 64)
            for q in range(2):
                v = slice(q * HD, (q + 1) * HD)
                dve.tensor_copy(dsk[v, :], d_bc[v, q:HEADS:2]).then_inc(sem["skip_ready"], p.counted("skip_ready"))
            norm_dve(p, dve, h_parts(0, 0, 0, range(3), uh, ul))

            at(p, "xbc")
            for q in range(2):
                dve.memset(xp[q][:, :], 0.0).then_inc(sem["pads_ready"], p.counted("pads_ready"))

            def copy_turned(tt):
                dve.wait_ge(sem["xt_turned"], tt + 1)
                if tt:
                    dve.wait_ge(sem["xt_stored"], 16 * tt)
                dve.tensor_copy(xtk[:, :, :].rearrange("p c t -> p (c t)"),
                                       PM[:, 0:3, :].rearrange("p b n -> p (b n)")[:, 0:ALL]).then_inc(sem["xt_copied"], p.counted("xt_copied"))

            for tt in range(XBT):
                p.skip("read_by_act", 3)
                dve.wait_ge(sem["read_by_act"], p.so_far("read_by_act"))
                n = PADW - 4
                if tt:
                    dve.wait_ge(sem["xs_ready"], 2 * tt)
                dve.tensor_scalar(cv[:, 0:n], xp[tt % 2][:, 0:n], col("conv_w", tt), col("conv_b", tt), ALU.mult, ALU.add).then_inc(sem["conv_step"], p.counted("conv_step"))
                for tap in range(1, CONV):
                    dve.wait_ge(sem["conv_step"], p.so_far("conv_step"))
                    dve.scalar_tensor_tensor(out=cv[:, 0:n], in0=xp[tt % 2][:, tap:tap + n],
                                                    scalar=col("conv_w", tap * XBT + tt), in1=cv[:, 0:n], op0=ALU.mult,
                                                    op1=ALU.add).then_inc(sem["conv_done" if tap == CONV - 1 else "conv_step"], p.counted("conv_done" if tap == CONV - 1 else "conv_step"))
                if tt:
                    copy_turned(tt - 1)
            copy_turned(XBT - 1)

            dve.wait_ge(sem["row_act"], 4)

            def row(ins):
                ins.then_inc(sem["row_dve"], p.counted("row_dve"))
                dve.wait_ge(sem["row_dve"], p.so_far("row_dve"))

            row(dve.tensor_scalar(rwq[:, :], rwe[:, :], 2.0, None, ALU.add))
            row(dve.reciprocal(rwq[:, :], rwq[:, :]))
            row(dve.tensor_tensor(rwe[:, :], rwe[:, :], rwq[:, :], ALU.mult))
            row(dve.tensor_tensor(rwq[:, :], rwe[:, :], rwe[:, :], ALU.mult))
            row(dve.tensor_scalar(rwp[:, :], rwq[:, :], 1.0 / 13, None, ALU.mult))
            for n in (11, 9, 7, 5, 3):
                row(dve.scalar_tensor_tensor(out=rwp[:, :], in0=rwp[:, :], scalar=1.0 / n, in1=rwq[:, :], op0=ALU.add, op1=ALU.mult))
            row(dve.scalar_tensor_tensor(out=rwp[:, :], in0=rwp[:, :], scalar=1.0, in1=rwe[:, :], op0=ALU.add, op1=ALU.mult))
            row(dve.tensor_scalar(rwx[:, :], rwx[:, :], 0.0, None, ALU.max))
            row(dve.scalar_tensor_tensor(out=rwdt[:, :], in0=rwp[:, :], scalar=2.0, in1=rwx[:, :], op0=ALU.mult, op1=ALU.add))
            row(dve.tensor_scalar(rwp[:, :], rwdt[:, :], alog[:, 0:1], -1.0, ALU.mult, ALU.mult))
            row(dve.tensor_scalar(a_bc[:, :], a_bc[:, :], -1.0, None, ALU.mult))
            for c in range(NALL):
                v = slice(c * P, (c + 1) * P)
                dve.tensor_tensor_scan(rwx[:, v], ones[0:R32, :], rwp[:, v], 0.0, ALU.mult, ALU.add).then_inc(sem["row_dve"], p.counted("row_dve"))
                dve.tensor_tensor_scan(rwe[:, v][:, ::-1], ones[0:R32, :], rwp[:, v][:, ::-1], 0.0, ALU.mult, ALU.add).then_inc(sem["row_dve"], p.counted("row_dve"))

            for s in range(2):
                dve.wait_ge(sem[f"ada_empty{s}"], ADA_FREED[0])
            add_ada(0, 16, 32)
            gain(2, 0, 32, 0, col("mlp_g", 0, KT))

            dve.wait_ge(sem["tab_turned"], 1)
            view = lambda b: PM[:, b, 0:NALL * R32].rearrange("p (c d h) -> p c d h", d=2, h=HEADS)
            te4 = te[:, :, :].rearrange("p c (d h) -> p c d h", h=HEADS)
            dve.tensor_scalar(tab[:, :, :, 0, :], view(0), -1.0, None, ALU.mult).then_inc(sem["tab_dve"], p.counted("tab_dve"))
            dve.tensor_copy(tab[:, :, :, 1, :], view(1)).then_inc(sem["tab_dve"], p.counted("tab_dve"))
            dve.wait_ge(sem["tab_dve"], p.so_far("tab_dve"))
            dve.tensor_tensor(dAt[:, :, :], PM[:, 1, 0:NALL * R32].rearrange("p (c h) -> p c h", h=R32),
                                     a_bc[:, :].unsqueeze(1).to_broadcast([P, NALL, R32]), ALU.mult).then_inc(sem["tab_dve"], p.counted("tab_dve"))
            dve.wait_ge(sem["tot_done"], p.after("tot_done"))
            dve.tensor_tensor(te4, view(2), tab[:, :, :, 0, :], ALU.add).then_inc(sem["tab_dve"], p.counted("tab_dve"))
            dve.wait_ge(sem["tab_dve"], p.so_far("tab_dve"))
            dve.tensor_scalar(te[:, :, :], te[:, :, :], 0.0, None, ALU.min).then_inc(sem["tab_dve"], p.counted("tab_dve"))
            dve.wait_ge(sem["tab_act"], p.after("tab_act", 2))
            dve.tensor_tensor(tab[:, :, :, 2, :], te4, tab[:, :, :, 1, :], ALU.mult).then_inc(sem["tab_dve"], p.counted("tab_dve"))
            dve.wait_ge(sem["tab_dve"], p.so_far("tab_dve"))
            dve.memset(yT[:, :, :], 0.0).then_inc(sem["scal_ready"], p.counted("scal_ready"))

            heads = lambda kind: scal[:, kind, :].unsqueeze(2).to_broadcast([P, HEADS, HD])
            wide = lambda t: t[:, :].rearrange("p (h q) -> p h q", q=HD)

            def scalars(c, d):
                src = tab[:, c:c + 1, d, :, :] if isinstance(c, int) else tab[:, bass.ds(c, 1), d, :, :]
                dve.wait_ge(sem["step_done"], p.so_far("step_done"))
                dve.wait_ge(sem["par_ready"], 2)
                dve.tensor_copy(scal[:, :, :].unsqueeze(1), src).then_inc(sem["scal_ready"], p.counted("scal_ready"))
                dve.wait_ge(sem["scal_ready"], p.so_far("scal_ready"))

            def to_end(s):
                if p.begun("S_done"):
                    dve.wait_ge(sem["S_done"], p.so_far("S_done"))
                dve.wait_ge(sem["par_ready"], 2)
                dve.tensor_tensor(wide(xte), xtb[s][:, 0:D].rearrange("p (h q) -> p h q", q=HD), heads(2), ALU.mult).then_inc(sem["xte_ready"], p.counted("xte_ready"))

            def next_state(s, first):
                if not first:
                    dve.tensor_tensor(wide(st[1 - s]), wide(st[s]), heads(3), ALU.mult).then_inc(sem["state_mul"], p.counted("state_mul"))
                for g in range(2):
                    v = st[1 - s][:, g * 512:(g + 1) * 512]
                    dve.wait_ge(sem["S_done"], p.after("S_done"))
                    if first:
                        dve.tensor_copy(v, PM[:, 1, :]).then_inc(sem["state_ready"], p.counted("state_ready"))
                    else:
                        dve.wait_ge(sem["state_mul"], p.so_far("state_mul"))
                        dve.tensor_tensor(v, v, PM[:, 1, :], ALU.add).then_inc(sem["state_ready"], p.counted("state_ready"))

            for d in range(2):
                mask = maskF if d == 0 else maskB
                for s in range(NCX):
                    c = NCH + (s if d == 0 else NCX - 1 - s)
                    dve.wait_ge(sem[f"step_full{s}"], p.after(f"step_full{s}"))
                    scalars(c, d)
                    to_end(s)
                    if d == 1 and s == 0:
                        dve.wait_ge(sem["y_done"], p.so_far("y_done"))
                    next_state(s, s == 0)
                    dve.wait_ge(sem["state_ready"], p.so_far("state_ready"))
                    dve.tensor_copy(scal[:, 0:1, 0:1], scal[:, 0:1, 0:1]).then_inc(sem["step_done"], p.counted("step_done"))
                with p.loop(NCH // 2, {"step_full0": 3, "step_full1": 3, "scal_ready": 2, "seg_ready": 2, "xte_ready": 2,
                                       "xdt_ready": 4, "D_exp": 2, "scores_done": 2, "W_ready": 4, "state_mul": 2,
                                       "S_done": 4, "state_ready": 4, "y_done": 2, "step_done": 2}) as i:
                    for s in range(2):
                        c = i * 2 + s if d == 0 else i * -2 + (NCH - 1 - s)
                        dve.wait_ge(sem[f"step_full{s}"], p.after(f"step_full{s}", 3))
                        scalars(c, d)
                        for h in range(HEADS):
                            ins = dve.scalar_tensor_tensor(out=Wb[:, h, :], in0=Abc[s][:, h, :], scalar=scal[:, 0, h:h + 1],
                                                           in1=mask[:, :], op0=ALU.add, op1=ALU.min)
                        ins.then_inc(sem["seg_ready"], p.counted("seg_ready"))
                        to_end(s)
                        for g in range(2):
                            dve.tensor_tensor(wide(tm[g]), xtb[s][:, g * 512:(g + 1) * 512].rearrange("p (h q) -> p h q", q=HD),
                                                     scal[:, 1, g * 8:(g + 1) * 8].unsqueeze(2).to_broadcast([P, 8, HD]), ALU.mult).then_inc(sem["xdt_ready"], p.counted("xdt_ready"))
                        dve.wait_ge(sem["D_exp"], p.after("D_exp"))
                        dve.wait_ge(sem["scores_done"], p.after("scores_done"))
                        for g in range(2):
                            v = Wb[:, g * 8:(g + 1) * 8, :]
                            dve.tensor_tensor(v, v, PM[:, 0, g * P:(g + 1) * P].unsqueeze(1).to_broadcast([P, 8, P]),
                                                     ALU.mult).then_inc(sem["W_ready"], p.counted("W_ready"))
                        next_state(s, False)
                        dve.wait_ge(sem["y_done"], p.after("y_done"))
                        v = yT[:, :, bass.ds(c * P, P)]
                        dve.tensor_tensor(v, v, PM[:, 2:4, :].rearrange("p b (t q) -> p (b t) q", q=P), ALU.add).then_inc(sem["step_done"], p.counted("step_done"))
            dve.wait_ge(sem["step_done"], p.so_far("step_done"))
            dve.wait_ge(sem["skip_ready"], p.so_far("skip_ready"))
            for k in range(KT):
                b = 0
                dve.wait_ge(sem[f"ld_full{b}"], p.after(f"ld_full{b}"))
                dve.scalar_tensor_tensor(out=yT[:, k, :], in0=ld[b][:, :], scalar=dsk[:, k:k + 1], in1=yT[:, k, :],
                                                op0=ALU.mult, op1=ALU.add).then_inc(sem["fin_dve"], p.counted("fin_dve"))
                dve.wait_ge(sem["fin_dve"], p.so_far("fin_dve"))
                dve.wait_ge(sem[f"ld_full{b + 1}"], p.after(f"ld_full{b + 1}"))
                dve.tensor_tensor(yT[:, k, :], yT[:, k, :], ld[b + 1][:, :], ALU.mult).then_inc(sem["fin_dve"], p.counted("fin_dve"))
            norm_dve(p, dve, y_parts())

            def add_to_h(k, s, l, t0, b):
                o = s * HALF
                return dve.scalar_tensor_tensor(out=hT[:, k, o:o + HALF], in0=PG[:, b, :], scalar=mod[:, l, t0 + k, 0:1],
                                                in1=hT[:, k, o:o + HALF], op0=ALU.mult, op1=ALU.add)

            def out_proj(l, t0):
                for u in range(4):
                    for s in range(2):
                        for t in range(2):
                            group(lambda b: add_to_h(2 * u + t, s, l, t0, b))

            dve.wait_ge(sem["v_loaded"], 16)
            for c in range(NCH):
                for q in range(2):
                    if c or q:
                        dve.wait_ge(sem["v_dve"], p.so_far("v_dve"))
                    dve.bn_stats(bst[:, q, :], vln[:, c, q * 512:(q + 1) * 512]).then_inc(sem["v_dve"], p.counted("v_dve"))
                dve.wait_ge(sem["v_dve"], p.so_far("v_dve"))
                dve.bn_aggr(mv[:, c, :], bst[:, :, :]).then_inc(sem["v_dve"], p.counted("v_dve"))
            at(p, "out")
            out_proj(0, 16)
            dve.wait_ge(sem["v_act"], 2)
            dve.wait_ge(sem["sg_loaded"], 80)
            for c in range(NCH):
                dve.tensor_scalar(vln[:, c, :], vln[:, c, :], mv[:, c, 0:1], rstd[:, c, 0:1], ALU.subtract, ALU.mult).then_inc(sem["v_dve"], p.counted("v_dve"))
                dve.wait_ge(sem["v_dve"], p.so_far("v_dve"))
                dve.tensor_tensor(vln[:, c, :], vln[:, c, :], lnrow[:, :], ALU.mult).then_inc(sem["v_dve"], p.counted("v_dve"))
            at(p, "sg")
            for q in range(2):
                group(lambda b: dve.tensor_copy(sgwT[:, 4 * q:4 * q + 4, :].rearrange("p g k -> p (g k)"), PG[:, b, :]))
            dve.wait_ge(sem["sg_loaded"], 96)
            dve.wait_ge(sem["v_dve"], p.so_far("v_dve"))
            for c in range(NCH):
                dve.tensor_tensor(vln[:, c, :], vln[:, c, :], lnrow[:, :], ALU.add).then_inc(sem["v_ready"], p.counted("v_ready"))
            for g in range(KT):
                for s in range(2):
                    dve.wait_ge(sem[f"gu_full{s}"], p.after(f"gu_full{s}"))
                    group(lambda b: dve.tensor_tensor(tm[s][:, :], PG[:, b, :], gu[s][:, :], ALU.mult))
                    dve.wait_ge(sem["sg_hi"], p.after("sg_hi"))
                    dve.tensor_tensor(yl2[:, g, s * HALF:(s + 1) * HALF], tm[s][:, :],
                                             yh2[:, g, s * HALF:(s + 1) * HALF].bitcast(F32), ALU.subtract).then_inc(sem["sg_lo"], p.counted("sg_lo"))
            out_proj(0, 16)
            dve.wait_ge(sem["read_by_dve"], p.so_far("read_by_dve"))

            def mlp(l):
                norm_dve(p, dve, h_parts(2 if l == 0 else 4, l, 24, range(2), vh, vl))
                dve.wait_ge(sem["u_lo"], p.so_far("u_lo"))
                at(p, f"mlp{l}")
                with p.loop(8, {"group_done": 24, "read_by_act": 8, "read_by_dve": 16, "relu_sq": 8, "hid_hi": 8, "hid_lo": 8}) as i:
                    for m in range(8):
                        t, o = (m // 4) * 2 + m % 2, (m // 2 % 2) * HALF
                        dve.wait_ge(sem["read_by_act"], p.after("read_by_act"))
                        if m:
                            dve.wait_ge(sem["hid_lo"], p.so_far("hid_lo"))
                        dve.tensor_tensor(uf[0][:, :], sq[m % 2][:, :], sq[m % 2][:, :], ALU.mult).then_inc(sem["relu_sq"], p.counted("relu_sq"))
                        dve.wait_ge(sem["relu_sq"], p.so_far("relu_sq"))
                        hi, lo = hh[:, t, o:o + HALF], hl[:, t, o:o + HALF]
                        dve.tensor_copy(hi, uf[0][:, :]).then_inc(sem["hid_hi"], p.counted("hid_hi"))
                        dve.wait_ge(sem["hid_hi"], p.so_far("hid_hi"))
                        dve.tensor_tensor(lo, uf[0][:, :], hi.bitcast(F32), ALU.subtract).then_inc(sem["hid_lo"], p.counted("hid_lo"))
                    p.skip("group_done", 8)
                    for j in range(2):
                        for s in range(2):
                            for t in range(4):
                                group(lambda b: add_to_h(4 * j + t, s, l, 40, b))
                dve.wait_ge(sem["read_by_dve"], p.so_far("read_by_dve"))

            mlp(0)
            for s in range(2):
                dve.wait_ge(sem[f"ada_empty{s}"], ADA_FREED[1])
            add_ada(1, 0, 48)
            gain(3, 1, 8, 0, col("mix_g", KT, KT))
            gain(4, 1, 32, 0, col("mlp_g", KT, KT))
            dve.tensor_tensor(gb[:, :], mod[:, 1, 16:24, 0], col("b_pw2", 0, KT), ALU.mult).then_inc(sem["mod_ready"], p.counted("mod_ready"))
            dve.memset(apad[0][:, :], 0.0).then_inc(sem["mod_ready"], p.counted("mod_ready"))
            dve.memset(apad[1][:, :], 0.0).then_inc(sem["mod_ready"], p.counted("mod_ready"))
            norm_dve(p, dve, h_parts(3, 1, 0, range(2), vh, vl))
            at(p, "pw1")
            for k in range(KT):
                for s in range(2):
                    dve.wait_ge(sem["read_by_act"], p.after("read_by_act", 2))
                    o = CW // 2 + s * HALF
                    dve.tensor_tensor(apad[k % 2][:, o:o + HALF], tm[0][:, :], tm[1][:, :], ALU.mult).then_inc(sem["glu_done"], p.counted("glu_done"))
                dve.wait_ge(sem["glu_done"], p.so_far("glu_done"))
                dve.tensor_scalar(cT[:, k, :], apad[k % 2][:, 0:TOK], col("w_dw", k), col("b_dw", k), ALU.mult, ALU.add).then_inc(sem["dw_step"], p.counted("dw_step"))
                for tap in range(1, CW):
                    dve.wait_ge(sem["dw_step"], p.so_far("dw_step"))
                    dve.scalar_tensor_tensor(out=cT[:, k, :], in0=apad[k % 2][:, tap:tap + TOK],
                                                    scalar=col("w_dw", tap * KT + k), in1=cT[:, k, :], op0=ALU.mult,
                                                    op1=ALU.add).then_inc(sem["dw_step"], p.counted("dw_step"))
            for s in range(2):
                o = s * HALF
                src = lambda k: cT[:, k, o:o + HALF]
                dve.wait_ge(sem["u_lo" if s else "dw_step"], p.so_far("u_lo" if s else "dw_step"))
                for k in range(1, KT):
                    dve.tensor_tensor(sacc[:, :], src(0) if k == 1 else sacc[:, :], src(k), ALU.add).then_inc(sem["ln_dve"], p.counted("ln_dve"))
                    dve.wait_ge(sem["ln_dve"], p.so_far("ln_dve"))
                dve.wait_ge(sem["mean_done"], p.after("mean_done"))
                for k in range(KT):
                    dve.scalar_tensor_tensor(out=src(k), in0=PM[:, 1, :], scalar=-1.0 / D, in1=src(k), op0=ALU.mult,
                                                    op1=ALU.add).then_inc(sem["ln_dve"], p.counted("ln_dve"))
                norm_dve(p, dve, c_parts(s))
            for k in range(KT):
                dve.tensor_scalar(hT[:, k, :], hT[:, k, :], gb[:, k:k + 1], None, ALU.add).then_inc(sem["bias_added"], p.counted("bias_added"))
            dve.wait_ge(sem["bias_added"], p.so_far("bias_added"))
            at(p, "pw2")
            out_proj(1, 16)
            dve.wait_ge(sem["read_by_dve"], p.so_far("read_by_dve"))
            mlp(1)
            dve.wait_ge(sem["fg_loaded"], 16)
            for c in range(NCH):
                dve.wait_ge(sem["out_act"], 3 * (c + 1))
                dve.scalar_tensor_tensor(out=fo[c % 2][:, :], in0=fo[c % 2][:, :], scalar=fm[:, c, 0:1], in1=fg[:, :],
                                                op0=ALU.mult, op1=ALU.mult).then_inc(sem["out_dve"], p.counted("out_dve"))


_INS = ["x", "c", "ctx", "c_ctx", "ada_w", "ada_b", "norm_mix_g", "norm_mlp_g", "mlp_w1", "mlp_w2",
        "hy_w_in", "ssd_conv_w", "ssd_conv_b", "ssd_dt_bias", "ssd_a_log", "ssd_d", "ssd_norm_g",
        "sg_ln_g", "sg_ln_b", "sg_w", "sg_b", "hy_w_out", "cf_w_pw1", "cf_b_pw1", "cf_w_dw", "cf_b_dw",
        "cf_ln_g", "cf_ln_b", "cf_w_pw2", "cf_b_pw2", "final_norm_g"]


def kernel(**inputs):
    import numpy as _np
    import concourse.bacc as _bacc
    from concourse import mybir as _mybir
    from concourse.bass_utils import run_bass_kernel_spmd as _run

    nc = _bacc.Bacc("TRN2", target_bir_lowering=False, num_devices=1)
    arrays, aps = {}, {}
    for name in _INS:
        v = _np.ascontiguousarray(inputs[name])
        arrays[f"in_{name}"] = v
        aps[name] = nc.dram_tensor(f"in_{name}", v.shape, _mybir.dt.from_np(v.dtype), kind="ExternalInput").ap()
    out = nc.dram_tensor("out_0", (1, TOK, D), _mybir.dt.float32, kind="ExternalOutput").ap()
    build(nc, aps, out)
    r = _run(nc, [arrays], core_ids=[0])
    return r.results[0]["out_0"]
```

```python
from contextlib import ExitStack, contextmanager

import concourse.bass as bass
from concourse import mybir

P = 128
F32 = mybir.dt.float32
F32R = mybir.dt.float32r
ALU = mybir.AluOpType
ACT = mybir.ActivationFunctionType

D = 1024
TOK = 1024
CTX = 256
ALL = TOK + CTX
KT = D // P
HALF = 512
SEGS = [(0, HALF), (HALF, HALF), (TOK, CTX)]
NCH = TOK // P
NCX = CTX // P
NALL = NCH + NCX
XBC = 1536
XBT = XBC // P
HEADS = 16
HD = 64
HID = 4096
EPS = 1e-6
UNIT = 2048
CONV = 5
CW = 31
PADW = 1288
CONF_PAD = 1056
POOL_TAPS = 9


class Lin:

    def __init__(self, c, step=0, i=None):
        self.c, self.step, self.i = c, step, i

    def plus(self, k):
        return Lin(self.c + k, self.step, self.i)

    def value(self, mul=1, add=0):
        v = self.c * mul + add
        return self.i * (self.step * mul) + v if self.step else v


class Program:

    def __init__(self, eng, names, start):
        self.e, self.step = eng, names
        self.cnt = {n: Lin(start.get(n, 0)) for n in names}

    def begun(self, name, k=0):
        v = self.cnt[name].plus(k)
        return v.step != 0 or v.c > 0

    def so_far(self, name, k=0):
        assert self.begun(name, k), name
        return self.cnt[name].plus(k).value(self.step[name])

    def skip(self, name, k=1):
        self.cnt[name] = self.cnt[name].plus(k)

    def after(self, name, k=1):
        self.skip(name, k)
        return self.so_far(name)

    def counted(self, name):
        self.skip(name)
        return self.step[name]

    @contextmanager
    def loop(self, n, per):
        start = {k: v.c for k, v in self.cnt.items()}
        with self.e.Fori(0, n) as i:
            for k, step in per.items():
                self.cnt[k] = Lin(start[k], step, i)
            yield i
        moved = {k: v.c - start[k] for k, v in self.cnt.items() if v.c != start[k]}
        assert moved == {k: v for k, v in per.items() if v}, f"signals in a turn: {moved}"
        for k in self.cnt:
            self.cnt[k] = Lin(start[k] + n * per.get(k, 0))


def build(nc, a, out):
    dram = lambda n, s: nc.dram_tensor(n, s, F32, kind="Internal").ap()
    xbcT = dram("scr_xbcT", [XBC, ALL])
    xtokD = dram("scr_xtok", [ALL, XBC])
    zT = dram("scr_zT", [D, TOK])
    guT = dram("scr_guT", [D, TOK])
    vtok = dram("scr_vtok", [TOK, D])
    acsD = dram("scr_acs", [2 * HEADS, ALL])

    stack = ExitStack()
    with stack:
        def sb(name, shape, dt=F32, at=stack):
            return at.enter_context(nc.sbuf_tensor(name, shape, dt))

        hT = sb("hT", [P, KT, TOK])
        raw = [sb(f"raw{i}", [P, UNIT]) for i in range(2)]
        wh = [sb(f"wh{i}", [P, UNIT], F32R) for i in range(2)]
        wl = [sb(f"wl{i}", [P, UNIT], F32R) for i in range(2)]
        ident = sb("ident", [P, P])
        ones = sb("ones", [P, P])
        maskF = sb("maskF", [P, P])
        maskB = sb("maskB", [P, P])
        mod = sb("mod", [P, 2, 48, 2])
        gsc = sb("gsc", [P, 6, KT])
        csil = sb("csil", [P, 16])
        G = ExitStack()
        adaw = [sb(f"adaw{i}", [P, D], at=G) for i in range(2)]
        pacc = adaw[0]
        prod = [sb(f"prod{i}", [P, TOK], at=G) for i in range(2)]
        G.close()
        sacc = sb("sacc", [P, HALF])
        rs = [sb("rs0", [P, HALF])]
        tm = [sb(f"tm{i}", [P, HALF]) for i in range(2)]
        sq = [sb(f"sq{i}", [P, HALF]) for i in range(2)]
        uf = [sb(f"uf{i}", [P, HALF]) for i in range(2)]
        PG = stack.enter_context(nc.psum_tensor("PG", [P, 4, 512], F32))
        PM = stack.enter_context(nc.psum_tensor("PM", [P, 4, 512], F32))

        rows = {}
        place = []
        n_rows = 0

        def add_rows(name, ap, r):
            nonlocal n_rows
            rows[name] = n_rows
            s = 0
            while s < r:
                k = min(r - s, P - n_rows % P)
                place.append((n_rows // P, n_rows % P, k, ap, s))
                n_rows += k
                s += k

        vec = lambda ap: ap.rearrange("(r p) -> r p", p=P)
        add_rows("c", vec(a["c"].rearrange("a d -> (a d)")), KT)
        add_rows("c_ctx", vec(a["c_ctx"]), KT)
        add_rows("ada_b", vec(a["ada_b"].rearrange("a d -> (a d)")), 96)
        add_rows("mix_g", vec(a["norm_mix_g"].rearrange("a d -> (a d)")), 2 * KT)
        add_rows("mlp_g", vec(a["norm_mlp_g"].rearrange("a d -> (a d)")), 2 * KT)
        add_rows("ssd_g", vec(a["ssd_norm_g"].rearrange("a d -> (a d)")), KT)
        add_rows("ln_g", vec(a["cf_ln_g"].rearrange("a d -> (a d)")), KT)
        add_rows("ln_b", vec(a["cf_ln_b"].rearrange("a d -> (a d)")), KT)
        add_rows("b_dw", vec(a["cf_b_dw"].rearrange("a d -> (a d)")), KT)
        add_rows("b_pw1", vec(a["cf_b_pw1"].rearrange("a d -> (a d)")), 2 * KT)
        add_rows("b_pw2", vec(a["cf_b_pw2"].rearrange("a d -> (a d)")), KT)
        add_rows("conv_b", vec(a["ssd_conv_b"].rearrange("a d -> (a d)")), XBT)
        add_rows("conv_w", vec(a["ssd_conv_w"].rearrange("a t d -> (a t d)")), CONV * XBT)
        add_rows("w_dw", vec(a["cf_w_dw"].rearrange("a t d -> (a t d)")), CW * KT)
        NB = (n_rows + P - 1) // P
        par = sb("par", [P, NB, P])

        def col(name, k=0, n=1):
            return par[:, :, :].rearrange("p b q -> p (b q)")[:, rows[name] + k:rows[name] + k + n]

        def cold(name, k):
            return par[:, :, :].rearrange("p b q -> p (b q)")[:, bass.ds(k + rows[name], 1)]

        R32 = 2 * HEADS
        alog = sb("alog", [R32, 1])
        dtb = sb("dtb", [R32, 1])
        a_bc = sb("a_bc", [P, R32])
        d_bc = sb("d_bc", [P, HEADS])
        dsk = sb("dsk", [P, KT])

        A = ExitStack()
        uh = sb("uh", [P, KT, ALL], F32R, A)
        ul = sb("ul", [P, KT, ALL], F32R, A)
        A1 = ExitStack()
        hcT = sb("hcT", [P, KT, CTX], at=A1)
        xin = [sb(f"xin{i}", [P, D], at=A1) for i in range(2)]
        prow = sb("prow", [P, NB, P], at=A1)
        A1.close()
        zo = sq + uf
        A2 = ExitStack()
        xp = [sb(f"xp{i}", [P, PADW], at=A2) for i in range(2)]
        cv = sb("cv", [P, PADW], at=A2)
        xs = sb("xs", [P, ALL], at=A2)
        xtk = sb("xtk", [P, NALL, P], at=A2)
        A2.close()
        A3 = ExitStack()
        rwx, rwe, rwq, rwp, rwdt = [sb(f"row_{n}", [R32, ALL], at=A3) for n in ("x", "e", "q", "p", "dt")]
        A3.close()
        A.close()

        B = ExitStack()
        yT = sb("yT", [P, KT, TOK], at=B)
        B1 = ExitStack()
        tab = sb("tab", [P, NALL, 2, 4, HEADS], at=B1)
        B2 = ExitStack()
        dAt = sb("dAt", [P, NALL, R32], at=B2)
        te = sb("te", [P, NALL, R32], at=B2)
        B2.close()
        bcT = [sb(f"bcT{i}", [P, 4, P], at=B1) for i in range(2)]
        xtb = [sb(f"xtb{i}", [P, D + 2 * P], at=B1) for i in range(2)]
        Abc = [sb(f"Abc{i}", [P, HEADS, P], at=B1) for i in range(2)]
        Eb = [sb(f"Eb{i}", [P, HEADS, P], at=B1) for i in range(2)]
        Wb = sb("Wb", [P, HEADS, P], at=B1)
        xd = [tm, [sacc, rs[0]]]
        xte = sb("xte", [P, D], at=B1)
        st = [sb(f"st{i}", [P, D], at=B1) for i in range(2)]
        scal = [sb(f"scal{i}", [P, 4, HEADS], at=B1) for i in range(2)]
        sm = sb("sm", [P, 2, P], at=B1)
        B1.close()
        yh = sb("yh", [P, KT, TOK], F32R, B)
        yl = sb("yl", [P, KT, TOK], F32R, B)
        ld = [sb(f"ld{i}", [P, TOK], at=B) for i in range(2)]
        B.close()

        C = ExitStack()
        vln = sb("vln", [P, NCH, D], at=C)
        yh2 = sb("yh2", [P, KT, TOK], F32R, C)
        yl2 = sb("yl2", [P, KT, TOK], F32R, C)
        gu = sq
        lnrow = sb("lnrow", [P, D], at=C)
        sgwT = sb("sgwT", [P, KT, P], at=C)
        bst = sb("bst", [P, 2, 6], at=C)
        mv = sb("mv", [P, NCH, 2], at=C)
        rstd = sb("rstd", [P, NCH, 1], at=C)
        sgb = lambda g: (sacc, rs[0])[g // 4][0:1, (g % 4) * P:(g % 4 + 1) * P]
        C.close()

        Dx = ExitStack()
        vh = sb("vh", [P, KT, TOK], F32R, Dx)
        vl = sb("vl", [P, KT, TOK], F32R, Dx)
        D1 = ExitStack()
        hh = sb("hh", [P, 4, TOK], F32R, D1)
        hl = sb("hl", [P, 4, TOK], F32R, D1)
        D1.close()
        D2 = ExitStack()
        cT = sb("cT", [P, KT, TOK], at=D2)
        apad = [sb(f"apad{i}", [P, CONF_PAD], at=D2) for i in range(2)]
        gb = sb("gb", [P, KT], at=D2)
        D2.close()
        D3 = ExitStack()
        fg = sb("fg", [P, D], at=D3)
        fo = [sb(f"fo{i}", [P, D], at=D3) for i in range(2)]
        fs = sb("fs", [P, D], at=D3)
        fm = sb("fm", [P, NCH, 1], at=D3)
        D3.close()
        Dx.close()

        names = {}
        for n in ("ada_step", "ada_added", "const_ready", "group_done", "read_by_act", "read_by_dve", "split_begun", "split_hi",
                  "par_turned", "par_ready", "skip_ready", "silu_c", "mod_ready",
                  "sq_ready", "sq_added", "stat_done", "ln_done", "rstd_ready", "norm_mul", "uf_ready", "u_hi", "u_lo",
                  "pads_ready", "conv_step", "conv_done", "xs_ready", "xt_turned", "xt_copied",
                  "row_act", "row_dve", "tab_turned", "tot_done", "tab_dve", "tab_act",
                  "y_cleared", "scal_ready", "sm_ready", "y_added", "seg_ready", "E_ready", "D_exp", "CE_ready", "xdt_ready", "xte_ready", "scores_done",
                  "W_ready", "S_done", "state_mul", "state_ready", "y_done", "step_done",
                  "fin_dve", "v_dve", "v_act", "v_ready", "sg_hi", "sg_lo",
                  "relu_sq", "hid_hi", "hid_lo", "glu_done", "dw_step", "dw_done", "prod_ready", "prod_added", "sq_summed", "mean_done", "ln_dve", "bias_added",
                  "out_dve", "out_act"):
            names[n] = 1
        for i in range(2):
            names[f"raw_empty{i}"] = 1
            names[f"ada_empty{i}"] = 1
            names[f"split_full{i}"] = 1
            for n in ("raw_full", "ada_full", "xin_full", "step_full", "gu_full"):
                names[f"{n}{i}"] = 16
        for i in range(4):
            names[f"zo_stored{i}"] = 16
            names[f"ld_full{i}"] = 16
        for n in ("par_loaded", "rec_loaded", "xs_stored", "xt_stored", "acs_stored", "acs_loaded", "v_loaded", "sg_loaded",
                  "fg_loaded", "out_stored0", "out_stored1"):
            names[n] = 16
        sem = {n: stack.enter_context(nc.semaphore(n)) for n in names}
        credit = {"read_by_act": 4, "read_by_dve": 4, "raw_empty0": 1, "raw_empty1": 1,
                  "ada_empty0": 1, "ada_empty1": 1, "step_done": 2, "y_done": 2,
                  "y_added": 1, "sm_ready": 1,
                  "relu_sq": 2, "zo_stored0": 1, "zo_stored1": 1, "zo_stored2": 1, "zo_stored3": 1}
        mirrored = {n: k for n, k in credit.items() if "_empty" not in n}
        marks = {}
        SHARED = ("group_done", "read_by_act", "read_by_dve")

        block = stack.enter_context(nc.Block())

        w_ada = [a["ada_w"][l].rearrange("(k p) n -> p k n", p=P) for l in range(2)]
        w_in = a["hy_w_in"][0].rearrange("(k p) n -> p k n", p=P)
        w_out = a["hy_w_out"][0].rearrange("(k p) n -> p k n", p=P)
        w_m1 = [a["mlp_w1"][l].rearrange("(k p) n -> p k n", p=P) for l in range(2)]
        w_m2 = [a["mlp_w2"][l].rearrange("(k p) n -> p k n", p=P) for l in range(2)]
        w_p1 = a["cf_w_pw1"][0].rearrange("(k p) n -> p k n", p=P)
        w_p2 = a["cf_w_pw2"][0].rearrange("(k p) n -> p k n", p=P)
        Z0, X0, T0, U0 = 0, D, D + XBC, D + XBC + 2 * HEADS
        V0 = U0 + D

        N_ADA0 = 2 * D // 256
        N_XBC = XBC // 256

        class Stream:

            def __init__(self):
                self.raw = self.split = 0

            @contextmanager
            def loop(self, p, n, gemms, per):
                raw0, split0 = self.raw, self.split
                with p.loop(n, per) as i:
                    yield i
                assert self.raw - raw0 == gemms and self.split - split0 == gemms
                self.raw, self.split = raw0 + n * gemms, split0 + n * gemms

        def walk(p, S, per, gemm, ada, later_ada, after_v, stage=lambda name: None, conv_tile=lambda: None):
            for u in range(N_ADA0):
                ada(w_ada[0], u * 256, 256)
            stage("xbc")
            for u in range(N_XBC):
                gemm(w_in, 0, 8, X0 + u * 256, 256, 6)
            gemm(w_in, 0, 8, T0, P, 3)
            for u in range(8):
                gemm(w_in, 0, 8, (Z0, U0)[u // 4] + u % 4 * 256, 256, 4)
                if u:
                    for q in range(4):
                        later_ada(w_ada[0], 2048 + (4 * (u - 1) + q) * P, q, 3 * KT)
            gemm(w_in, 0, 8, V0, 256, 4)
            for q in range(4):
                later_ada(w_ada[0], 2048 + (28 + q) * P, q, 3 * KT)
            for u in range(1, 4):
                gemm(w_in, 0, 8, V0 + u * 256, 256, 4)
            after_v()
            for k0 in (0, 8):
                stage("out" if k0 == 0 else "out2")
                with S.loop(p, 2, 2, per(2, 0)) as i:
                    for j in range(2):
                        gemm(w_out, k0, 8, i * 512 + j * 256, 256, 4)
            for l in range(2):
                adas = 6 if l == 0 else 0
                with S.loop(p, 8, 4, per(4, adas)) as i:
                    for j in range(2):
                        gemm(w_m1[l], 0, 8, i * 512 + j * 256, 256, 4)
                    for j in range(2):
                        for q in ((0, 1, 2, 3), (4, 5))[j][:adas]:
                            later_ada(w_ada[1], i * 768 + q * P, q, 7 * KT)
                        gemm(w_m2[l], i * 4, 4, j * 512, 512, 8)
                if l == 0:
                    for u in range(2):
                        gemm(w_p1, 0, 8, (u * P,), 256, 4)
                    with S.loop(p, 3, 2, per(2, 0, 2, convs=2)) as i:
                        for j in range(2):
                            gemm(w_p1, 0, 8, (i * 256 + (j + 2) * P,), 256, 4)
                            conv_tile()
                    for u in range(4):
                        gemm(w_p2, 0, 8, u * 256, 256, 4)
                        if u < 2:
                            conv_tile()

        ADA_FREED = [1 + 16, 1 + 16 + 24]

        @block.sync
        def _(sp):
            p = Program(sp, names, {})
            S = Stream()

            def load(w, k0, kn, c0, cn):
                s = S.raw % 2
                S.raw += 1
                sp.wait_ge(sem[f"raw_empty{s}"], p.after(f"raw_empty{s}"))
                if isinstance(c0, tuple):
                    dst = raw[s][:, :].rearrange("p (k b c) -> p b k c", b=2, c=P)
                    for b in range(2):
                        sp.dma_start(dst[:, b], w[:, :, bass.ds(c0[0] + b * D, P)]).then_inc(sem[f"raw_full{s}"], 16)
                else:
                    dst = raw[s][:, 0:kn * cn].rearrange("p (k c) -> p k c", c=cn)
                    ks = slice(k0, k0 + kn) if isinstance(k0, int) else bass.ds(k0, kn)
                    cs = slice(c0, c0 + cn) if isinstance(c0, int) else bass.ds(c0, cn)
                    sp.dma_start(dst, w[:, ks, cs]).then_inc(sem[f"raw_full{s}"], 16)

            def gemm(w, k0, kn, c0, cn, groups):
                load(w, k0, kn, c0, cn)
                S.split += 1

            def later_ada(w, c0, q, n_norm):
                sp.wait_ge(sem["u_lo"], n_norm)
                sp.wait_ge(sem[f"ada_empty{q % 2}"], p.after(f"ada_empty{q % 2}"))
                sp.dma_start(adaw[q % 2][:, :].rearrange("p (k c) -> p k c", c=P),
                             w[:, :, slice(c0, c0 + P) if isinstance(c0, int) else bass.ds(c0, P)]).then_inc(sem[f"ada_full{q % 2}"], 16)

            def per(gemms, adas, loads=1, convs=0):
                return {**{f"raw_empty{s}": gemms // 2 for s in range(2)}, **{f"ada_empty{s}": adas // 2 for s in range(2)}}

            def step(s, c, d, lat):
                sp.wait_ge(sem["step_done"], p.after("step_done"))
                toks = slice(c * P, c * P + P) if isinstance(c, int) else bass.ds(c * P, P)
                full = sem[f"step_full{s}"]
                sp.dma_start(xtb[s][:, :], xtokD[toks, 0:D + 2 * P]).then_inc(full, 16)
                if lat:
                    sp.dma_start(bcT[s][:, :, :], xbcT[D:XBC, toks].rearrange("(b p) t -> p b t", p=P)).then_inc(full, 16)
                    sp.dma_start(Abc[s][:, :, :], acsD[d * HEADS:(d + 1) * HEADS, toks].partition_broadcast(P)).then_inc(full, 16)

            def scan_loads():
                sp.wait_ge(sem["xs_stored"], 16 * XBT)
                sp.wait_ge(sem["xt_stored"], 16 * XBT)
                sp.wait_ge(sem["acs_loaded"], 16)
                sp.wait_ge(sem["tab_dve"], 6)
                for d in range(2):
                    for j in range(NCX):
                        step(j, NCH + (j if d == 0 else NCX - 1 - j), d, False)
                    with p.loop(NCH // 2, {"step_done": 2}) as i:
                        for j in range(2):
                            step(j, i * 2 + j if d == 0 else i * -2 + (NCH - 1 - j), d, True)

            walk(p, S, per, gemm, lambda w, c0, cn: load(w, 0, 8, c0, cn), later_ada, scan_loads)

        @block.gpsimd
        def _(pool):
            p = Program(pool, names, {})
            S = Stream()
            for n, k in credit.items():
                pool.sem_inc(sem[n], k * names[n])
            pool.memset(ident[:, :], 0.0).then_inc(sem["const_ready"], p.counted("const_ready"))
            pool.memset(ones[:, :], 1.0).then_inc(sem["const_ready"], p.counted("const_ready"))
            pool.memset(maskF[:, :], 1.0).then_inc(sem["const_ready"], p.counted("const_ready"))
            pool.memset(maskB[:, :], 1.0).then_inc(sem["const_ready"], p.counted("const_ready"))
            pool.wait_ge(sem["const_ready"], p.so_far("const_ready"))
            pool.affine_select(out=ident[:, :], in_=ident[:, :], compare_op=ALU.not_equal, fill=1.0, base=0,
                                      pattern=[[-1, P]], channel_multiplier=1).then_inc(sem["const_ready"], p.counted("const_ready"))
            pool.affine_select(out=maskF[:, :], in_=maskF[:, :], compare_op=ALU.is_ge, fill=0.0, base=0,
                                      pattern=[[1, P]], channel_multiplier=-1).then_inc(sem["const_ready"], p.counted("const_ready"))
            pool.affine_select(out=maskB[:, :], in_=maskB[:, :], compare_op=ALU.is_ge, fill=0.0, base=0,
                                      pattern=[[-1, P]], channel_multiplier=1).then_inc(sem["const_ready"], p.counted("const_ready"))
            pool.wait_ge(sem["const_ready"], p.so_far("const_ready"))

            ends = [None, None]

            def loop_ended():
                if in_loop[0] is not None:
                    c = p.cnt["group_done"].c
                    ends[:] = [c - in_loop[0], c]
                    in_loop[0] = None

            def enter():
                loop_ended()
                pool.wait_ge(sem["group_done"], ends[0])

            def gemm(w, k0, kn, c0, cn, groups):
                s, t = S.raw % 2, S.split % 2
                S.raw += 1
                S.split += 1
                n = kn * cn
                pool.wait_ge(sem[f"raw_full{s}"], p.after(f"raw_full{s}", 2 if isinstance(c0, tuple) else 1))
                if in_loop[0] is not None:
                    pool.wait_ge(sem["group_done"], p.so_far("group_done", -in_loop[0]))
                    in_loop[0] = groups
                elif ends[0] is not None:
                    pool.wait_ge(sem["group_done"], ends[0])
                p.skip("group_done", groups)
                if in_loop[0] is None:
                    ends[:] = [ends[1], p.cnt["group_done"].c]
                pool.sem_inc(sem["split_begun"], 1)
                pool.tensor_scalar(wh[t][:, 0:n], raw[s][:, 0:n], 1.0, None, ALU.mult).then_inc(sem["split_hi"], p.counted("split_hi"))
                pool.wait_ge(sem["split_hi"], p.so_far("split_hi"))
                pool.tensor_tensor(wl[t][:, 0:n], raw[s][:, 0:n], wh[t][:, 0:n].bitcast(F32), ALU.subtract).then_inc(sem[f"split_full{t}"], p.counted(f"split_full{t}"))
                pool.wait_ge(sem[f"split_full{t}"], p.so_far(f"split_full{t}"))
                pool.sem_inc(sem[f"raw_empty{s}"], 1)

            def ada(w, c0, cn):
                p.skip(f"raw_full{S.raw % 2}")
                S.raw += 1

            def per(gemms, adas, loads=1, convs=0):
                d = {f"raw_full{s}": gemms // 2 * loads for s in range(2)}
                for s in range(2):
                    d[f"split_full{s}"] = gemms // 2
                enter()
                in_loop[0] = 8 if gemms == 4 else 4
                return {**d, "split_hi": gemms, "group_done": 24 if gemms == 4 else 8,
                        "prod_ready": convs * POOL_TAPS, "prod_added": convs * (POOL_TAPS - 1)}

            def conv_tile():
                p.skip("prod_ready")
                for t in range(1, POOL_TAPS):
                    pool.wait_ge(sem["prod_ready"], p.after("prod_ready"))
                    if t > 1:
                        pool.wait_ge(sem["prod_added"], p.so_far("prod_added"))
                    pool.tensor_tensor(pacc[:, :], pacc[:, :], prod[t % 2][:, :], ALU.add).then_inc(sem["prod_added"], p.counted("prod_added"))

            def to_end(s):
                pool.wait_ge(sem["scal_ready"], p.after("scal_ready"))
                if p.begun("S_done"):
                    pool.wait_ge(sem["S_done"], p.so_far("S_done"))
                p.skip("S_done", 2)
                pool.tensor_tensor(xte[:, :].rearrange("p (h q) -> p h q", q=HD), xtb[s][:, 0:D].rearrange("p (h q) -> p h q", q=HD),
                                   scal[s][:, 2, :].unsqueeze(2).to_broadcast([P, HEADS, HD]),
                                   ALU.mult).then_inc(sem["xte_ready"], p.counted("xte_ready"))

            def scan_gates():
                for d in range(2):
                    for j in range(NCX):
                        pool.wait_ge(sem[f"step_full{j}"], p.after(f"step_full{j}"))
                        to_end(j)
                    with p.loop(NCH // 2, {"step_full0": 3, "step_full1": 3, "E_ready": 2, "CE_ready": 4, "scal_ready": 2,
                                           "S_done": 4, "xte_ready": 2}) as i:
                        for s in range(2):
                            pool.wait_ge(sem[f"step_full{s}"], p.after(f"step_full{s}", 3))
                            to_end(s)
                            pool.wait_ge(sem["E_ready"], p.after("E_ready"))
                            for g in range(2):
                                v = Eb[s][:, g * 8:(g + 1) * 8, :]
                                cT_ = bcT[s][:, 2 + g, :].unsqueeze(1).to_broadcast([P, 8, P])
                                pool.tensor_tensor(v, v, cT_, ALU.mult).then_inc(sem["CE_ready"], p.counted("CE_ready"))

            def stage(name):
                loop_ended()
                p.cnt["group_done"] = Lin({"xbc": 2 * NALL, "out": p.cnt["group_done"].c,
                                           "out2": p.cnt["group_done"].c + 2 + 2 * KT}[name])

            in_loop = [None]
            walk(p, S, per, gemm, ada, lambda w, c0, q, n_norm: None, scan_gates, stage, conv_tile)

        @block.tensor
        def _(pe):
            p = Program(pe, names, mirrored)
            S = Stream()
            prev = [None]
            bank = [0]

            def next_bank(evac, j):
                if j < 4 and prev[0] is not None and prev[0] != evac:
                    pe.wait_ge(sem[prev[0]], p.so_far(prev[0], j - 3))
                else:
                    pe.wait_ge(sem[evac], p.so_far(evac, -3))
                p.skip(evac)
                b = bank[0]
                bank[0] = (b + 1) % 4
                return b

            def mark(name):
                marks[name] = {n: p.cnt[n].c for n in SHARED}, bank[0]

            def drained(evac):
                if prev[0] is not None:
                    pe.wait_ge(sem[prev[0]], p.so_far(prev[0]))
                prev[0] = evac

            def unit(width, kn, tiles, segs, rhs, evac, j0, ready=None, loads=1, between=lambda n: None):
                t_ = S.split % 2
                S.raw += 1
                S.split += 1
                p.skip(f"raw_full{(S.raw - 1) % 2}", loads)
                pe.wait_ge(sem[f"split_full{t_}"], p.after(f"split_full{t_}"))
                order = [(t, s) for s in segs for t in range(tiles)]
                for n, (t, s) in enumerate(order):
                    b = next_bank(evac, j0 + n)
                    w = SEGS[s][1]
                    for k in range(kn):
                        if ready:
                            ready(n, t, s, k)
                        o = k * width + t * P
                        H, L = wh[t_][:, o:o + P], wl[t_][:, o:o + P]
                        xh, xl = rhs(k, s)
                        pe.matmul(PG[:, b, 0:w], H, xh, start=(k == 0), stop=False)
                        pe.matmul(PG[:, b, 0:w], H, xl, start=False, stop=False)
                        ins = pe.matmul(PG[:, b, 0:w], L, xh, start=False, stop=(k == kn - 1))
                    ins.then_inc(sem["group_done"], p.counted("group_done"))
                    between(n)

            def later_ada(q, out_col):
                s = q % 2
                pe.wait_ge(sem["ada_added"], p.after("ada_added"))
                pe.matmul(PM[:, 3, slice(out_col, out_col + 1) if isinstance(out_col, int) else bass.ds(out_col, 1)], adaw[s][:, 0:P], ones[:, 0:1],
                          start=True, stop=True).then_inc(sem[f"ada_empty{s}"], 1)

            def ada_unit(cols, out_col):
                s = S.raw % 2
                S.raw += 1
                pe.wait_ge(sem[f"raw_full{s}"], p.after(f"raw_full{s}"))
                for t in range(cols // P):
                    for k in range(KT):
                        o = out_col + 2 * t
                        dst = PM[:, 3, o:o + 2] if isinstance(o, int) else PM[:, 3, bass.ds(o, 2)]
                        ins = pe.matmul(dst, raw[s][:, k * cols + t * P:k * cols + (t + 1) * P],
                                        csil[:, k:k + 9:8], start=(k == 0), stop=(k == KT - 1))
                ins.then_inc(sem[f"raw_empty{s}"], 1)

            def per(gemms, adas, **more):
                d = {f"raw_full{s}": gemms // 2 for s in range(2)}
                for s in range(2):
                    d[f"split_full{s}"] = gemms // 2
                return {**d, "ada_added": adas, **more}

            pe.wait_ge(sem["const_ready"], 7)
            pe.wait_ge(sem["par_loaded"], 16 * (len(place)))
            for b in range(NB):
                n = min(P, n_rows - b * P)
                ins = pe.transpose(PM[:, b // 4, (b % 4) * P:(b % 4) * P + n], prow[0:n, b, :], ident[0:n, 0:n])
            ins.then_inc(sem["par_turned"], p.counted("par_turned"))
            prev[0] = "read_by_act"
            for c in range(NALL):
                pe.wait_ge(sem[f"xin_full{c % 2}"], p.after(f"xin_full{c % 2}"))
                for hf in range(2):
                    b = next_bank("read_by_act", 4)
                    for q in range(4):
                        ins = pe.transpose(PG[:, b, q * P:(q + 1) * P], xin[c % 2][:, (4 * hf + q) * P:(4 * hf + q + 1) * P],
                                           ident[:, :])
                    ins.then_inc(sem["group_done"], p.counted("group_done"))
                if c == 1:
                    pe.wait_ge(sem["silu_c"], 1)
                if c >= NALL - N_ADA0:
                    ada_unit(256, 4 * (c - (NALL - N_ADA0)))
            def stats(n, width=HALF):
                pe.wait_ge(sem["sq_added"], p.after("sq_added", n))
                p.skip("sq_ready", n + 1)
                if p.cnt["stat_done"].c >= 1:
                    pe.wait_ge(sem["ln_done"], p.cnt["stat_done"].c)
                pe.matmul(PM[:, 0, 0:width], ones[:, :], sacc[:, 0:width], start=True, stop=True).then_inc(sem["stat_done"], p.counted("stat_done"))

            def sums(k0, k1, n=KT):
                if k0 == 0 and p.cnt["stat_done"].c >= 1:
                    pe.wait_ge(sem["ln_done"], p.cnt["stat_done"].c)
                for k in range(k0, k1):
                    pe.wait_ge(sem["sq_ready"], p.after("sq_ready"))
                    name = "stat_done" if k == n - 1 else "sq_summed"
                    pe.matmul(PM[:, 0, :], ones[:, :], sq[k % 2][:, :], start=k == 0, stop=k == n - 1).then_inc(sem[name], p.counted(name))

            pe.wait_ge(sem["par_ready"], 2)
            sums(0, KT)
            u_base = {"n": 0}

            def u_ready(n, t, s, k):
                if t == 0:
                    pe.wait_ge(sem["u_lo"], u_base["n"] + s * KT + k + 1)

            def u_rhs(k, s):
                o, w = SEGS[s]
                return uh[:, k, o:o + w], ul[:, k, o:o + w]

            drained("read_by_act")
            mark("xbc")

            def turn(tt):
                pe.wait_ge(sem["xs_ready"], 2 * (tt + 1))
                if tt:
                    pe.wait_ge(sem["xt_copied"], tt)
                for c in range(NALL):
                    dst = PM[:, c // 4, (c % 4) * P:(c % 4 + 1) * P]
                    ins = pe.transpose(dst, xs[:, c * P:(c + 1) * P], ident[:, :])
                ins.then_inc(sem["xt_turned"], p.counted("xt_turned"))

            for u in range(N_XBC):
                t_ = S.split % 2
                S.raw += 1
                S.split += 1
                p.skip(f"raw_full{(S.raw - 1) % 2}")
                pe.wait_ge(sem[f"split_full{t_}"], p.after(f"split_full{t_}"))
                for t in range(2):
                    for s in range(3):
                        if u == 0 and t == 0 and s:
                            stats(KT - 1, SEGS[s][1])
                        b = next_bank("read_by_act", 4)
                        w = SEGS[s][1]
                        for k in range(KT):
                            if u == 0 and t == 0:
                                u_ready(0, 0, s, k)
                            o = k * 256 + t * P
                            H, L = wh[t_][:, o:o + P], wl[t_][:, o:o + P]
                            xh, xl = u_rhs(k, s)
                            pe.matmul(PG[:, b, 0:w], H, xh, start=(k == 0), stop=False)
                            pe.matmul(PG[:, b, 0:w], H, xl, start=False, stop=False)
                            ins = pe.matmul(PG[:, b, 0:w], L, xh, start=False, stop=(k == KT - 1))
                        ins.then_inc(sem["group_done"], p.counted("group_done"))
                    if 2 * u + t >= 1:
                        turn(2 * u + t - 1)
            unit(P, 8, 1, range(3), u_rhs, "read_by_act", 4)
            turn(XBT - 1)
            lat = range(2)
            mark("zg")
            for m0 in (16, 32):
                with S.loop(p, 2, 2, per(2, 8, group_done=8, read_by_act=8)) as i:
                    for j in range(2):
                        unit(256, 8, 2, lat, u_rhs, "read_by_act", 4,
                             between=lambda n: later_ada(4 * j + n, i * 16 + (2 * m0 + 2 * (4 * j + n))))
            mark("v")
            with S.loop(p, 2, 2, per(2, 0, group_done=8, read_by_act=8)) as i:
                for j in range(2):
                    t_ = S.split % 2
                    S.raw += 1
                    S.split += 1
                    p.skip(f"raw_full{(S.raw - 1) % 2}")
                    pe.wait_ge(sem[f"split_full{t_}"], p.after(f"split_full{t_}"))
                    for cc in range(NCH // 2):
                        b = next_bank("read_by_act", 4)
                        for c2 in range(2):
                            c = 2 * cc + c2
                            dst = PG[:, b, c2 * 256:(c2 + 1) * 256]
                            for k in range(KT):
                                H, L = wh[t_][:, k * 256:(k + 1) * 256], wl[t_][:, k * 256:(k + 1) * 256]
                                xh, xl = uh[:, k, c * P:(c + 1) * P], ul[:, k, c * P:(c + 1) * P]
                                pe.matmul(dst, xh, H, start=(k == 0), stop=False)
                                pe.matmul(dst, xl, H, start=False, stop=False)
                                ins = pe.matmul(dst, xh, L, start=False, stop=(k == KT - 1))
                        ins.then_inc(sem["group_done"], p.counted("group_done"))

            pe.wait_ge(sem["acs_loaded"], 16)
            pe.wait_ge(sem["xt_copied"], XBT)
            for c in range(NALL):
                pe.transpose(PM[:, 0, c * 32:(c + 1) * 32], rwq[:, c * P:(c + 1) * P], ident[0:32, 0:32])
                ins = pe.transpose(PM[:, 1, c * 32:(c + 1) * 32], rwdt[:, c * P:(c + 1) * P], ident[0:32, 0:32])
            ins.then_inc(sem["tab_turned"], p.counted("tab_turned"))
            pe.wait_ge(sem["tab_dve"], 3)
            pe.matmul(PM[:, 2, 0:NALL * 32], ones[:, :], dAt[:, :, :].rearrange("p c h -> p (c h)"),
                             start=True, stop=True).then_inc(sem["tot_done"], p.counted("tot_done"))

            def states(s):
                for g in range(2):
                    if p.begun("state_ready", -3):
                        pe.wait_ge(sem["state_ready"], p.so_far("state_ready", -3))
                    p.skip("state_ready")
                    pe.matmul(PG[:, 2 * s + g, :], xtb[s][:, D + g * P:D + (g + 1) * P], xte[:, g * 512:(g + 1) * 512],
                              start=True, stop=True).then_inc(sem["S_done"], p.counted("S_done"))

            drained("read_by_act")
            pe.wait_ge(sem["tab_dve"], 6)
            pe.wait_ge(sem["tab_act"], 2)
            for d in range(2):
                for s in range(NCX):
                    pe.wait_ge(sem[f"step_full{s}"], p.after(f"step_full{s}"))
                    pe.wait_ge(sem["xte_ready"], p.after("xte_ready"))
                    states(s)
                    p.skip("step_done")
                with p.loop(NCH // 2, {"step_full0": 3, "step_full1": 3, "xte_ready": 2, "xdt_ready": 4, "W_ready": 4,
                                       "CE_ready": 4, "sm_ready": 2, "scores_done": 2, "S_done": 4, "state_ready": 4,
                                       "y_done": 4, "y_added": 2, "step_done": 2}) as i:
                    for s in range(2):
                        pe.wait_ge(sem[f"step_full{s}"], p.after(f"step_full{s}", 3))
                        pe.wait_ge(sem["sm_ready"], p.so_far("sm_ready"))
                        p.skip("sm_ready")
                        for g in range(2):
                            ins = pe.matmul(PM[:, 0, g * P:(g + 1) * P], bcT[s][:, g, :], bcT[s][:, 2 + g, :],
                                            start=True, stop=True)
                        ins.then_inc(sem["scores_done"], p.counted("scores_done"))
                        pe.wait_ge(sem["state_ready"], p.so_far("state_ready"))
                        pe.wait_ge(sem["xte_ready"], p.after("xte_ready"))
                        states(s)
                        pe.wait_ge(sem["xdt_ready"], p.after("xdt_ready", 2))
                        for g in range(2):
                            read = ("y_added", "step_done")[g]
                            pe.wait_ge(sem[read], p.so_far(read))
                            p.skip(read)
                            heads = range(8 * g, 8 * g + 8)
                            dst = [PM[h % 2 * HD:h % 2 * HD + HD, 2 + g, (h // 2 % 4) * P:(h // 2 % 4 + 1) * P] for h in range(HEADS)]
                            pe.wait_ge(sem["CE_ready"], p.after("CE_ready"))
                            for h in heads:
                                pe.matmul(dst[h], st[s][:, h * HD:(h + 1) * HD], Eb[s][:, h, :], start=h % 8 < 2, stop=False)
                            pe.wait_ge(sem["W_ready"], p.after("W_ready"))
                            for h in heads:
                                ins = pe.matmul(dst[h], xd[s][g][:, h % 8 * HD:(h % 8 + 1) * HD], Wb[:, h, :], start=False, stop=h % 8 >= 6)
                            ins.then_inc(sem["y_done"], p.counted("y_done"))

            def project(hi, lo, ready, middle=lambda: None, norm_next=False):
                def between(u, n):
                    if u == 0 and n == 1:
                        middle()
                    if u == 3 and norm_next and n in (1, 2):
                        sums(4 * n - 4, 4 * n)

                for u in range(4):
                    unit(256, 8, 2, lat, lambda k, s: (hi[:, k, SEGS[s][0]:SEGS[s][0] + HALF], lo[:, k, SEGS[s][0]:SEGS[s][0] + HALF]),
                         "read_by_dve", 4, ready=ready if u == 0 else None, between=lambda n: between(u, n))

            def y_stats():
                for g in range(2):
                    stats(3)

            y_stats()
            u_base["n"] = 3 * KT
            drained("read_by_dve")
            mark("out")
            project(yh, yl, u_ready, middle=y_stats)
            pe.wait_ge(sem["sg_loaded"], 80)
            drained("read_by_dve")
            mark("sg")
            for g2 in range(2):
                b = next_bank("read_by_dve", 4)
                for q in range(4):
                    ins = pe.transpose(PG[:, b, q * P:(q + 1) * P], uf[g2][:, q * P:(q + 1) * P], ident[:, :])
                ins.then_inc(sem["group_done"], p.counted("group_done"))
            pe.wait_ge(sem["v_ready"], NCH)
            pe.wait_ge(sem["read_by_dve"], p.so_far("read_by_dve"))
            for g in range(KT):
                for s in lat:
                    b = next_bank("read_by_dve", 4)
                    for q in range(4):
                        dst = PG[:, b, q * P:(q + 1) * P]
                        pe.matmul(dst, vln[:, 4 * s + q, g * P:(g + 1) * P], sgwT[:, g, :], start=True, stop=False)
                        ins = pe.matmul(dst, ones[0:1, :], sgb(g), start=False, stop=True)
                    ins.then_inc(sem["group_done"], p.counted("group_done"))
            def sg_ready(n, t, s, k):
                if t == 0:
                    pe.wait_ge(sem["sg_lo"], 2 * k + s + 1)

            project(yh2, yl2, sg_ready, norm_next=True)
            u_base["n"] += 16

            def v_rhs(k, s):
                o, w = SEGS[s]
                return vh[:, k, o:o + w], vl[:, k, o:o + w]

            def h_rhs(j):
                return lambda k, s: (hh[:, k, SEGS[s][0]:SEGS[s][0] + HALF], hl[:, k, SEGS[s][0]:SEGS[s][0] + HALF])

            def mlp(l):
                adas = 6 if l == 0 else 0
                drained("read_by_dve")
                mark(f"mlp{l}")

                def between_1(i, n, first):
                    if first and n == 1:
                        stats(KT - 1)
                    if adas and n >= 8 - adas:
                        later_ada(n - 2, i * 12 + 2 * (n - 2))

                def between_2(n, last):
                    if last and l == 0 and 3 <= n < 7:
                        sums(2 * n - 6, 2 * n - 4)

                def turn(i, first=False, last=False):
                    prev[0] = "read_by_dve"
                    for j in range(2):
                        unit(256, 8, 2, lat, v_rhs, "read_by_act", 4 * j, ready=u_ready if first and j == 0 else None,
                             between=lambda n: between_1(i, 4 * j + n, first))
                    prev[0] = "read_by_act"
                    base = p.cnt["hid_lo"]

                    def hid_ready(n, t, s, k):
                        if t == 0:
                            p.cnt["hid_lo"] = base.plus((k // 2) * 4 + s * 2 + k % 2 + 1)
                            pe.wait_ge(sem["hid_lo"], p.so_far("hid_lo"))

                    for j in range(2):
                        unit(512, 4, 4, lat, h_rhs(j), "read_by_dve", 8 * j, ready=hid_ready if j == 0 else None,
                             between=lambda n: between_2(n, last and j == 1))
                    p.cnt["hid_lo"] = base.plus(8)

                turn(0, first=True)
                with S.loop(p, 6, 4, per(4, adas, group_done=24, read_by_act=8, read_by_dve=16, hid_lo=8)) as i:
                    turn(i + 1)
                turn(7, last=True)
                prev[0] = "read_by_dve"
                u_base["n"] += 16

            mlp(0)
            drained("read_by_act")
            mark("pw1")
            for u in range(2):
                unit(256, 8, 2, lat, v_rhs, "read_by_act", 4, ready=u_ready if u == 0 else None, loads=2,
                     between=lambda n: stats(KT - 1) if u == 0 and n == 1 else None)
            with S.loop(p, 3, 2, {**per(2, 0, group_done=8, read_by_act=8), "raw_full0": 2, "raw_full1": 2}) as i:
                for j in range(2):
                    unit(256, 8, 2, lat, v_rhs, "read_by_act", 4, loads=2)
            for k in range(KT):
                pe.wait_ge(sem["dw_done"], p.after("dw_done"))
                for s in lat:
                    ins = pe.matmul(PM[:, 1 + s, :], ones[:, :], cT[:, k, s * HALF:(s + 1) * HALF], start=k == 0, stop=k == KT - 1)
            ins.then_inc(sem["mean_done"], p.counted("mean_done"))
            sums(0, KT)
            u_base["n"] += 16
            drained("read_by_dve")
            mark("pw2")
            project(vh, vl, u_ready, middle=lambda: stats(KT - 1), norm_next=True)
            u_base["n"] += 16
            mlp(1)
            drained("read_by_act")
            mark("final")
            for c in range(NCH):
                for hf in range(2):
                    b = next_bank("read_by_act", 4)
                    for q in range(4):
                        ins = pe.transpose(PG[:, b, q * P:(q + 1) * P], hT[:, 4 * hf + q, c * P:(c + 1) * P], ident[:, :])
                    ins.then_inc(sem["group_done"], p.counted("group_done"))
        def part(w, items, by_pe=False):
            return w, items, by_pe

        def h_parts(g, l, shift, segs, dh, dl):
            got = []
            for s in segs:
                o, w = SEGS[s]
                j = 1 if s == 2 else 0
                src = (lambda k: hcT[:, k, :]) if s == 2 else (lambda k, o=o, w=w: hT[:, k, o:o + w])
                got.append(part(w, [(src(k), gsc[:, g + j, k:k + 1], mod[:, l, shift + k, j:j + 1],
                                     dh[:, k, o:o + w], dl[:, k, o:o + w]) for k in range(KT)], by_pe=s == 0))
            return got

        def y_parts():
            return [part(HALF, [(yT[:, k, s * HALF:(s + 1) * HALF], col("ssd_g", k), None,
                                 yh[:, k, s * HALF:(s + 1) * HALF], yl[:, k, s * HALF:(s + 1) * HALF])
                                for k in range(4 * g, 4 * g + 4)]) for s in range(2) for g in range(2)]

        def c_parts(s):
            return [part(HALF, [(cT[:, k, s * HALF:(s + 1) * HALF], col("ln_g", k), col("ln_b", k),
                                 vh[:, k, s * HALF:(s + 1) * HALF], vl[:, k, s * HALF:(s + 1) * HALF]) for k in range(KT)], by_pe=s == 0)]

        behind_projection = lambda k, s: (k // 2) * 4 + s * 2 + k % 2 + 1
        behind_mlp = lambda k, s: (k // 4) * 8 + s * 4 + k % 4 + 1

        def norm_act(p, act, parts, dim, func=ACT.Identity, behind=None, mods=0):
            for s, (w, items, by_pe) in enumerate(parts):
                for k, it in enumerate(items):
                    if behind:
                        act.wait_ge(sem["read_by_dve"], p.so_far("read_by_dve", behind(k, s) - 16))
                    if by_pe:
                        if k > 1:
                            act.wait_ge(sem["sq_summed"], p.after("sq_summed"))
                        act.activation(sq[k % 2][:, 0:w], it[0], ACT.Square).then_inc(sem["sq_ready"], p.counted("sq_ready"))
                        continue
                    if k:
                        if p.begun("sq_added", -1):
                            act.wait_ge(sem["sq_added"], p.so_far("sq_added", -1))
                        p.skip("sq_added")
                    dst = sq[k % 2] if k else sacc
                    act.activation(dst[:, 0:w], it[0], ACT.Square).then_inc(sem["sq_ready"], p.counted("sq_ready"))
                if by_pe:
                    p.skip("sq_summed")
                act.wait_ge(sem["stat_done"], p.after("stat_done"))
                r = rs[0]
                if mods:
                    act.wait_ge(sem["mod_ready"], mods)
                if p.begun("norm_mul"):
                    act.wait_ge(sem["norm_mul"], p.so_far("norm_mul"))
                act.activation(r[:, 0:w], PM[:, 0, 0:w], ACT.Ln, bias=EPS, scale=1.0 / dim).then_inc(sem["ln_done"], p.counted("ln_done"))
                act.wait_ge(sem["ln_done"], p.so_far("ln_done"))
                act.activation(r[:, 0:w], r[:, 0:w], ACT.Exp, scale=-0.5).then_inc(sem["rstd_ready"], p.counted("rstd_ready"))
                for k, (src, g, b, hi, lo) in enumerate(items):
                    act.wait_ge(sem["norm_mul"], p.after("norm_mul"))
                    if p.begun("u_lo", -1):
                        act.wait_ge(sem["u_lo"], p.so_far("u_lo", -1))
                    p.skip("u_lo")
                    if b is None:
                        act.activation(uf[k % 2][:, 0:w], tm[k % 2][:, 0:w], func, scale=g).then_inc(sem["uf_ready"], p.counted("uf_ready"))
                    else:
                        act.activation(uf[k % 2][:, 0:w], tm[k % 2][:, 0:w], func, scale=g, bias=b).then_inc(sem["uf_ready"], p.counted("uf_ready"))
                    act.wait_ge(sem["uf_ready"], p.so_far("uf_ready"))
                    act.activation(hi, uf[k % 2][:, 0:w], ACT.Copy).then_inc(sem["u_hi"], p.counted("u_hi"))

        def norm_dve(p, dve, parts):
            for w, items, by_pe in parts:
                if by_pe:
                    p.skip("sq_ready", len(items))
                else:
                    dve.wait_ge(sem["sq_ready"], p.after("sq_ready"))
                for k in range(1, 1 if by_pe else len(items)):
                    dve.wait_ge(sem["sq_ready"], p.after("sq_ready"))
                    if k > 1:
                        dve.wait_ge(sem["sq_added"], p.so_far("sq_added"))
                    dve.tensor_tensor(sacc[:, 0:w], sacc[:, 0:w], sq[k % 2][:, 0:w], ALU.add).then_inc(sem["sq_added"], p.counted("sq_added"))
                dve.wait_ge(sem["rstd_ready"], p.after("rstd_ready"))

                def lo_part(k):
                    dve.wait_ge(sem["u_hi"], p.after("u_hi"))
                    hi, lo = items[k][3], items[k][4]
                    dve.tensor_tensor(lo, uf[k % 2][:, 0:w], hi.bitcast(F32), ALU.subtract).then_inc(sem["u_lo"], p.counted("u_lo"))

                for k, it in enumerate(items):
                    if p.begun("uf_ready", -1):
                        dve.wait_ge(sem["uf_ready"], p.so_far("uf_ready", -1))
                    p.skip("uf_ready")
                    dve.tensor_tensor(tm[k % 2][:, 0:w], it[0], rs[0][:, 0:w], ALU.mult).then_inc(sem["norm_mul"], p.counted("norm_mul"))
                    if k:
                        lo_part(k - 1)
                lo_part(len(items) - 1)

        def at(p, name):
            counts, p.bank = marks[name]
            for n, c in counts.items():
                p.cnt[n] = Lin(c)

        @block.scalar
        def _(act):
            p = Program(act, names, mirrored)
            p.bank = 0

            def group(fn, evac=True):
                b = p.bank
                p.bank = (b + 1) % 4
                act.wait_ge(sem["group_done"], p.after("group_done"))
                return fn(b).then_inc(sem["read_by_act"], p.counted("read_by_act"))

            for blk, q0, k, ap, s0 in place:
                act.dma_start(prow[q0:q0 + k, blk, :], ap[s0:s0 + k]).then_inc(sem["par_loaded"], p.counted("par_loaded"))
            x2, c2 = a["x"][0], a["ctx"][0]
            tok_rows = lambda c: x2[c * P:(c + 1) * P, :] if c < NCH else c2[(c - NCH) * P:(c - NCH + 1) * P, :]
            for c in range(2):
                act.dma_start(xin[c][:, :], tok_rows(c)).then_inc(sem[f"xin_full{c}"], 16)
            rec = a["ssd_a_log"].rearrange("a b h -> (a b h)")
            act.dma_start(alog[:, :], rec.unsqueeze(1)).then_inc(sem["rec_loaded"], p.counted("rec_loaded"))
            act.dma_start(a_bc[:, :], rec.partition_broadcast(P)).then_inc(sem["rec_loaded"], p.counted("rec_loaded"))
            act.dma_start(dtb[:, :], a["ssd_dt_bias"].rearrange("a b h -> (a b h)").unsqueeze(1)).then_inc(sem["rec_loaded"], p.counted("rec_loaded"))
            act.dma_start(d_bc[:, :], a["ssd_d"].rearrange("a h -> (a h)").partition_broadcast(P)).then_inc(sem["rec_loaded"], p.counted("rec_loaded"))
            act.wait_ge(sem["par_turned"], 1)
            flat = par[:, :, :].rearrange("p b q -> p (b q)")
            act.activation(flat[:, 0:512], PM[:, 0, :], ACT.Copy).then_inc(sem["par_ready"], p.counted("par_ready"))
            act.activation(flat[:, 512:n_rows], PM[:, 1, 0:n_rows - 512], ACT.Copy).then_inc(sem["par_ready"], p.counted("par_ready"))
            act.wait_ge(sem["par_ready"], p.so_far("par_ready"))
            act.activation(csil[:, :], col("c", 0, 16), ACT.Silu).then_inc(sem["silu_c"], p.counted("silu_c"))
            for c in range(NALL):
                for hf in range(2):
                    dst = hT[:, 4 * hf:4 * hf + 4, c * P:(c + 1) * P] if c < NCH else \
                        hcT[:, 4 * hf:4 * hf + 4, (c - NCH) * P:(c - NCH + 1) * P]
                    group(lambda b: act.activation(dst, PG[:, b, :].rearrange("p (q t) -> p q t", t=P), ACT.Copy))
                if c + 2 < NALL:
                    act.dma_start(xin[c % 2][:, :], tok_rows(c + 2)).then_inc(sem[f"xin_full{c % 2}"], 16)
            act.wait_ge(sem["read_by_act"], p.so_far("read_by_act"))
            norm_act(p, act, h_parts(0, 0, 0, range(3), uh, ul), D, mods=3)

            at(p, "xbc")
            act.wait_ge(sem["pads_ready"], 2)

            def silu(tt):
                act.wait_ge(sem["conv_done"], tt + 1)
                act.wait_ge(sem["xt_turned"], tt)
                act.wait_ge(sem["xs_stored"], 16 * tt)
                act.activation(xs[:, 0:TOK], cv[:, 0:TOK], ACT.Silu).then_inc(sem["xs_ready"], p.counted("xs_ready"))
                act.activation(xs[:, TOK:ALL], cv[:, TOK + 4:TOK + 4 + CTX], ACT.Silu).then_inc(sem["xs_ready"], p.counted("xs_ready"))
                act.wait_ge(sem["xs_ready"], p.so_far("xs_ready"))
                act.dma_start(xbcT[tt * P:(tt + 1) * P, :], xs[:, :]).then_inc(sem["xs_stored"], p.counted("xs_stored"))

            def store_turned(tt):
                act.wait_ge(sem["xt_copied"], tt + 1)
                act.dma_start(xtokD.rearrange("(c p) n -> p c n", p=P)[:, :, tt * P:(tt + 1) * P], xtk[:, :, :]).then_inc(sem["xt_stored"], p.counted("xt_stored"))

            for tt in range(XBT):
                for s in range(3):
                    o, w = SEGS[s]
                    q = 2 + o + (4 if s == 2 else 0)
                    if s == 0 and tt >= 2:
                        act.wait_ge(sem["conv_done"], tt - 1)
                    group(lambda b: act.activation(xp[tt % 2][:, q:q + w], PG[:, b, 0:w], ACT.Copy))
                    if s == 0 and tt >= 1:
                        silu(tt - 1)
                        if tt >= 2:
                            store_turned(tt - 2)
            silu(XBT - 1)
            store_turned(XBT - 2)
            store_turned(XBT - 1)
            act.wait_ge(sem["xs_stored"], 16 * XBT)
            act.wait_ge(sem["xt_stored"], 16 * XBT)
            act.wait_ge(sem["rec_loaded"], 64)
            for s in range(3):
                o, w = SEGS[s]
                group(lambda b: act.activation(rwx[:, o:o + w], PG[0:R32, b, 0:w], ACT.Identity, bias=dtb[:, 0:1]))
            act.wait_ge(sem["read_by_act"], p.so_far("read_by_act"))
            act.activation(rwe[:, :], rwx[:, :], ACT.Abs).then_inc(sem["row_act"], p.counted("row_act"))
            act.wait_ge(sem["row_act"], p.so_far("row_act"))
            act.activation(rwe[:, :], rwe[:, :], ACT.Exp, scale=-1.0).then_inc(sem["row_act"], p.counted("row_act"))
            act.activation(alog[:, :], alog[:, :], ACT.Exp).then_inc(sem["row_act"], p.counted("row_act"))
            act.activation(a_bc[:, :], a_bc[:, :], ACT.Exp).then_inc(sem["row_act"], p.counted("row_act"))

            def zo_loop(n_units, func, dst):
                per = {"group_done": 8, "read_by_act": 8, **{f"zo_stored{b}": 2 for b in range(4)}}
                with p.loop(2, per) as i:
                    for j in range(2):
                        for n in range(4):
                            b = p.bank
                            act.wait_ge(sem[f"zo_stored{b}"], p.so_far(f"zo_stored{b}"))
                            group(lambda b: act.activation(zo[b][:, :], PG[:, b, :], func))
                            act.wait_ge(sem["read_by_act"], p.so_far("read_by_act"))
                            act.dma_start(*dst(i, j, n, b)).then_inc(sem[f"zo_stored{b}"], p.counted(f"zo_stored{b}"))

            def by_feature(t):
                def dst(i, j, n, b):
                    s, q = n // 2, n % 2
                    return t[bass.ds(i * 512 + (j * 256 + q * P), P), s * HALF:(s + 1) * HALF], zo[b][:, :]
                return dst

            zo_loop(4, ACT.Silu, by_feature(zT))
            zo_loop(4, ACT.Gelu_apprx_tanh, by_feature(guT))
            act.wait_ge(sem["row_dve"], 3 + 12 + 2 * NALL)
            act.dma_start(acsD[0:HEADS, :], rwx[0:HEADS, :]).then_inc(sem["acs_stored"], p.counted("acs_stored"))
            act.dma_start(acsD[HEADS:2 * HEADS, :], rwe[HEADS:2 * HEADS, :]).then_inc(sem["acs_stored"], p.counted("acs_stored"))
            act.wait_ge(sem["acs_stored"], 32)
            act.dma_start(rwq[:, :], acsD[:, :]).then_inc(sem["acs_loaded"], p.counted("acs_loaded"))
            v3 = vtok.rearrange("(c p) n -> p c n", p=P)
            zo_loop(4, ACT.Gelu_apprx_tanh,
                    lambda i, j, n, b: (v3[:, 2 * n:2 * n + 2, bass.ds(i * 512 + j * 256, 256)],
                                        zo[b][:, :].rearrange("p (c n) -> p c n", c=2)))

            act.wait_ge(sem["tab_dve"], 5)
            act.activation(te[:, :, :], te[:, :, :], ACT.Exp).then_inc(sem["tab_act"], p.counted("tab_act"))
            act.activation(tab[:, :, :, 3, :], PM[:, 2, 0:NALL * R32].rearrange("p (c d h) -> p c d h", d=2, h=HEADS),
                                  ACT.Exp).then_inc(sem["tab_act"], p.counted("tab_act"))
            for d in range(2):
                for s in range(NCX):
                    p.skip(f"step_full{s}")
                    p.skip("scal_ready")
                with p.loop(NCH // 2, {"step_full0": 3, "step_full1": 3, "scal_ready": 2, "y_done": 4, "E_ready": 2,
                                       "seg_ready": 4, "D_exp": 4}) as i:
                    for s in range(2):
                        act.wait_ge(sem[f"step_full{s}"], p.after(f"step_full{s}", 3))
                        act.activation(Eb[s][:, :, :], Abc[s][:, :, :], ACT.Exp).then_inc(sem["E_ready"], p.counted("E_ready"))
                        act.wait_ge(sem["scal_ready"], p.after("scal_ready"))
                        for g in range(2):
                            act.wait_ge(sem["y_done"], p.so_far("y_done", g - 1))
                            for h in range(8 * g, 8 * g + 8):
                                ins = act.activation(Wb[:, h, :], Abc[s][:, h, :], ACT.Relu, bias=scal[s][:, 0, h:h + 1], scale=-1.0)
                            ins.then_inc(sem["seg_ready"], p.counted("seg_ready"))
                            act.wait_ge(sem["seg_ready"], p.so_far("seg_ready"))
                            v = Wb[:, 8 * g:8 * g + 8, :]
                            act.activation(v, v, ACT.Exp, scale=-1.0).then_inc(sem["D_exp"], p.counted("D_exp"))
                        p.skip("y_done", 2)
            act.wait_ge(sem["step_done"], 2 + 2 * NALL)
            for b in range(4):
                act.wait_ge(sem[f"zo_stored{b}"], p.so_far(f"zo_stored{b}"))
            for k in range(KT):
                for q, t in ((0, xbcT), (1, zT)):
                    b = q
                    if k >= 1:
                        act.wait_ge(sem["fin_dve"], 2 * (k - 1) + q + 1)
                    act.dma_start(ld[b][:, :], t[k * P:(k + 1) * P, 0:TOK]).then_inc(sem[f"ld_full{b}"], 16)
            act.wait_ge(sem["fin_dve"], 2 * KT)
            norm_act(p, act, y_parts(), D // 2)

            act.wait_ge(sem["u_lo"], p.so_far("u_lo"))
            for q in range(2):
                act.dma_start(uf[q][:, :].rearrange("p (g k) -> p g k", k=P),
                                     a["sg_w"][0, 4 * q:4 * q + 4].rearrange("g q k -> q g k")).then_inc(sem["sg_loaded"], p.counted("sg_loaded"))
                act.dma_start((sacc, rs[0])[q][0:1, :], a["sg_b"][0, 4 * q:4 * q + 4].rearrange("g q -> (g q)").unsqueeze(0)).then_inc(sem["sg_loaded"], p.counted("sg_loaded"))
            act.dma_start(lnrow[:, :], a["sg_ln_g"].rearrange("a d -> (a d)").partition_broadcast(P)).then_inc(sem["sg_loaded"], p.counted("sg_loaded"))
            act.dma_start(vln[:, :, :], v3).then_inc(sem["v_loaded"], p.counted("v_loaded"))
            at(p, "out")
            p.skip("group_done", 16)
            act.wait_ge(sem["v_dve"], 3 * NCH)
            act.activation(rstd[:, :, :], mv[:, :, 1:2], ACT.Ln, bias=EPS).then_inc(sem["v_act"], p.counted("v_act"))
            act.wait_ge(sem["v_act"], p.so_far("v_act"))
            act.activation(rstd[:, :, :], rstd[:, :, :], ACT.Exp, scale=-0.5).then_inc(sem["v_act"], p.counted("v_act"))
            act.wait_ge(sem["v_dve"], 5 * NCH)
            act.dma_start(lnrow[:, :], a["sg_ln_b"].rearrange("a d -> (a d)").partition_broadcast(P)).then_inc(sem["sg_loaded"], p.counted("sg_loaded"))
            at(p, "sg")
            p.skip("read_by_dve", 2)
            act.wait_ge(sem["read_by_dve"], p.so_far("read_by_dve"))
            for g in range(KT):
                for s in range(2):
                    if g:
                        act.wait_ge(sem["sg_lo"], 2 * (g - 1) + s + 1)
                    act.dma_start(gu[s][:, :], guT[g * P:(g + 1) * P, s * HALF:(s + 1) * HALF]).then_inc(sem[f"gu_full{s}"], 16)
                for s in range(2):
                    act.wait_ge(sem["read_by_dve"], p.after("read_by_dve"))
                    act.activation(yh2[:, g, s * HALF:(s + 1) * HALF], tm[s][:, :], ACT.Copy).then_inc(sem["sg_hi"], p.counted("sg_hi"))

            def mlp(l):
                at(p, f"mlp{l}")
                norm_act(p, act, h_parts(2 if l == 0 else 4, l, 24, range(2), vh, vl), D, behind=behind_projection, mods=5)
                with p.loop(8, {"group_done": 24, "read_by_act": 8, "relu_sq": 8}) as i:
                    for m in range(8):
                        act.wait_ge(sem["relu_sq"], p.so_far("relu_sq", -1))
                        p.skip("relu_sq")
                        group(lambda b: act.activation(sq[m % 2][:, :], PG[:, b, :], ACT.Relu))
                    p.skip("group_done", 16)
                act.wait_ge(sem["read_by_act"], p.so_far("read_by_act"))

            mlp(0)
            at(p, "pw1")
            norm_act(p, act, h_parts(3, 1, 0, range(2), vh, vl), D, behind=behind_mlp, mods=9)
            def products(k, taps):
                act.wait_ge(sem["glu_done"], 2 * k + 2)
                for t in taps:
                    tap = CW - POOL_TAPS + t
                    if t == 0:
                        if k:
                            act.wait_ge(sem["dw_done"], k)
                    elif k * (POOL_TAPS - 1) + t - 2 > 0:
                        act.wait_ge(sem["prod_added"], k * (POOL_TAPS - 1) + t - 2)
                    dst = prod[t % 2] if t else pacc
                    act.activation(dst[:, :], apad[k % 2][:, tap:tap + TOK], ACT.Copy, scale=col("w_dw", tap * KT + k)).then_inc(sem["prod_ready"], p.counted("prod_ready"))

            for k in range(KT + 1):
                for s in range(2):
                    if k:
                        products(k - 1, range(5 * s, 5 + (POOL_TAPS - 5) * s))
                    if k == KT:
                        continue
                    m = 2 * k + s
                    if m >= 1:
                        act.wait_ge(sem["glu_done"], m)
                    group(lambda b: act.activation(tm[0][:, :], PG[:, b, :], ACT.Identity, bias=col("b_pw1", k)))
                    group(lambda b: act.activation(tm[1][:, :], PG[:, b, :], ACT.Sigmoid, bias=col("b_pw1", KT + k)))
            for s in range(2):
                act.wait_ge(sem["ln_dve"], KT * (s + 1))
                norm_act(p, act, c_parts(s), D, ACT.Silu)
            mlp(1)
            at(p, "final")
            act.wait_ge(sem["group_done"], p.so_far("group_done", 1))
            act.dma_start(fg[:, :], a["final_norm_g"].partition_broadcast(P)).then_inc(sem["fg_loaded"], p.counted("fg_loaded"))
            for c in range(NCH):
                if p.begun(f"out_stored{c % 2}"):
                    act.wait_ge(sem[f"out_stored{c % 2}"], p.so_far(f"out_stored{c % 2}"))
                for hf in range(2):
                    group(lambda b: act.activation(fo[c % 2][:, hf * 512:(hf + 1) * 512], PG[:, b, :], ACT.Copy))
                act.wait_ge(sem["read_by_act"], p.so_far("read_by_act"))
                act.activation(fs[:, :], fo[c % 2][:, :], ACT.Square, accum_out=fm[:, c, :]).then_inc(sem["out_act"], p.counted("out_act"))
                act.wait_ge(sem["out_act"], p.so_far("out_act"))
                act.activation(fm[:, c, :], fm[:, c, :], ACT.Ln, bias=EPS, scale=1.0 / D).then_inc(sem["out_act"], p.counted("out_act"))
                act.wait_ge(sem["out_act"], p.so_far("out_act"))
                act.activation(fm[:, c, :], fm[:, c, :], ACT.Exp, scale=-0.5).then_inc(sem["out_act"], p.counted("out_act"))
                act.wait_ge(sem["out_dve"], c + 1)
                act.dma_start(out[0, c * P:(c + 1) * P, :], fo[c % 2][:, :]).then_inc(sem[f"out_stored{c % 2}"], p.counted(f"out_stored{c % 2}"))
            for q in range(2):
                act.wait_ge(sem[f"out_stored{q}"], p.so_far(f"out_stored{q}"))

        @block.vector
        def _(dve):
            p = Program(dve, names, mirrored)
            p.bank = 0

            def group(fn):
                b = p.bank
                p.bank = (b + 1) % 4
                dve.wait_ge(sem["group_done"], p.after("group_done"))
                return fn(b).then_inc(sem["read_by_dve"], p.counted("read_by_dve"))

            def add_ada(l, t0, n, nj=1):
                src = PM[:, 3, 2 * t0:2 * (t0 + n)].rearrange("p (t j) -> p t j", j=2)[:, :, 0:nj]
                b = col("ada_b", l * 48 + t0, n).unsqueeze(2).to_broadcast([P, n, nj])
                dve.tensor_tensor(mod[:, l, t0:t0 + n, 0:nj], src, b, ALU.add).then_inc(sem["mod_ready"], p.counted("mod_ready"))
                dve.wait_ge(sem["mod_ready"], p.so_far("mod_ready"))

            def later_ada(q):
                s = q % 2
                dve.wait_ge(sem[f"ada_full{s}"], p.after(f"ada_full{s}"))
                v = adaw[s][:, :].rearrange("p (k c) -> p k c", c=P)
                dve.tensor_tensor(v, v, csil[:, 0:KT].unsqueeze(2).to_broadcast([P, KT, P]), ALU.mult).then_inc(sem["ada_step"], p.counted("ada_step"))
                for n in (4, 2, 1):
                    dve.wait_ge(sem["ada_step"], p.so_far("ada_step"))
                    name = "ada_step" if n > 1 else "ada_added"
                    dve.tensor_tensor(v[:, 0:n], v[:, 0:n], v[:, n:2 * n], ALU.add).then_inc(sem[name], p.counted(name))

            def gain(idx, l, t0, j, g):
                dve.scalar_tensor_tensor(out=gsc[:, idx, :], in0=mod[:, l, t0:t0 + KT, j], scalar=1.0, in1=g,
                                                op0=ALU.add, op1=ALU.mult).then_inc(sem["mod_ready"], p.counted("mod_ready"))

            dve.wait_ge(sem["par_ready"], 2)
            for s in range(2):
                dve.wait_ge(sem[f"raw_empty{s}"], 1 + N_ADA0 // 2)
            add_ada(0, 0, 16, 2)
            gain(0, 0, 8, 0, col("mix_g", 0, KT))
            gain(1, 0, 8, 1, col("mix_g", 0, KT))
            dve.wait_ge(sem["rec_loaded"], 64)
            for q in range(2):
                v = slice(q * HD, (q + 1) * HD)
                dve.tensor_copy(dsk[v, :], d_bc[v, q:HEADS:2]).then_inc(sem["skip_ready"], p.counted("skip_ready"))
            norm_dve(p, dve, h_parts(0, 0, 0, range(3), uh, ul))

            at(p, "xbc")
            for q in range(2):
                dve.memset(xp[q][:, :], 0.0).then_inc(sem["pads_ready"], p.counted("pads_ready"))

            def copy_turned(tt):
                dve.wait_ge(sem["xt_turned"], tt + 1)
                if tt:
                    dve.wait_ge(sem["xt_stored"], 16 * tt)
                dve.tensor_copy(xtk[:, :, :].rearrange("p c t -> p (c t)"),
                                       PM[:, 0:3, :].rearrange("p b n -> p (b n)")[:, 0:ALL]).then_inc(sem["xt_copied"], p.counted("xt_copied"))

            for tt in range(XBT):
                p.skip("read_by_act", 3)
                dve.wait_ge(sem["read_by_act"], p.so_far("read_by_act"))
                n = PADW - 4
                if tt:
                    dve.wait_ge(sem["xs_ready"], 2 * tt)
                dve.tensor_scalar(cv[:, 0:n], xp[tt % 2][:, 0:n], col("conv_w", tt), col("conv_b", tt), ALU.mult, ALU.add).then_inc(sem["conv_step"], p.counted("conv_step"))
                for tap in range(1, CONV):
                    dve.wait_ge(sem["conv_step"], p.so_far("conv_step"))
                    dve.scalar_tensor_tensor(out=cv[:, 0:n], in0=xp[tt % 2][:, tap:tap + n],
                                                    scalar=col("conv_w", tap * XBT + tt), in1=cv[:, 0:n], op0=ALU.mult,
                                                    op1=ALU.add).then_inc(sem["conv_done" if tap == CONV - 1 else "conv_step"], p.counted("conv_done" if tap == CONV - 1 else "conv_step"))
                if tt:
                    copy_turned(tt - 1)
            copy_turned(XBT - 1)

            with p.loop(2, {"ada_full0": 4, "ada_full1": 4, "ada_step": 24, "ada_added": 8}) as i:
                for q in range(8):
                    later_ada(q)
            dve.wait_ge(sem["row_act"], 4)

            def row(ins):
                ins.then_inc(sem["row_dve"], p.counted("row_dve"))
                dve.wait_ge(sem["row_dve"], p.so_far("row_dve"))

            row(dve.tensor_scalar(rwq[:, :], rwe[:, :], 2.0, None, ALU.add))
            row(dve.reciprocal(rwq[:, :], rwq[:, :]))
            later_ada(0)
            row(dve.tensor_tensor(rwe[:, :], rwe[:, :], rwq[:, :], ALU.mult))
            row(dve.tensor_tensor(rwq[:, :], rwe[:, :], rwe[:, :], ALU.mult))
            later_ada(1)
            row(dve.tensor_scalar(rwp[:, :], rwq[:, :], 1.0 / 13, None, ALU.mult))
            for q, n in enumerate((11, 9, 7, 5, 3)):
                row(dve.scalar_tensor_tensor(out=rwp[:, :], in0=rwp[:, :], scalar=1.0 / n, in1=rwq[:, :], op0=ALU.add, op1=ALU.mult))
                later_ada(2 + q)
            row(dve.scalar_tensor_tensor(out=rwp[:, :], in0=rwp[:, :], scalar=1.0, in1=rwe[:, :], op0=ALU.add, op1=ALU.mult))
            later_ada(7)
            row(dve.tensor_scalar(rwx[:, :], rwx[:, :], 0.0, None, ALU.max))
            later_ada(8)
            row(dve.scalar_tensor_tensor(out=rwdt[:, :], in0=rwp[:, :], scalar=2.0, in1=rwx[:, :], op0=ALU.mult, op1=ALU.add))
            later_ada(9)
            row(dve.tensor_scalar(rwp[:, :], rwdt[:, :], alog[:, 0:1], -1.0, ALU.mult, ALU.mult))
            row(dve.tensor_scalar(a_bc[:, :], a_bc[:, :], -1.0, None, ALU.mult))
            later_ada(10)
            for c in range(NALL):
                v = slice(c * P, (c + 1) * P)
                if c % 2 == 1:
                    later_ada(11 + c // 2)
                dve.tensor_tensor_scan(rwx[:, v], ones[0:R32, :], rwp[:, v], 0.0, ALU.mult, ALU.add).then_inc(sem["row_dve"], p.counted("row_dve"))
                dve.tensor_tensor_scan(rwe[:, v][:, ::-1], ones[0:R32, :], rwp[:, v][:, ::-1], 0.0, ALU.mult, ALU.add).then_inc(sem["row_dve"], p.counted("row_dve"))

            for s in range(2):
                dve.wait_ge(sem[f"ada_empty{s}"], ADA_FREED[0])
            add_ada(0, 16, 32)
            gain(2, 0, 32, 0, col("mlp_g", 0, KT))

            dve.wait_ge(sem["tab_turned"], 1)
            view = lambda b: PM[:, b, 0:NALL * R32].rearrange("p (c d h) -> p c d h", d=2, h=HEADS)
            te4 = te[:, :, :].rearrange("p c (d h) -> p c d h", h=HEADS)
            dve.tensor_copy(tab[:, :, :, 0, :], view(0)).then_inc(sem["tab_dve"], p.counted("tab_dve"))
            dve.tensor_copy(tab[:, :, :, 1, :], view(1)).then_inc(sem["tab_dve"], p.counted("tab_dve"))
            dve.wait_ge(sem["tab_dve"], p.so_far("tab_dve"))
            dve.tensor_tensor(dAt[:, :, :], PM[:, 1, 0:NALL * R32].rearrange("p (c h) -> p c h", h=R32),
                                     a_bc[:, :].unsqueeze(1).to_broadcast([P, NALL, R32]), ALU.mult).then_inc(sem["tab_dve"], p.counted("tab_dve"))
            dve.wait_ge(sem["tot_done"], p.after("tot_done"))
            dve.tensor_tensor(te4, view(2), tab[:, :, :, 0, :], ALU.subtract).then_inc(sem["tab_dve"], p.counted("tab_dve"))
            dve.wait_ge(sem["tab_dve"], p.so_far("tab_dve"))
            dve.tensor_scalar(te[:, :, :], te[:, :, :], 0.0, None, ALU.min).then_inc(sem["tab_dve"], p.counted("tab_dve"))
            dve.wait_ge(sem["tab_act"], p.after("tab_act", 2))
            dve.tensor_tensor(tab[:, :, :, 2, :], te4, tab[:, :, :, 1, :], ALU.mult).then_inc(sem["tab_dve"], p.counted("tab_dve"))
            dve.wait_ge(sem["tab_dve"], p.so_far("tab_dve"))
            dve.memset(yT[:, :, :], 0.0).then_inc(sem["y_cleared"], p.counted("y_cleared"))
            dve.wait_ge(sem["y_cleared"], p.so_far("y_cleared"))

            wide = lambda t: t[:, :].rearrange("p (h q) -> p h q", q=HD)

            def scalars(s, c, d):
                src = tab[:, c:c + 1, d, :, :] if isinstance(c, int) else tab[:, bass.ds(c, 1), d, :, :]
                dve.wait_ge(sem["step_done"], p.so_far("step_done"))
                dve.wait_ge(sem["par_ready"], 2)
                dve.tensor_copy(scal[s][:, :, :].unsqueeze(1), src).then_inc(sem["scal_ready"], p.counted("scal_ready"))
                dve.wait_ge(sem["scal_ready"], p.so_far("scal_ready"))

            def prepare(s, c, d):
                dve.wait_ge(sem[f"step_full{s}"], p.after(f"step_full{s}", 3))
                scalars(s, c, d)
                for g in range(2):
                    dve.tensor_tensor(wide(xd[s][g]), xtb[s][:, g * 512:(g + 1) * 512].rearrange("p (h q) -> p h q", q=HD),
                                      scal[s][:, 1, g * 8:(g + 1) * 8].unsqueeze(2).to_broadcast([P, 8, HD]),
                                      ALU.mult).then_inc(sem["xdt_ready"], p.counted("xdt_ready"))

            def weights(mask):
                dve.wait_ge(sem["scores_done"], p.after("scores_done"))
                dve.tensor_tensor(sm[:, :, :], PM[:, 0, 0:2 * P].rearrange("p (g t) -> p g t", t=P),
                                  mask[:, :].unsqueeze(1).to_broadcast([P, 2, P]), ALU.mult).then_inc(sem["sm_ready"], p.counted("sm_ready"))
                dve.wait_ge(sem["sm_ready"], p.so_far("sm_ready"))
                for g in range(2):
                    v = Wb[:, g * 8:(g + 1) * 8, :]
                    dve.wait_ge(sem["D_exp"], p.after("D_exp"))
                    dve.tensor_tensor(v, v, sm[:, g:g + 1, :].to_broadcast([P, 8, P]), ALU.mult).then_inc(sem["W_ready"], p.counted("W_ready"))

            def next_state(s, first):
                if not first:
                    dve.tensor_tensor(wide(st[1 - s]), wide(st[s]), scal[s][:, 3, :].unsqueeze(2).to_broadcast([P, HEADS, HD]),
                                      ALU.mult).then_inc(sem["state_mul"], p.counted("state_mul"))
                for g in range(2):
                    v = st[1 - s][:, g * 512:(g + 1) * 512]
                    dve.wait_ge(sem["S_done"], p.after("S_done"))
                    if first:
                        dve.tensor_copy(v, PG[:, 2 * s + g, :]).then_inc(sem["state_ready"], p.counted("state_ready"))
                    else:
                        dve.wait_ge(sem["state_mul"], p.so_far("state_mul"))
                        dve.tensor_tensor(v, v, PG[:, 2 * s + g, :], ALU.add).then_inc(sem["state_ready"], p.counted("state_ready"))

            def add_y(c):
                for g, read in enumerate(("y_added", "step_done")):
                    v = yT[:, 4 * g:4 * g + 4, c * P:(c + 1) * P] if isinstance(c, int) else yT[:, 4 * g:4 * g + 4, bass.ds(c * P, P)]
                    dve.wait_ge(sem["y_done"], p.after("y_done"))
                    dve.tensor_tensor(v, v, PM[:, 2 + g, :].rearrange("p (t q) -> p t q", q=P), ALU.add).then_inc(sem[read], p.counted(read))

            for d in range(2):
                mask = maskF if d == 0 else maskB
                chunk = lambda n: n if d == 0 else n * -1 + (NCH - 1)
                for s in range(NCX):
                    c = NCH + (s if d == 0 else NCX - 1 - s)
                    dve.wait_ge(sem[f"step_full{s}"], p.after(f"step_full{s}"))
                    scalars(s, c, d)
                    next_state(s, s == 0)
                    dve.wait_ge(sem["state_ready"], p.so_far("state_ready"))
                    dve.tensor_copy(scal[s][:, 0:1, 0:1], scal[s][:, 0:1, 0:1]).then_inc(sem["step_done"], p.counted("step_done"))
                prepare(0, chunk(0), d)
                with p.loop(NCH // 2 - 1, {"step_full0": 3, "step_full1": 3, "scal_ready": 2, "xdt_ready": 4, "D_exp": 4,
                                           "scores_done": 2, "sm_ready": 2, "W_ready": 4, "state_mul": 2, "S_done": 4,
                                           "state_ready": 4, "y_done": 4, "y_added": 2, "step_done": 2}) as i:
                    for s in range(2):
                        weights(mask)
                        next_state(s, False)
                        prepare(1 - s, chunk(i * 2 + (s + 1)), d)
                        add_y(chunk(i * 2 + s))
                for s in range(2):
                    weights(mask)
                    next_state(s, False)
                    if s == 0:
                        prepare(1, chunk(NCH - 1), d)
                    add_y(chunk(NCH - 2 + s))
            dve.wait_ge(sem["step_done"], p.so_far("step_done"))
            dve.wait_ge(sem["skip_ready"], p.so_far("skip_ready"))
            for k in range(KT):
                b = 0
                dve.wait_ge(sem[f"ld_full{b}"], p.after(f"ld_full{b}"))
                dve.scalar_tensor_tensor(out=yT[:, k, :], in0=ld[b][:, :], scalar=dsk[:, k:k + 1], in1=yT[:, k, :],
                                                op0=ALU.mult, op1=ALU.add).then_inc(sem["fin_dve"], p.counted("fin_dve"))
                dve.wait_ge(sem["fin_dve"], p.so_far("fin_dve"))
                dve.wait_ge(sem[f"ld_full{b + 1}"], p.after(f"ld_full{b + 1}"))
                dve.tensor_tensor(yT[:, k, :], yT[:, k, :], ld[b + 1][:, :], ALU.mult).then_inc(sem["fin_dve"], p.counted("fin_dve"))
            norm_dve(p, dve, y_parts())

            def add_to_h(k, s, l, t0, b):
                o = s * HALF
                return dve.scalar_tensor_tensor(out=hT[:, k, o:o + HALF], in0=PG[:, b, :], scalar=mod[:, l, t0 + k, 0:1],
                                                in1=hT[:, k, o:o + HALF], op0=ALU.mult, op1=ALU.add)

            def out_proj(l, t0):
                for u in range(4):
                    for s in range(2):
                        for t in range(2):
                            group(lambda b: add_to_h(2 * u + t, s, l, t0, b))

            dve.wait_ge(sem["v_loaded"], 16)
            for c in range(NCH):
                for q in range(2):
                    if c or q:
                        dve.wait_ge(sem["v_dve"], p.so_far("v_dve"))
                    dve.bn_stats(bst[:, q, :], vln[:, c, q * 512:(q + 1) * 512]).then_inc(sem["v_dve"], p.counted("v_dve"))
                dve.wait_ge(sem["v_dve"], p.so_far("v_dve"))
                dve.bn_aggr(mv[:, c, :], bst[:, :, :]).then_inc(sem["v_dve"], p.counted("v_dve"))
            at(p, "out")
            out_proj(0, 16)
            dve.wait_ge(sem["v_act"], 2)
            dve.wait_ge(sem["sg_loaded"], 80)
            for c in range(NCH):
                dve.tensor_scalar(vln[:, c, :], vln[:, c, :], mv[:, c, 0:1], rstd[:, c, 0:1], ALU.subtract, ALU.mult).then_inc(sem["v_dve"], p.counted("v_dve"))
                dve.wait_ge(sem["v_dve"], p.so_far("v_dve"))
                dve.tensor_tensor(vln[:, c, :], vln[:, c, :], lnrow[:, :], ALU.mult).then_inc(sem["v_dve"], p.counted("v_dve"))
            at(p, "sg")
            for q in range(2):
                group(lambda b: dve.tensor_copy(sgwT[:, 4 * q:4 * q + 4, :].rearrange("p g k -> p (g k)"), PG[:, b, :]))
            dve.wait_ge(sem["sg_loaded"], 96)
            dve.wait_ge(sem["v_dve"], p.so_far("v_dve"))
            for c in range(NCH):
                dve.tensor_tensor(vln[:, c, :], vln[:, c, :], lnrow[:, :], ALU.add).then_inc(sem["v_ready"], p.counted("v_ready"))
            for g in range(KT):
                for s in range(2):
                    dve.wait_ge(sem[f"gu_full{s}"], p.after(f"gu_full{s}"))
                    group(lambda b: dve.tensor_tensor(tm[s][:, :], PG[:, b, :], gu[s][:, :], ALU.mult))
                    dve.wait_ge(sem["sg_hi"], p.after("sg_hi"))
                    dve.tensor_tensor(yl2[:, g, s * HALF:(s + 1) * HALF], tm[s][:, :],
                                             yh2[:, g, s * HALF:(s + 1) * HALF].bitcast(F32), ALU.subtract).then_inc(sem["sg_lo"], p.counted("sg_lo"))
            out_proj(0, 16)
            dve.wait_ge(sem["read_by_dve"], p.so_far("read_by_dve"))

            def mlp(l):
                norm_dve(p, dve, h_parts(2 if l == 0 else 4, l, 24, range(2), vh, vl))
                dve.wait_ge(sem["u_lo"], p.so_far("u_lo"))
                at(p, f"mlp{l}")
                with p.loop(8, {"group_done": 24, "read_by_act": 8, "read_by_dve": 16, "relu_sq": 8, "hid_hi": 8, "hid_lo": 8,
                                **({"ada_full0": 3, "ada_full1": 3, "ada_step": 18, "ada_added": 6} if l == 0 else {})}) as i:
                    for m in range(8):
                        if l == 0 and m >= 2:
                            later_ada(m - 2)
                        t, o = (m // 4) * 2 + m % 2, (m // 2 % 2) * HALF
                        dve.wait_ge(sem["read_by_act"], p.after("read_by_act"))
                        if m:
                            dve.wait_ge(sem["hid_lo"], p.so_far("hid_lo"))
                        dve.tensor_tensor(uf[0][:, :], sq[m % 2][:, :], sq[m % 2][:, :], ALU.mult).then_inc(sem["relu_sq"], p.counted("relu_sq"))
                        dve.wait_ge(sem["relu_sq"], p.so_far("relu_sq"))
                        hi, lo = hh[:, t, o:o + HALF], hl[:, t, o:o + HALF]
                        dve.tensor_copy(hi, uf[0][:, :]).then_inc(sem["hid_hi"], p.counted("hid_hi"))
                        dve.wait_ge(sem["hid_hi"], p.so_far("hid_hi"))
                        dve.tensor_tensor(lo, uf[0][:, :], hi.bitcast(F32), ALU.subtract).then_inc(sem["hid_lo"], p.counted("hid_lo"))
                    p.skip("group_done", 8)
                    for j in range(2):
                        for s in range(2):
                            for t in range(4):
                                group(lambda b: add_to_h(4 * j + t, s, l, 40, b))
                dve.wait_ge(sem["read_by_dve"], p.so_far("read_by_dve"))

            mlp(0)
            for s in range(2):
                dve.wait_ge(sem[f"ada_empty{s}"], ADA_FREED[1])
            add_ada(1, 0, 48)
            gain(3, 1, 8, 0, col("mix_g", KT, KT))
            gain(4, 1, 32, 0, col("mlp_g", KT, KT))
            dve.tensor_tensor(gb[:, :], mod[:, 1, 16:24, 0], col("b_pw2", 0, KT), ALU.mult).then_inc(sem["mod_ready"], p.counted("mod_ready"))
            dve.memset(apad[0][:, :], 0.0).then_inc(sem["mod_ready"], p.counted("mod_ready"))
            dve.memset(apad[1][:, :], 0.0).then_inc(sem["mod_ready"], p.counted("mod_ready"))
            norm_dve(p, dve, h_parts(3, 1, 0, range(2), vh, vl))
            at(p, "pw1")
            for k in range(KT):
                for s in range(2):
                    dve.wait_ge(sem["read_by_act"], p.after("read_by_act", 2))
                    o = CW // 2 + s * HALF
                    dve.tensor_tensor(apad[k % 2][:, o:o + HALF], tm[0][:, :], tm[1][:, :], ALU.mult).then_inc(sem["glu_done"], p.counted("glu_done"))
                dve.wait_ge(sem["glu_done"], p.so_far("glu_done"))
                dve.tensor_scalar(cT[:, k, :], apad[k % 2][:, 0:TOK], col("w_dw", k), col("b_dw", k), ALU.mult, ALU.add).then_inc(sem["dw_step"], p.counted("dw_step"))
                for tap in range(1, CW - POOL_TAPS):
                    dve.wait_ge(sem["dw_step"], p.so_far("dw_step"))
                    dve.scalar_tensor_tensor(out=cT[:, k, :], in0=apad[k % 2][:, tap:tap + TOK],
                                                    scalar=col("w_dw", tap * KT + k), in1=cT[:, k, :], op0=ALU.mult,
                                                    op1=ALU.add).then_inc(sem["dw_step"], p.counted("dw_step"))
                dve.wait_ge(sem["dw_step"], p.so_far("dw_step"))
                dve.wait_ge(sem["prod_added"], (POOL_TAPS - 1) * (k + 1))
                dve.tensor_tensor(cT[:, k, :], cT[:, k, :], pacc[:, :], ALU.add).then_inc(sem["dw_done"], p.counted("dw_done"))
            dve.wait_ge(sem["mean_done"], p.after("mean_done"))
            for s in range(2):
                o = s * HALF
                src = lambda k: cT[:, k, o:o + HALF]
                for k in range(KT):
                    dve.scalar_tensor_tensor(out=src(k), in0=PM[:, 1 + s, :], scalar=-1.0 / D, in1=src(k), op0=ALU.mult,
                                                    op1=ALU.add).then_inc(sem["ln_dve"], p.counted("ln_dve"))
                norm_dve(p, dve, c_parts(s))
            for k in range(KT):
                dve.tensor_scalar(hT[:, k, :], hT[:, k, :], gb[:, k:k + 1], None, ALU.add).then_inc(sem["bias_added"], p.counted("bias_added"))
            dve.wait_ge(sem["bias_added"], p.so_far("bias_added"))
            at(p, "pw2")
            out_proj(1, 16)
            dve.wait_ge(sem["read_by_dve"], p.so_far("read_by_dve"))
            mlp(1)
            dve.wait_ge(sem["fg_loaded"], 16)
            for c in range(NCH):
                dve.wait_ge(sem["out_act"], 3 * (c + 1))
                dve.scalar_tensor_tensor(out=fo[c % 2][:, :], in0=fo[c % 2][:, :], scalar=fm[:, c, 0:1], in1=fg[:, :],
                                                op0=ALU.mult, op1=ALU.mult).then_inc(sem["out_dve"], p.counted("out_dve"))


_INS = ["x", "c", "ctx", "c_ctx", "ada_w", "ada_b", "norm_mix_g", "norm_mlp_g", "mlp_w1", "mlp_w2",
        "hy_w_in", "ssd_conv_w", "ssd_conv_b", "ssd_dt_bias", "ssd_a_log", "ssd_d", "ssd_norm_g",
        "sg_ln_g", "sg_ln_b", "sg_w", "sg_b", "hy_w_out", "cf_w_pw1", "cf_b_pw1", "cf_w_dw", "cf_b_dw",
        "cf_ln_g", "cf_ln_b", "cf_w_pw2", "cf_b_pw2", "final_norm_g"]


def kernel(**inputs):
    import numpy as _np
    import concourse.bacc as _bacc
    from concourse import mybir as _mybir
    from concourse.bass_utils import run_bass_kernel_spmd as _run

    nc = _bacc.Bacc("TRN2", target_bir_lowering=False, num_devices=1)
    arrays, aps = {}, {}
    for name in _INS:
        v = _np.ascontiguousarray(inputs[name])
        arrays[f"in_{name}"] = v
        aps[name] = nc.dram_tensor(f"in_{name}", v.shape, _mybir.dt.from_np(v.dtype), kind="ExternalInput").ap()
    out = nc.dram_tensor("out_0", (1, TOK, D), _mybir.dt.float32, kind="ExternalOutput").ap()
    build(nc, aps, out)
    r = _run(nc, [arrays], core_ids=[0])
    return r.results[0]["out_0"]
```

```python
from contextlib import ExitStack, contextmanager

import concourse.bass as bass
from concourse import mybir

P = 128
F32 = mybir.dt.float32
F32R = mybir.dt.float32r
ALU = mybir.AluOpType
ACT = mybir.ActivationFunctionType

D = 1024
TOK = 1024
CTX = 256
ALL = TOK + CTX
KT = D // P
HALF = 512
SEGS = [(0, HALF), (HALF, HALF), (TOK, CTX)]
NCH = TOK // P
NCX = CTX // P
NALL = NCH + NCX
XBC = 1536
XBT = XBC // P
HEADS = 16
HD = 64
HID = 4096
EPS = 1e-6
UNIT = 2048
CONV = 5
CW = 31
PADW = 1288
CONF_PAD = 1056
POOL_TAPS = 10


class Lin:

    def __init__(self, c, step=0, i=None):
        self.c, self.step, self.i = c, step, i

    def plus(self, k):
        return Lin(self.c + k, self.step, self.i)

    def value(self, mul=1, add=0):
        v = self.c * mul + add
        return self.i * (self.step * mul) + v if self.step else v


class Program:

    def __init__(self, eng, names, start):
        self.e, self.step = eng, names
        self.cnt = {n: Lin(start.get(n, 0)) for n in names}

    def begun(self, name, k=0):
        v = self.cnt[name].plus(k)
        return v.step != 0 or v.c > 0

    def so_far(self, name, k=0):
        assert self.begun(name, k), name
        return self.cnt[name].plus(k).value(self.step[name])

    def skip(self, name, k=1):
        self.cnt[name] = self.cnt[name].plus(k)

    def after(self, name, k=1):
        self.skip(name, k)
        return self.so_far(name)

    def counted(self, name):
        self.skip(name)
        return self.step[name]

    @contextmanager
    def loop(self, n, per):
        start = {k: v.c for k, v in self.cnt.items()}
        with self.e.Fori(0, n) as i:
            for k, step in per.items():
                self.cnt[k] = Lin(start[k], step, i)
            yield i
        moved = {k: v.c - start[k] for k, v in self.cnt.items() if v.c != start[k]}
        assert moved == {k: v for k, v in per.items() if v}, f"signals in a turn: {moved}"
        for k in self.cnt:
            self.cnt[k] = Lin(start[k] + n * per.get(k, 0))


def build(nc, a, out):
    dram = lambda n, s: nc.dram_tensor(n, s, F32, kind="Internal").ap()
    xbcT = dram("scr_xbcT", [XBC, ALL])
    xtokD = dram("scr_xtok", [ALL, XBC])
    zT = dram("scr_zT", [D, TOK])
    guT = dram("scr_guT", [D, TOK])
    vtok = dram("scr_vtok", [TOK, D])
    acsD = dram("scr_acs", [2 * HEADS, ALL])

    stack = ExitStack()
    with stack:
        def sb(name, shape, dt=F32, at=stack):
            return at.enter_context(nc.sbuf_tensor(name, shape, dt))

        hT = sb("hT", [P, KT, TOK])
        raw = [sb(f"raw{i}", [P, UNIT]) for i in range(2)]
        wh = [sb(f"wh{i}", [P, UNIT], F32R) for i in range(2)]
        wl = [sb(f"wl{i}", [P, UNIT], F32R) for i in range(2)]
        ident = sb("ident", [P, P])
        ones = sb("ones", [P, P])
        maskF = sb("maskF", [P, P])
        maskB = sb("maskB", [P, P])
        mod = sb("mod", [P, 2, 48, 2])
        gsc = sb("gsc", [P, 6, KT])
        csil = sb("csil", [P, 16])
        zero = sb("zero", [P, 1])
        G = ExitStack()
        adaw = [sb(f"adaw{i}", [P, D], at=G) for i in range(2)]
        pacc = adaw[0]
        prod = [sb(f"prod{i}", [P, TOK], at=G) for i in range(2)]
        G.close()
        sacc = sb("sacc", [P, HALF])
        rs = [sb("rs0", [P, HALF])]
        tm = [sb(f"tm{i}", [P, HALF]) for i in range(2)]
        sq = [sb(f"sq{i}", [P, HALF]) for i in range(2)]
        uf = [sb(f"uf{i}", [P, HALF]) for i in range(2)]
        PG = stack.enter_context(nc.psum_tensor("PG", [P, 4, 512], F32))
        PM = stack.enter_context(nc.psum_tensor("PM", [P, 4, 512], F32))

        rows = {}
        place = []
        n_rows = 0

        def add_rows(name, ap, r):
            nonlocal n_rows
            rows[name] = n_rows
            s = 0
            while s < r:
                k = min(r - s, P - n_rows % P)
                place.append((n_rows // P, n_rows % P, k, ap, s))
                n_rows += k
                s += k

        vec = lambda ap: ap.rearrange("(r p) -> r p", p=P)
        add_rows("c", vec(a["c"].rearrange("a d -> (a d)")), KT)
        add_rows("c_ctx", vec(a["c_ctx"]), KT)
        add_rows("ada_b", vec(a["ada_b"].rearrange("a d -> (a d)")), 96)
        add_rows("mix_g", vec(a["norm_mix_g"].rearrange("a d -> (a d)")), 2 * KT)
        add_rows("mlp_g", vec(a["norm_mlp_g"].rearrange("a d -> (a d)")), 2 * KT)
        add_rows("ssd_g", vec(a["ssd_norm_g"].rearrange("a d -> (a d)")), KT)
        add_rows("ln_g", vec(a["cf_ln_g"].rearrange("a d -> (a d)")), KT)
        add_rows("ln_b", vec(a["cf_ln_b"].rearrange("a d -> (a d)")), KT)
        add_rows("b_dw", vec(a["cf_b_dw"].rearrange("a d -> (a d)")), KT)
        add_rows("b_pw1", vec(a["cf_b_pw1"].rearrange("a d -> (a d)")), 2 * KT)
        add_rows("b_pw2", vec(a["cf_b_pw2"].rearrange("a d -> (a d)")), KT)
        add_rows("conv_b", vec(a["ssd_conv_b"].rearrange("a d -> (a d)")), XBT)
        add_rows("conv_w", vec(a["ssd_conv_w"].rearrange("a t d -> (a t d)")), CONV * XBT)
        add_rows("w_dw", vec(a["cf_w_dw"].rearrange("a t d -> (a t d)")), CW * KT)
        NB = (n_rows + P - 1) // P
        par = sb("par", [P, NB, P])

        def col(name, k=0, n=1):
            return par[:, :, :].rearrange("p b q -> p (b q)")[:, rows[name] + k:rows[name] + k + n]

        def cold(name, k):
            return par[:, :, :].rearrange("p b q -> p (b q)")[:, bass.ds(k + rows[name], 1)]

        R32 = 2 * HEADS
        alog = sb("alog", [R32, 1])
        dtb = sb("dtb", [R32, 1])
        a_bc = sb("a_bc", [P, R32])
        d_bc = sb("d_bc", [P, HEADS])
        dsk = sb("dsk", [P, KT])

        A = ExitStack()
        uh = sb("uh", [P, KT, ALL], F32R, A)
        ul = sb("ul", [P, KT, ALL], F32R, A)
        A1 = ExitStack()
        hcT = sb("hcT", [P, KT, CTX], at=A1)
        xin = [sb(f"xin{i}", [P, D], at=A1) for i in range(2)]
        prow = sb("prow", [P, NB, P], at=A1)
        A1.close()
        zo = sq + uf
        A2 = ExitStack()
        xp = [sb(f"xp{i}", [P, PADW], at=A2) for i in range(2)]
        cv = sb("cv", [P, PADW], at=A2)
        xs = sb("xs", [P, ALL], at=A2)
        xtk = sb("xtk", [P, NALL, P], at=A2)
        A2.close()
        A3 = ExitStack()
        rwx, rwe, rwq, rwp, rwdt = [sb(f"row_{n}", [R32, ALL], at=A3) for n in ("x", "e", "q", "p", "dt")]
        A3.close()
        A.close()

        B = ExitStack()
        yT = sb("yT", [P, KT, TOK], at=B)
        B1 = ExitStack()
        bcT = [sb(f"bcT{i}", [P, 4, P], at=B1) for i in range(2)]
        xtb = [sb(f"xtb{i}", [P, D + 2 * P], at=B1) for i in range(2)]
        Abc = [sb(f"Abc{i}", [P, HEADS, P], at=B1) for i in range(2)]
        Eb = [sb(f"Eb{i}", [P, HEADS, P], at=B1) for i in range(2)]
        scal = [sb(f"scal{i}", [P, 4, HEADS], at=B1) for i in range(2)]
        sm = sb("sm", [P, 2, P], at=B1)
        sb("to_the_rows", [P, P], at=B1)
        tab = sb("tab", [P, NALL, 2, 4, HEADS], at=B1)
        B2 = ExitStack()
        dAt = sb("dAt", [P, NALL, R32], at=B2)
        te = sb("te", [P, NALL, R32], at=B2)
        B2.close()
        Wb = sb("Wb", [P, HEADS, P], at=B1)
        xd = [tm, [sacc, rs[0]]]
        xte = sb("xte", [P, D], at=B1)
        st = [sb(f"st{i}", [P, D], at=B1) for i in range(2)]
        B1.close()
        yh = sb("yh", [P, KT, TOK], F32R, B)
        yl = sb("yl", [P, KT, TOK], F32R, B)
        B.close()

        C = ExitStack()
        vln = sb("vln", [P, NCH, D], at=C)
        yh2 = sb("yh2", [P, KT, TOK], F32R, C)
        yl2 = sb("yl2", [P, KT, TOK], F32R, C)
        gu = sq
        lnrow = sb("lnrow", [P, D], at=C)
        sgwT = sb("sgwT", [P, KT, P], at=C)
        bst = sb("bst", [P, 2, 6], at=C)
        mv = sb("mv", [P, NCH, 2], at=C)
        rstd = sb("rstd", [P, NCH, 1], at=C)
        sgb = lambda g: (sacc, rs[0])[g // 4][0:1, (g % 4) * P:(g % 4 + 1) * P]
        C.close()

        Dx = ExitStack()
        vh = sb("vh", [P, KT, TOK], F32R, Dx)
        vl = sb("vl", [P, KT, TOK], F32R, Dx)
        D1 = ExitStack()
        hh = sb("hh", [P, 4, TOK], F32R, D1)
        hl = sb("hl", [P, 4, TOK], F32R, D1)
        D1.close()
        D2 = ExitStack()
        cT = sb("cT", [P, KT, TOK], at=D2)
        apad = [sb(f"apad{i}", [P, CONF_PAD], at=D2) for i in range(2)]
        gb = sb("gb", [P, KT], at=D2)
        D2.close()
        D3 = ExitStack()
        fg = sb("fg", [P, D], at=D3)
        fo = [sb(f"fo{i}", [P, D], at=D3) for i in range(4)]
        fs = sb("fs", [P, D], at=D3)
        fm = sb("fm", [P, NCH, 1], at=D3)
        D3.close()
        Dx.close()

        names = {}
        for n in ("ada_step", "ada_added", "const_ready", "group_done", "read_by_act", "read_by_dve", "split_begun", "split_hi",
                  "par_turned", "par_ready", "skip_ready", "silu_c", "mod_ready",
                  "sq_ready", "sq_added", "stat_done", "ln_done", "rstd_ready", "norm_mul", "uf_ready", "u_hi", "u_lo",
                  "pads_ready", "conv_step", "conv_done", "xs_ready", "xt_turned", "xt_copied",
                  "row_act", "row_dve", "tab_turned", "tot_done", "tab_dve", "tab_act",
                  "scal_ready", "sm_ready", "y_added", "seg_ready", "seg1_ready", "E_ready", "D_exp", "CE_ready", "xdt_ready", "xte_ready", "scores_done",
                  "W_ready", "S_done", "state_mul", "state_ready", "y_done", "step_done",
                  "fin_dve", "v_dve", "v_act", "v_ready", "sg_hi", "sg_lo",
                  "relu_sq", "hid_hi", "hid_lo", "glu_done", "dw_step", "dw_done", "prod_ready", "prod_added", "sq_summed", "mean_done", "ln_dve", "bias_added",
                  "tok_turned", "out_dve", "out_act"):
            names[n] = 1
        for i in range(2):
            names[f"raw_empty{i}"] = 1
            names[f"ada_empty{i}"] = 1
            names[f"split_full{i}"] = 1
            for n in ("raw_full", "ada_full", "xin_full", "step_full", "gu_full"):
                names[f"{n}{i}"] = 16
        for i in range(4):
            names[f"zo_stored{i}"] = 16
        for n in ("z_full0", "z_full1", "par_loaded", "rec_loaded", "xs_stored", "xt_stored", "acs_stored", "acs_loaded", "v_loaded", "sg_loaded",
                  "fg_loaded", "out_stored0", "out_stored1", "out_stored2", "out_stored3"):
            names[n] = 16
        sem = {n: stack.enter_context(nc.semaphore(n)) for n in names}
        credit = {"read_by_act": 4, "read_by_dve": 4, "raw_empty0": 1, "raw_empty1": 1,
                  "ada_empty0": 1, "ada_empty1": 1, "step_done": 2, "y_done": 4, "fin_dve": 2,
                  "y_added": 1, "sm_ready": 1,
                  "relu_sq": 2, "zo_stored0": 1, "zo_stored1": 1, "zo_stored2": 1, "zo_stored3": 1}
        mirrored = {n: k for n, k in credit.items() if "_empty" not in n}
        marks = {}
        SHARED = ("group_done", "read_by_act", "read_by_dve")

        block = stack.enter_context(nc.Block())

        w_ada = [a["ada_w"][l].rearrange("(k p) n -> p k n", p=P) for l in range(2)]
        w_in = a["hy_w_in"][0].rearrange("(k p) n -> p k n", p=P)
        w_out = a["hy_w_out"][0].rearrange("(k p) n -> p k n", p=P)
        w_m1 = [a["mlp_w1"][l].rearrange("(k p) n -> p k n", p=P) for l in range(2)]
        w_m2 = [a["mlp_w2"][l].rearrange("(k p) n -> p k n", p=P) for l in range(2)]
        w_p1 = a["cf_w_pw1"][0].rearrange("(k p) n -> p k n", p=P)
        w_p2 = a["cf_w_pw2"][0].rearrange("(k p) n -> p k n", p=P)
        Z0, X0, T0, U0 = 0, D, D + XBC, D + XBC + 2 * HEADS
        V0 = U0 + D

        N_ADA0 = 2 * D // 256
        N_XBC = XBC // 256

        class Stream:

            def __init__(self):
                self.raw = self.split = 0

            @contextmanager
            def loop(self, p, n, gemms, per):
                raw0, split0 = self.raw, self.split
                with p.loop(n, per) as i:
                    yield i
                assert self.raw - raw0 == gemms and self.split - split0 == gemms
                self.raw, self.split = raw0 + n * gemms, split0 + n * gemms

        def walk(p, S, per, gemm, ada, later_ada, after_v, stage=lambda name: None, conv_tile=lambda: None):
            for u in range(N_ADA0):
                ada(w_ada[0], u * 256, 256)
            stage("xbc")
            for u in range(N_XBC):
                gemm(w_in, 0, 8, X0 + u * 256, 256, 6)
            gemm(w_in, 0, 8, T0, P, 3)
            for u in range(8):
                gemm(w_in, 0, 8, (Z0, U0)[u // 4] + u % 4 * 256, 256, 4)
                if u:
                    for q in range(4):
                        later_ada(w_ada[0], 2048 + (4 * (u - 1) + q) * P, q, 3 * KT)
            gemm(w_in, 0, 8, V0, 256, 4)
            for q in range(4):
                later_ada(w_ada[0], 2048 + (28 + q) * P, q, 3 * KT)
            for u in range(1, 4):
                gemm(w_in, 0, 8, V0 + u * 256, 256, 4)
            after_v()
            for k0 in (0, 8):
                stage("out" if k0 == 0 else "out2")
                with S.loop(p, 2, 2, per(2, 0)) as i:
                    for j in range(2):
                        gemm(w_out, k0, 8, i * 512 + j * 256, 256, 4)
            for l in range(2):
                adas = 6 if l == 0 else 0
                with S.loop(p, 8, 4, per(4, adas)) as i:
                    for j in range(2):
                        gemm(w_m1[l], 0, 8, i * 512 + j * 256, 256, 4)
                    for j in range(2):
                        for q in ((0, 1, 2, 3), (4, 5))[j][:adas]:
                            later_ada(w_ada[1], i * 768 + q * P, q, 7 * KT)
                        gemm(w_m2[l], i * 4, 4, j * 512, 512, 8)
                if l == 0:
                    for u in range(2):
                        gemm(w_p1, 0, 8, (u * P,), 256, 4)
                    with S.loop(p, 3, 2, per(2, 0, 2, convs=2)) as i:
                        for j in range(2):
                            gemm(w_p1, 0, 8, (i * 256 + (j + 2) * P,), 256, 4)
                            conv_tile()
                    for u in range(4):
                        gemm(w_p2, 0, 8, u * 256, 256, 4)
                        if u < 2:
                            conv_tile()

        GROUPS_SCAN = 2 * NALL + 3 * (XBT + 1) + 3 * 16
        tok = lambda c: (PG, PM)[c % 4 // 2][:, 2 * (c % 2):2 * (c % 2) + 2, :].rearrange("p b n -> p (b n)")
        ADA_FREED = [1 + 16, 1 + 16 + 24]

        @block.sync
        def _(sp):
            p = Program(sp, names, {"fin_dve": 1})
            S = Stream()

            def load(w, k0, kn, c0, cn):
                s = S.raw % 2
                S.raw += 1
                sp.wait_ge(sem[f"raw_empty{s}"], p.after(f"raw_empty{s}"))
                if isinstance(c0, tuple):
                    dst = raw[s][:, :].rearrange("p (k b c) -> p b k c", b=2, c=P)
                    for b in range(2):
                        sp.dma_start(dst[:, b], w[:, :, bass.ds(c0[0] + b * D, P)]).then_inc(sem[f"raw_full{s}"], 16)
                else:
                    dst = raw[s][:, 0:kn * cn].rearrange("p (k c) -> p k c", c=cn)
                    ks = slice(k0, k0 + kn) if isinstance(k0, int) else bass.ds(k0, kn)
                    cs = slice(c0, c0 + cn) if isinstance(c0, int) else bass.ds(c0, cn)
                    sp.dma_start(dst, w[:, ks, cs]).then_inc(sem[f"raw_full{s}"], 16)

            def gemm(w, k0, kn, c0, cn, groups):
                load(w, k0, kn, c0, cn)
                S.split += 1

            def later_ada(w, c0, q, n_norm):
                sp.wait_ge(sem["u_lo"], n_norm)
                sp.wait_ge(sem[f"ada_empty{q % 2}"], p.after(f"ada_empty{q % 2}"))
                sp.dma_start(adaw[q % 2][:, :].rearrange("p (k c) -> p k c", c=P),
                             w[:, :, slice(c0, c0 + P) if isinstance(c0, int) else bass.ds(c0, P)]).then_inc(sem[f"ada_full{q % 2}"], 16)

            def per(gemms, adas, loads=1, convs=0):
                return {**{f"raw_empty{s}": gemms // 2 for s in range(2)}, **{f"ada_empty{s}": adas // 2 for s in range(2)}}

            def step(s, c, d, lat, early=False):
                if early:
                    sp.wait_ge(sem["state_ready"], p.after("state_ready", 2))
                else:
                    sp.wait_ge(sem["step_done"], p.after("step_done"))
                toks = slice(c * P, c * P + P) if isinstance(c, int) else bass.ds(c * P, P)
                full = sem[f"step_full{s}"]
                sp.dma_start(xtb[s][:, :], xtokD[toks, 0:D + 2 * P]).then_inc(full, 16)
                if lat:
                    sp.dma_start(bcT[s][:, :, :], xbcT[D:XBC, toks].rearrange("(b p) t -> p b t", p=P)).then_inc(full, 16)
                    sp.dma_start(Abc[s][:, :, :], acsD[d * HEADS:(d + 1) * HEADS, toks].partition_broadcast(P)).then_inc(full, 16)
                if early and d == 0:
                    sp.wait_ge(sem["step_done"], p.after("step_done"))
                elif early:
                    p.skip("step_done")
                if lat and d == 0:
                    sp.dma_start(prod[s][:, :].rearrange("p (k t) -> p k t", t=P),
                                 xbcT[0:D, toks].rearrange("(k p) t -> p k t", p=P)).then_inc(full, 16)

            def load_z(s, c):
                toks = slice(c * P, c * P + P) if isinstance(c, int) else bass.ds(c * P, P)
                sp.wait_ge(sem["fin_dve"], p.so_far("fin_dve"))
                p.skip("fin_dve")
                sp.dma_start(prod[s][:, :].rearrange("p (k t) -> p k t", t=P),
                             zT[0:D, toks].rearrange("(k p) t -> p k t", p=P)).then_inc(sem[f"z_full{s}"], 16)

            def scan_loads():
                sp.wait_ge(sem["xs_stored"], 16 * XBT)
                sp.wait_ge(sem["xt_stored"], 16 * XBT)
                sp.wait_ge(sem["acs_loaded"], 16)
                sp.wait_ge(sem["tab_dve"], 6)
                sp.wait_ge(sem["group_done"], GROUPS_SCAN)
                for b in range(4):
                    sp.wait_ge(sem[f"zo_stored{b}"], 16 * (1 + 12))
                for d in range(2):
                    for j in range(NCX):
                        step(j, NCH + (j if d == 0 else NCX - 1 - j), d, False)
                    p.skip("state_ready", 2 * NCX)
                    for j in range(2):
                        step(j, j if d == 0 else NCH - 1 - j, d, True)
                    with p.loop(NCH // 2 - 1, {"step_done": 2, "fin_dve": 2 * d, "state_ready": 4}) as i:
                        for j in range(2):
                            if d == 0:
                                step(j, i * 2 + (2 + j), d, True, early=True)
                            else:
                                load_z(j, i * -2 + (NCH - 1 - j))
                                step(j, i * -2 + (NCH - 3 - j), d, True, early=True)
                    p.skip("state_ready", 4)
                    if d == 0:
                        continue
                    for j in range(2):
                        load_z(j, 1 - j)

            walk(p, S, per, gemm, lambda w, c0, cn: load(w, 0, 8, c0, cn), later_ada, scan_loads)
            for c in range(NCH):
                sp.wait_ge(sem["out_dve"], c + 1)
                sp.dma_start(out[0, c * P:(c + 1) * P, :], fo[c % 4][:, :]).then_inc(sem[f"out_stored{c % 4}"], 16)
            for q in range(4):
                sp.wait_ge(sem[f"out_stored{q}"], 16 * (NCH // 4))

        @block.gpsimd
        def _(pool):
            p = Program(pool, names, {})
            S = Stream()
            for n, k in credit.items():
                pool.sem_inc(sem[n], k * names[n])
            pool.memset(ident[:, :], 0.0).then_inc(sem["const_ready"], p.counted("const_ready"))
            pool.memset(zero[:, :], 0.0).then_inc(sem["const_ready"], p.counted("const_ready"))
            pool.memset(ones[:, :], 1.0).then_inc(sem["const_ready"], p.counted("const_ready"))
            pool.memset(maskF[:, :], 1.0).then_inc(sem["const_ready"], p.counted("const_ready"))
            pool.memset(maskB[:, :], 1.0).then_inc(sem["const_ready"], p.counted("const_ready"))
            pool.wait_ge(sem["const_ready"], p.so_far("const_ready"))
            pool.affine_select(out=ident[:, :], in_=ident[:, :], compare_op=ALU.not_equal, fill=1.0, base=0,
                                      pattern=[[-1, P]], channel_multiplier=1).then_inc(
                                          sem["const_ready"], p.counted("const_ready"))
            pool.affine_select(out=maskF[:, :], in_=maskF[:, :], compare_op=ALU.is_ge, fill=0.0, base=0,
                                      pattern=[[1, P]], channel_multiplier=-1).then_inc(
                                          sem["const_ready"], p.counted("const_ready"))
            pool.affine_select(out=maskB[:, :], in_=maskB[:, :], compare_op=ALU.is_ge, fill=0.0, base=0,
                                      pattern=[[-1, P]], channel_multiplier=1).then_inc(
                                          sem["const_ready"], p.counted("const_ready"))
            pool.wait_ge(sem["const_ready"], p.so_far("const_ready"))

            ends = [None, None]

            def loop_ended():
                if in_loop[0] is not None:
                    c = p.cnt["group_done"].c
                    ends[:] = [c - in_loop[0], c]
                    in_loop[0] = None

            def enter():
                loop_ended()
                pool.wait_ge(sem["group_done"], ends[0])

            def gemm(w, k0, kn, c0, cn, groups):
                s, t = S.raw % 2, S.split % 2
                S.raw += 1
                S.split += 1
                n = kn * cn
                pool.wait_ge(sem[f"raw_full{s}"], p.after(f"raw_full{s}", 2 if isinstance(c0, tuple) else 1))
                if in_loop[0] is not None:
                    pool.wait_ge(sem["group_done"], p.so_far("group_done", -in_loop[0]))
                    in_loop[0] = groups
                elif ends[0] is not None:
                    pool.wait_ge(sem["group_done"], ends[0])
                p.skip("group_done", groups)
                if in_loop[0] is None:
                    ends[:] = [ends[1], p.cnt["group_done"].c]
                pool.sem_inc(sem["split_begun"], 1)
                pool.tensor_tensor(wh[t][:, 0:n], raw[s][:, 0:n], zero[:, 0:1].to_broadcast([P, n]), ALU.add).then_inc(
                    sem["split_hi"], p.counted("split_hi"))
                pool.wait_ge(sem["split_hi"], p.so_far("split_hi"))
                pool.tensor_tensor(wl[t][:, 0:n], raw[s][:, 0:n], wh[t][:, 0:n].bitcast(F32), ALU.subtract).then_inc(
                    sem[f"split_full{t}"], p.counted(f"split_full{t}"))
                pool.wait_ge(sem[f"split_full{t}"], p.so_far(f"split_full{t}"))
                pool.sem_inc(sem[f"raw_empty{s}"], 1)

            def ada(w, c0, cn):
                p.skip(f"raw_full{S.raw % 2}")
                S.raw += 1

            def per(gemms, adas, loads=1, convs=0):
                d = {f"raw_full{s}": gemms // 2 * loads for s in range(2)}
                for s in range(2):
                    d[f"split_full{s}"] = gemms // 2
                enter()
                in_loop[0] = 8 if gemms == 4 else 4
                return {**d, "split_hi": gemms, "group_done": 24 if gemms == 4 else 8,
                        "prod_ready": convs * POOL_TAPS, "prod_added": convs * (POOL_TAPS - 1)}

            def conv_tile():
                p.skip("prod_ready")
                for t in range(1, POOL_TAPS):
                    pool.wait_ge(sem["prod_ready"], p.after("prod_ready"))
                    if t > 1:
                        pool.wait_ge(sem["prod_added"], p.so_far("prod_added"))
                    pool.tensor_tensor(pacc[:, :], pacc[:, :], prod[t % 2][:, :], ALU.add).then_inc(
                        sem["prod_added"], p.counted("prod_added"))

            def to_end(s):
                pool.wait_ge(sem["scal_ready"], p.after("scal_ready"))
                if p.begun("S_done"):
                    pool.wait_ge(sem["S_done"], p.so_far("S_done"))
                p.skip("S_done", 2)
                pool.tensor_tensor(xte[:, :].rearrange("p (h q) -> p h q", q=HD), xtb[s][:, 0:D].rearrange("p (h q) -> p h q", q=HD),
                                   scal[s][:, 2, :].unsqueeze(2).to_broadcast([P, HEADS, HD]),
                                   ALU.mult).then_inc(sem["xte_ready"], p.counted("xte_ready"))

            def scan_gates():
                for d in range(2):
                    for j in range(NCX):
                        pool.wait_ge(sem[f"step_full{j}"], p.after(f"step_full{j}"))
                        to_end(j)
                    with p.loop(NCH // 2, {"step_full0": 4 - d, "step_full1": 4 - d, "E_ready": 2, "CE_ready": 4, "scal_ready": 2,
                                           "S_done": 4, "xte_ready": 2}) as i:
                        for s in range(2):
                            pool.wait_ge(sem[f"step_full{s}"], p.after(f"step_full{s}", 4 - d))
                            to_end(s)
                            pool.wait_ge(sem["E_ready"], p.after("E_ready"))
                            for g in range(2):
                                v = Eb[s][:, g * 8:(g + 1) * 8, :]
                                cT_ = bcT[s][:, 2 + g, :].unsqueeze(1).to_broadcast([P, 8, P])
                                pool.tensor_tensor(v, v, cT_, ALU.mult).then_inc(sem["CE_ready"], p.counted("CE_ready"))

            def stage(name):
                loop_ended()
                p.cnt["group_done"] = Lin({"xbc": 2 * NALL, "out": p.cnt["group_done"].c,
                                           "out2": p.cnt["group_done"].c + 2 + 2 * KT}[name])

            in_loop = [None]
            walk(p, S, per, gemm, ada, lambda w, c0, q, n_norm: None, scan_gates, stage, conv_tile)

        @block.tensor
        def _(pe):
            p = Program(pe, names, mirrored)
            S = Stream()
            prev = [None]
            bank = [0]

            def next_bank(evac, j):
                if j < 4 and prev[0] is not None and prev[0] != evac:
                    pe.wait_ge(sem[prev[0]], p.so_far(prev[0], j - 3))
                else:
                    pe.wait_ge(sem[evac], p.so_far(evac, -3))
                p.skip(evac)
                b = bank[0]
                bank[0] = (b + 1) % 4
                return b

            def mark(name):
                marks[name] = {n: p.cnt[n].c for n in SHARED}, bank[0]

            def drained(evac):
                if prev[0] is not None:
                    pe.wait_ge(sem[prev[0]], p.so_far(prev[0]))
                prev[0] = evac

            def unit(width, kn, tiles, segs, rhs, evac, j0, ready=None, loads=1, between=lambda n: None):
                t_ = S.split % 2
                S.raw += 1
                S.split += 1
                p.skip(f"raw_full{(S.raw - 1) % 2}", loads)
                pe.wait_ge(sem[f"split_full{t_}"], p.after(f"split_full{t_}"))
                order = [(t, s) for s in segs for t in range(tiles)]
                for n, (t, s) in enumerate(order):
                    b = next_bank(evac, j0 + n)
                    w = SEGS[s][1]
                    for k in range(kn):
                        if ready:
                            ready(n, t, s, k)
                        o = k * width + t * P
                        H, L = wh[t_][:, o:o + P], wl[t_][:, o:o + P]
                        xh, xl = rhs(k, s)
                        pe.matmul(PG[:, b, 0:w], H, xh, start=(k == 0), stop=False)
                        pe.matmul(PG[:, b, 0:w], H, xl, start=False, stop=False)
                        ins = pe.matmul(PG[:, b, 0:w], L, xh, start=False, stop=(k == kn - 1))
                    ins.then_inc(sem["group_done"], p.counted("group_done"))
                    between(n)

            def later_ada(q, out_col):
                s = q % 2
                pe.wait_ge(sem["ada_added"], p.after("ada_added"))
                pe.matmul(PM[:, 3, slice(out_col, out_col + 1) if isinstance(out_col, int) else bass.ds(out_col, 1)], adaw[s][:, 0:P], ones[:, 0:1],
                          start=True, stop=True).then_inc(sem[f"ada_empty{s}"], 1)

            def ada_unit(cols, out_col):
                s = S.raw % 2
                S.raw += 1
                pe.wait_ge(sem[f"raw_full{s}"], p.after(f"raw_full{s}"))
                for t in range(cols // P):
                    for k in range(KT):
                        o = out_col + 2 * t
                        dst = PM[:, 3, o:o + 2] if isinstance(o, int) else PM[:, 3, bass.ds(o, 2)]
                        ins = pe.matmul(dst, raw[s][:, k * cols + t * P:k * cols + (t + 1) * P],
                                        csil[:, k:k + 9:8], start=(k == 0), stop=(k == KT - 1))
                ins.then_inc(sem[f"raw_empty{s}"], 1)

            def per(gemms, adas, **more):
                d = {f"raw_full{s}": gemms // 2 for s in range(2)}
                for s in range(2):
                    d[f"split_full{s}"] = gemms // 2
                return {**d, "ada_added": adas, **more}

            pe.wait_ge(sem["const_ready"], 8)
            pe.wait_ge(sem["par_loaded"], 16 * (len(place)))
            for b in range(NB):
                n = min(P, n_rows - b * P)
                ins = pe.transpose(PM[:, b // 4, (b % 4) * P:(b % 4) * P + n], prow[0:n, b, :], ident[0:n, 0:n])
            ins.then_inc(sem["par_turned"], p.counted("par_turned"))
            prev[0] = "read_by_act"
            for c in range(NALL):
                pe.wait_ge(sem[f"xin_full{c % 2}"], p.after(f"xin_full{c % 2}"))
                for hf in range(2):
                    b = next_bank("read_by_act", 4)
                    for q in range(4):
                        ins = pe.transpose(PG[:, b, q * P:(q + 1) * P], xin[c % 2][:, (4 * hf + q) * P:(4 * hf + q + 1) * P],
                                           ident[:, :])
                    ins.then_inc(sem["group_done"], p.counted("group_done"))
                if c == 1:
                    pe.wait_ge(sem["silu_c"], 1)
                if c >= NALL - N_ADA0:
                    ada_unit(256, 4 * (c - (NALL - N_ADA0)))
            def stats(n, width=HALF):
                pe.wait_ge(sem["sq_added"], p.after("sq_added", n))
                p.skip("sq_ready", n + 1)
                if p.cnt["stat_done"].c >= 1:
                    pe.wait_ge(sem["ln_done"], p.cnt["stat_done"].c)
                pe.matmul(PM[:, 0, 0:width], ones[:, :], sacc[:, 0:width], start=True, stop=True).then_inc(
                    sem["stat_done"], p.counted("stat_done"))

            def sums(k0, k1, n=KT):
                if k0 == 0 and p.cnt["stat_done"].c >= 1:
                    pe.wait_ge(sem["ln_done"], p.cnt["stat_done"].c)
                for k in range(k0, k1):
                    pe.wait_ge(sem["sq_ready"], p.after("sq_ready"))
                    name = "stat_done" if k == n - 1 else "sq_summed"
                    pe.matmul(PM[:, 0, :], ones[:, :], sq[k % 2][:, :], start=k == 0, stop=k == n - 1).then_inc(
                        sem[name], p.counted(name))

            pe.wait_ge(sem["par_ready"], 2)
            sums(0, KT)
            u_base = {"n": 0}

            def u_ready(n, t, s, k):
                if t == 0:
                    pe.wait_ge(sem["u_lo"], u_base["n"] + s * KT + k + 1)

            def u_rhs(k, s):
                o, w = SEGS[s]
                return uh[:, k, o:o + w], ul[:, k, o:o + w]

            drained("read_by_act")
            mark("xbc")

            def turn(tt):
                pe.wait_ge(sem["xs_ready"], 2 * (tt + 1))
                if tt:
                    pe.wait_ge(sem["xt_copied"], tt)
                for c in range(NALL):
                    dst = PM[:, c // 4, (c % 4) * P:(c % 4 + 1) * P]
                    ins = pe.transpose(dst, xs[:, c * P:(c + 1) * P], ident[:, :])
                ins.then_inc(sem["xt_turned"], p.counted("xt_turned"))

            for u in range(N_XBC):
                t_ = S.split % 2
                S.raw += 1
                S.split += 1
                p.skip(f"raw_full{(S.raw - 1) % 2}")
                pe.wait_ge(sem[f"split_full{t_}"], p.after(f"split_full{t_}"))
                for t in range(2):
                    for s in range(3):
                        if u == 0 and t == 0 and s:
                            stats(KT - 1, SEGS[s][1])
                        b = next_bank("read_by_act", 4)
                        w = SEGS[s][1]
                        for k in range(KT):
                            if u == 0 and t == 0:
                                u_ready(0, 0, s, k)
                            o = k * 256 + t * P
                            H, L = wh[t_][:, o:o + P], wl[t_][:, o:o + P]
                            xh, xl = u_rhs(k, s)
                            pe.matmul(PG[:, b, 0:w], H, xh, start=(k == 0), stop=False)
                            pe.matmul(PG[:, b, 0:w], H, xl, start=False, stop=False)
                            ins = pe.matmul(PG[:, b, 0:w], L, xh, start=False, stop=(k == KT - 1))
                        ins.then_inc(sem["group_done"], p.counted("group_done"))
                    if 2 * u + t >= 1:
                        turn(2 * u + t - 1)
            unit(P, 8, 1, range(3), u_rhs, "read_by_act", 4)
            turn(XBT - 1)
            lat = range(2)
            mark("zg")
            for m0 in (16, 32):
                with S.loop(p, 2, 2, per(2, 8, group_done=8, read_by_act=8)) as i:
                    for j in range(2):
                        unit(256, 8, 2, lat, u_rhs, "read_by_act", 4,
                             between=lambda n: later_ada(4 * j + n, i * 16 + (2 * m0 + 2 * (4 * j + n))))
            mark("v")
            for u in range(4):
                t_ = S.split % 2
                S.raw += 1
                S.split += 1
                p.skip(f"raw_full{(S.raw - 1) % 2}")
                pe.wait_ge(sem[f"split_full{t_}"], p.after(f"split_full{t_}"))
                for cc in range(NCH // 2):
                    b = next_bank("read_by_act", 4)
                    for c2 in range(2):
                        c = 2 * cc + c2
                        dst = PG[:, b, c2 * 256:(c2 + 1) * 256]
                        for k in range(KT):
                            H, L = wh[t_][:, k * 256:(k + 1) * 256], wl[t_][:, k * 256:(k + 1) * 256]
                            xh, xl = uh[:, k, c * P:(c + 1) * P], ul[:, k, c * P:(c + 1) * P]
                            pe.matmul(dst, xh, H, start=(k == 0), stop=False)
                            pe.matmul(dst, xl, H, start=False, stop=False)
                            ins = pe.matmul(dst, xh, L, start=False, stop=(k == KT - 1))
                    ins.then_inc(sem["group_done"], p.counted("group_done"))
                if u == 1:
                    pe.wait_ge(sem["acs_loaded"], 16)
                    pe.wait_ge(sem["xt_copied"], XBT)
                    for c in range(NALL):
                        pe.transpose(PM[:, 0, c * 32:(c + 1) * 32], rwq[:, c * P:(c + 1) * P], ident[0:32, 0:32])
                        ins = pe.transpose(PM[:, 1, c * 32:(c + 1) * 32], rwdt[:, c * P:(c + 1) * P], ident[0:32, 0:32])
                    ins.then_inc(sem["tab_turned"], p.counted("tab_turned"))
                if u == 2:
                    pe.wait_ge(sem["tab_dve"], 3)
                    pe.matmul(PM[:, 2, 0:NALL * 32], ones[:, :], dAt[:, :, :].rearrange("p c h -> p (c h)"),
                              start=True, stop=True).then_inc(sem["tot_done"], p.counted("tot_done"))
            assert p.cnt["group_done"].c == GROUPS_SCAN

            def states(s):
                for g in range(2):
                    if p.begun("state_ready", -3):
                        pe.wait_ge(sem["state_ready"], p.so_far("state_ready", -3))
                    p.skip("state_ready")
                    pe.matmul(PG[:, 2 * s + g, :], xtb[s][:, D + g * P:D + (g + 1) * P], xte[:, g * 512:(g + 1) * 512],
                              start=True, stop=True).then_inc(sem["S_done"], p.counted("S_done"))

            drained("read_by_act")
            pe.wait_ge(sem["tab_dve"], 6)
            pe.wait_ge(sem["tab_act"], 2)
            for d in range(2):
                for s in range(NCX):
                    pe.wait_ge(sem[f"step_full{s}"], p.after(f"step_full{s}"))
                    pe.wait_ge(sem["xte_ready"], p.after("xte_ready"))
                    states(s)
                    p.skip("step_done")
                with p.loop(NCH // 2, {"step_full0": 4 - d, "step_full1": 4 - d, "xte_ready": 2, "xdt_ready": 4, "W_ready": 4,
                                       "CE_ready": 4, "sm_ready": 2, "scores_done": 2, "S_done": 4, "state_ready": 4,
                                       "y_done": 4, "y_added": 2, "step_done": 2}) as i:
                    for s in range(2):
                        pe.wait_ge(sem[f"step_full{s}"], p.after(f"step_full{s}", 4 - d))
                        pe.wait_ge(sem["sm_ready"], p.so_far("sm_ready"))
                        p.skip("sm_ready")
                        for g in range(2):
                            ins = pe.matmul(PM[:, 0, g * P:(g + 1) * P], bcT[s][:, g, :], bcT[s][:, 2 + g, :],
                                            start=True, stop=True)
                        ins.then_inc(sem["scores_done"], p.counted("scores_done"))
                        pe.wait_ge(sem["state_ready"], p.so_far("state_ready"))
                        pe.wait_ge(sem["xte_ready"], p.after("xte_ready"))
                        states(s)
                        pe.wait_ge(sem["xdt_ready"], p.after("xdt_ready", 2))
                        for g in range(2):
                            read = ("y_added", "step_done")[g]
                            pe.wait_ge(sem[read], p.so_far(read))
                            p.skip(read)
                            heads = range(8 * g, 8 * g + 8)
                            dst = [PM[h % 2 * HD:h % 2 * HD + HD, 2 + g, (h // 2 % 4) * P:(h // 2 % 4 + 1) * P] for h in range(HEADS)]
                            pe.wait_ge(sem["CE_ready"], p.after("CE_ready"))
                            for h in heads:
                                pe.matmul(dst[h], st[s][:, h * HD:(h + 1) * HD], Eb[s][:, h, :], start=h % 8 < 2, stop=False)
                            pe.wait_ge(sem["W_ready"], p.after("W_ready"))
                            for h in heads:
                                ins = pe.matmul(dst[h], xd[s][g][:, h % 8 * HD:(h % 8 + 1) * HD], Wb[:, h, :], start=False, stop=h % 8 >= 6)
                            ins.then_inc(sem["y_done"], p.counted("y_done"))

            def project(hi, lo, ready, middle=lambda: None, norm_next=False):
                def between(u, n):
                    if u == 0 and n == 1:
                        middle()
                    if u == 3 and norm_next and n in (1, 2):
                        sums(4 * n - 4, 4 * n)

                for u in range(4):
                    unit(256, 8, 2, lat, lambda k, s: (hi[:, k, SEGS[s][0]:SEGS[s][0] + HALF], lo[:, k, SEGS[s][0]:SEGS[s][0] + HALF]),
                         "read_by_dve", 4, ready=ready if u == 0 else None, between=lambda n: between(u, n))

            def y_stats():
                for g in range(2):
                    stats(3)

            y_stats()
            u_base["n"] = 3 * KT
            drained("read_by_dve")
            mark("out")
            project(yh, yl, u_ready, middle=y_stats)
            pe.wait_ge(sem["sg_loaded"], 80)
            drained("read_by_dve")
            mark("sg")
            for g2 in range(2):
                b = next_bank("read_by_dve", 4)
                for q in range(4):
                    ins = pe.transpose(PG[:, b, q * P:(q + 1) * P], uf[g2][:, q * P:(q + 1) * P], ident[:, :])
                ins.then_inc(sem["group_done"], p.counted("group_done"))
            pe.wait_ge(sem["v_ready"], NCH)
            pe.wait_ge(sem["read_by_dve"], p.so_far("read_by_dve"))
            for g in range(KT):
                for s in lat:
                    b = next_bank("read_by_dve", 4)
                    for q in range(4):
                        dst = PG[:, b, q * P:(q + 1) * P]
                        pe.matmul(dst, vln[:, 4 * s + q, g * P:(g + 1) * P], sgwT[:, g, :], start=True, stop=False)
                        ins = pe.matmul(dst, ones[0:1, :], sgb(g), start=False, stop=True)
                    ins.then_inc(sem["group_done"], p.counted("group_done"))
            def sg_ready(n, t, s, k):
                if t == 0:
                    pe.wait_ge(sem["sg_lo"], 2 * k + s + 1)

            project(yh2, yl2, sg_ready, norm_next=True)
            u_base["n"] += 16

            def v_rhs(k, s):
                o, w = SEGS[s]
                return vh[:, k, o:o + w], vl[:, k, o:o + w]

            def h_rhs(j):
                return lambda k, s: (hh[:, k, SEGS[s][0]:SEGS[s][0] + HALF], hl[:, k, SEGS[s][0]:SEGS[s][0] + HALF])

            def mlp(l):
                adas = 6 if l == 0 else 0
                drained("read_by_dve")
                mark(f"mlp{l}")

                def between_1(i, n, first):
                    if first and n == 1:
                        stats(KT - 1)
                    if adas and n >= 8 - adas:
                        later_ada(n - 2, i * 12 + 2 * (n - 2))

                def between_2(n, last):
                    if last and l == 0 and 3 <= n < 7:
                        sums(2 * n - 6, 2 * n - 4)

                def turn(i, first=False, last=False):
                    prev[0] = "read_by_dve"
                    for j in range(2):
                        unit(256, 8, 2, lat, v_rhs, "read_by_act", 4 * j, ready=u_ready if first and j == 0 else None,
                             between=lambda n: between_1(i, 4 * j + n, first))
                    prev[0] = "read_by_act"
                    base = p.cnt["hid_lo"]

                    def hid_ready(n, t, s, k):
                        if t == 0:
                            p.cnt["hid_lo"] = base.plus((k // 2) * 4 + s * 2 + k % 2 + 1)
                            pe.wait_ge(sem["hid_lo"], p.so_far("hid_lo"))

                    for j in range(2):
                        unit(512, 4, 4, lat, h_rhs(j), "read_by_dve", 8 * j, ready=hid_ready if j == 0 else None,
                             between=lambda n: between_2(n, last and j == 1))
                    p.cnt["hid_lo"] = base.plus(8)

                turn(0, first=True)
                with S.loop(p, 6, 4, per(4, adas, group_done=24, read_by_act=8, read_by_dve=16, hid_lo=8)) as i:
                    turn(i + 1)
                turn(7, last=True)
                prev[0] = "read_by_dve"
                u_base["n"] += 16

            mlp(0)
            drained("read_by_act")
            mark("pw1")
            for u in range(2):
                unit(256, 8, 2, lat, v_rhs, "read_by_act", 4, ready=u_ready if u == 0 else None, loads=2,
                     between=lambda n: stats(KT - 1) if u == 0 and n == 1 else None)
            with S.loop(p, 3, 2, {**per(2, 0, group_done=8, read_by_act=8), "raw_full0": 2, "raw_full1": 2}) as i:
                for j in range(2):
                    unit(256, 8, 2, lat, v_rhs, "read_by_act", 4, loads=2)
            for k in range(KT):
                pe.wait_ge(sem["dw_done"], p.after("dw_done"))
                for s in lat:
                    ins = pe.matmul(PM[:, 1 + s, :], ones[:, :], cT[:, k, s * HALF:(s + 1) * HALF], start=k == 0, stop=k == KT - 1)
            ins.then_inc(sem["mean_done"], p.counted("mean_done"))
            sums(0, KT)
            u_base["n"] += 16
            drained("read_by_dve")
            mark("pw2")
            project(vh, vl, u_ready, middle=lambda: stats(KT - 1), norm_next=True)
            u_base["n"] += 16
            mlp(1)
            drained("read_by_act")
            for c in range(NCH):
                if c >= 4:
                    pe.wait_ge(sem["out_dve"], c - 3)
                for k in range(KT):
                    ins = pe.transpose(tok(c)[:, k * P:(k + 1) * P], hT[:, k, c * P:(c + 1) * P], ident[:, :])
                ins.then_inc(sem["tok_turned"], p.counted("tok_turned"))
        def part(w, items, by_pe=False):
            return w, items, by_pe

        def h_parts(g, l, shift, segs, dh, dl):
            got = []
            for s in segs:
                o, w = SEGS[s]
                j = 1 if s == 2 else 0
                src = (lambda k: hcT[:, k, :]) if s == 2 else (lambda k, o=o, w=w: hT[:, k, o:o + w])
                got.append(part(w, [(src(k), gsc[:, g + j, k:k + 1], mod[:, l, shift + k, j:j + 1],
                                     dh[:, k, o:o + w], dl[:, k, o:o + w]) for k in range(KT)], by_pe=s == 0))
            return got

        def y_parts():
            return [part(HALF, [(yT[:, k, s * HALF:(s + 1) * HALF], col("ssd_g", k), None,
                                 yh[:, k, s * HALF:(s + 1) * HALF], yl[:, k, s * HALF:(s + 1) * HALF])
                                for k in range(4 * g, 4 * g + 4)]) for s in range(2) for g in range(2)]

        def c_parts(s):
            return [part(HALF, [(cT[:, k, s * HALF:(s + 1) * HALF], col("ln_g", k), col("ln_b", k),
                                 vh[:, k, s * HALF:(s + 1) * HALF], vl[:, k, s * HALF:(s + 1) * HALF]) for k in range(KT)], by_pe=s == 0)]

        behind_projection = lambda k, s: (k // 2) * 4 + s * 2 + k % 2 + 1
        behind_mlp = lambda k, s: (k // 4) * 8 + s * 4 + k % 4 + 1

        def norm_act(p, act, parts, dim, func=ACT.Identity, behind=None, mods=0):
            for s, (w, items, by_pe) in enumerate(parts):
                for k, it in enumerate(items):
                    if behind:
                        act.wait_ge(sem["read_by_dve"], p.so_far("read_by_dve", behind(k, s) - 16))
                    if by_pe:
                        if k > 1:
                            act.wait_ge(sem["sq_summed"], p.after("sq_summed"))
                        act.activation(sq[k % 2][:, 0:w], it[0], ACT.Square).then_inc(sem["sq_ready"], p.counted("sq_ready"))
                        continue
                    if k:
                        if p.begun("sq_added", -1):
                            act.wait_ge(sem["sq_added"], p.so_far("sq_added", -1))
                        p.skip("sq_added")
                    dst = sq[k % 2] if k else sacc
                    act.activation(dst[:, 0:w], it[0], ACT.Square).then_inc(sem["sq_ready"], p.counted("sq_ready"))
                if by_pe:
                    p.skip("sq_summed")
                act.wait_ge(sem["stat_done"], p.after("stat_done"))
                r = rs[0]
                if mods:
                    act.wait_ge(sem["mod_ready"], mods)
                if p.begun("norm_mul"):
                    act.wait_ge(sem["norm_mul"], p.so_far("norm_mul"))
                act.activation(r[:, 0:w], PM[:, 0, 0:w], ACT.Ln, bias=EPS, scale=1.0 / dim).then_inc(
                    sem["ln_done"], p.counted("ln_done"))
                act.wait_ge(sem["ln_done"], p.so_far("ln_done"))
                act.activation(r[:, 0:w], r[:, 0:w], ACT.Exp, scale=-0.5).then_inc(sem["rstd_ready"], p.counted("rstd_ready"))
                for k, (src, g, b, hi, lo) in enumerate(items):
                    act.wait_ge(sem["norm_mul"], p.after("norm_mul"))
                    if p.begun("u_lo", -1):
                        act.wait_ge(sem["u_lo"], p.so_far("u_lo", -1))
                    p.skip("u_lo")
                    if b is None:
                        act.activation(uf[k % 2][:, 0:w], tm[k % 2][:, 0:w], func, scale=g).then_inc(
                            sem["uf_ready"], p.counted("uf_ready"))
                    else:
                        act.activation(uf[k % 2][:, 0:w], tm[k % 2][:, 0:w], func, scale=g, bias=b).then_inc(
                            sem["uf_ready"], p.counted("uf_ready"))
                    act.wait_ge(sem["uf_ready"], p.so_far("uf_ready"))
                    act.activation(hi, uf[k % 2][:, 0:w], ACT.Copy).then_inc(sem["u_hi"], p.counted("u_hi"))

        def norm_dve(p, dve, parts):
            for w, items, by_pe in parts:
                if by_pe:
                    p.skip("sq_ready", len(items))
                else:
                    dve.wait_ge(sem["sq_ready"], p.after("sq_ready"))
                for k in range(1, 1 if by_pe else len(items)):
                    dve.wait_ge(sem["sq_ready"], p.after("sq_ready"))
                    if k > 1:
                        dve.wait_ge(sem["sq_added"], p.so_far("sq_added"))
                    dve.tensor_tensor(sacc[:, 0:w], sacc[:, 0:w], sq[k % 2][:, 0:w], ALU.add).then_inc(
                        sem["sq_added"], p.counted("sq_added"))
                dve.wait_ge(sem["rstd_ready"], p.after("rstd_ready"))

                def lo_part(k):
                    dve.wait_ge(sem["u_hi"], p.after("u_hi"))
                    hi, lo = items[k][3], items[k][4]
                    dve.tensor_tensor(lo, uf[k % 2][:, 0:w], hi.bitcast(F32), ALU.subtract).then_inc(
                        sem["u_lo"], p.counted("u_lo"))

                for k, it in enumerate(items):
                    if p.begun("uf_ready", -1):
                        dve.wait_ge(sem["uf_ready"], p.so_far("uf_ready", -1))
                    p.skip("uf_ready")
                    dve.tensor_tensor(tm[k % 2][:, 0:w], it[0], rs[0][:, 0:w], ALU.mult).then_inc(
                        sem["norm_mul"], p.counted("norm_mul"))
                    if k:
                        lo_part(k - 1)
                lo_part(len(items) - 1)

        def at(p, name):
            counts, p.bank = marks[name]
            for n, c in counts.items():
                p.cnt[n] = Lin(c)

        @block.scalar
        def _(act):
            p = Program(act, names, mirrored)
            p.bank = 0

            def group(fn):
                b = p.bank
                p.bank = (b + 1) % 4
                act.wait_ge(sem["group_done"], p.after("group_done"))
                return fn(b).then_inc(sem["read_by_act"], p.counted("read_by_act"))

            for blk, q0, k, ap, s0 in place:
                act.dma_start(prow[q0:q0 + k, blk, :], ap[s0:s0 + k]).then_inc(sem["par_loaded"], p.counted("par_loaded"))
            x2, c2 = a["x"][0], a["ctx"][0]
            tok_rows = lambda c: x2[c * P:(c + 1) * P, :] if c < NCH else c2[(c - NCH) * P:(c - NCH + 1) * P, :]
            for c in range(2):
                act.dma_start(xin[c][:, :], tok_rows(c)).then_inc(sem[f"xin_full{c}"], 16)
            rec = a["ssd_a_log"].rearrange("a b h -> (a b h)")
            act.dma_start(alog[:, :], rec.unsqueeze(1)).then_inc(sem["rec_loaded"], p.counted("rec_loaded"))
            act.dma_start(a_bc[:, :], rec.partition_broadcast(P)).then_inc(sem["rec_loaded"], p.counted("rec_loaded"))
            act.dma_start(dtb[:, :], a["ssd_dt_bias"].rearrange("a b h -> (a b h)").unsqueeze(1)).then_inc(
                sem["rec_loaded"], p.counted("rec_loaded"))
            act.dma_start(d_bc[:, :], a["ssd_d"].rearrange("a h -> (a h)").partition_broadcast(P)).then_inc(
                sem["rec_loaded"], p.counted("rec_loaded"))
            act.wait_ge(sem["par_turned"], 1)
            flat = par[:, :, :].rearrange("p b q -> p (b q)")
            act.activation(flat[:, 0:512], PM[:, 0, :], ACT.Copy).then_inc(sem["par_ready"], p.counted("par_ready"))
            act.activation(flat[:, 512:n_rows], PM[:, 1, 0:n_rows - 512], ACT.Copy).then_inc(
                sem["par_ready"], p.counted("par_ready"))
            act.wait_ge(sem["par_ready"], p.so_far("par_ready"))
            act.activation(csil[:, :], col("c", 0, 16), ACT.Silu).then_inc(sem["silu_c"], p.counted("silu_c"))
            for c in range(NALL):
                for hf in range(2):
                    dst = hT[:, 4 * hf:4 * hf + 4, c * P:(c + 1) * P] if c < NCH else \
                        hcT[:, 4 * hf:4 * hf + 4, (c - NCH) * P:(c - NCH + 1) * P]
                    group(lambda b: act.activation(dst, PG[:, b, :].rearrange("p (q t) -> p q t", t=P), ACT.Copy))
                if c + 2 < NALL:
                    act.dma_start(xin[c % 2][:, :], tok_rows(c + 2)).then_inc(sem[f"xin_full{c % 2}"], 16)
            act.wait_ge(sem["read_by_act"], p.so_far("read_by_act"))
            norm_act(p, act, h_parts(0, 0, 0, range(3), uh, ul), D, mods=3)

            at(p, "xbc")
            act.wait_ge(sem["pads_ready"], 2)

            def silu(tt):
                act.wait_ge(sem["conv_done"], tt + 1)
                act.wait_ge(sem["xt_turned"], tt)
                act.wait_ge(sem["xs_stored"], 16 * tt)
                act.activation(xs[:, 0:TOK], cv[:, 0:TOK], ACT.Silu).then_inc(sem["xs_ready"], p.counted("xs_ready"))
                act.activation(xs[:, TOK:ALL], cv[:, TOK + 4:TOK + 4 + CTX], ACT.Silu).then_inc(
                    sem["xs_ready"], p.counted("xs_ready"))
                act.wait_ge(sem["xs_ready"], p.so_far("xs_ready"))
                act.dma_start(xbcT[tt * P:(tt + 1) * P, :], xs[:, :]).then_inc(sem["xs_stored"], p.counted("xs_stored"))

            def store_turned(tt):
                act.wait_ge(sem["xt_copied"], tt + 1)
                act.dma_start(xtokD.rearrange("(c p) n -> p c n", p=P)[:, :, tt * P:(tt + 1) * P], xtk[:, :, :]).then_inc(
                    sem["xt_stored"], p.counted("xt_stored"))

            for tt in range(XBT):
                for s in range(3):
                    o, w = SEGS[s]
                    q = 2 + o + (4 if s == 2 else 0)
                    if s == 0 and tt >= 2:
                        act.wait_ge(sem["conv_done"], tt - 1)
                    group(lambda b: act.activation(xp[tt % 2][:, q:q + w], PG[:, b, 0:w], ACT.Copy))
                    if s == 0 and tt >= 1:
                        silu(tt - 1)
                        if tt >= 2:
                            store_turned(tt - 2)
            silu(XBT - 1)
            store_turned(XBT - 2)
            store_turned(XBT - 1)
            act.wait_ge(sem["xs_stored"], 16 * XBT)
            act.wait_ge(sem["xt_stored"], 16 * XBT)
            act.wait_ge(sem["rec_loaded"], 64)
            for s in range(3):
                o, w = SEGS[s]
                group(lambda b: act.activation(rwx[:, o:o + w], PG[0:R32, b, 0:w], ACT.Identity, bias=dtb[:, 0:1]))
            act.wait_ge(sem["read_by_act"], p.so_far("read_by_act"))
            act.activation(rwe[:, :], rwx[:, :], ACT.Abs).then_inc(sem["row_act"], p.counted("row_act"))
            act.wait_ge(sem["row_act"], p.so_far("row_act"))
            act.activation(rwe[:, :], rwe[:, :], ACT.Exp, scale=-1.0).then_inc(sem["row_act"], p.counted("row_act"))
            act.activation(alog[:, :], alog[:, :], ACT.Exp).then_inc(sem["row_act"], p.counted("row_act"))
            act.activation(a_bc[:, :], a_bc[:, :], ACT.Exp).then_inc(sem["row_act"], p.counted("row_act"))

            def zo_unit(c0, func, dst):
                for n in range(4):
                    b = p.bank
                    act.wait_ge(sem[f"zo_stored{b}"], p.so_far(f"zo_stored{b}"))
                    group(lambda b: act.activation(zo[b][:, :], PG[:, b, :], func))
                    act.wait_ge(sem["read_by_act"], p.so_far("read_by_act"))
                    act.dma_start(*dst(c0, n, b)).then_inc(sem[f"zo_stored{b}"], p.counted(f"zo_stored{b}"))

            def zo_loop(func, dst):
                per = {"group_done": 8, "read_by_act": 8, **{f"zo_stored{b}": 2 for b in range(4)}}
                with p.loop(2, per) as i:
                    for j in range(2):
                        zo_unit(i * 512 + j * 256, func, dst)

            def by_feature(t):
                def dst(c0, n, b):
                    s, q = n // 2, n % 2
                    return t[bass.ds(c0 + q * P, P), s * HALF:(s + 1) * HALF], zo[b][:, :]
                return dst

            zo_loop(ACT.Silu, by_feature(zT))
            zo_loop(ACT.Gelu_apprx_tanh, by_feature(guT))
            act.wait_ge(sem["row_dve"], 3 + 12 + 2 * NALL)
            act.dma_start(acsD[0:HEADS, :], rwx[0:HEADS, :]).then_inc(sem["acs_stored"], p.counted("acs_stored"))
            act.dma_start(acsD[HEADS:2 * HEADS, :], rwe[HEADS:2 * HEADS, :]).then_inc(
                sem["acs_stored"], p.counted("acs_stored"))
            act.wait_ge(sem["acs_stored"], 32)
            act.dma_start(rwq[:, :], acsD[:, :]).then_inc(sem["acs_loaded"], p.counted("acs_loaded"))
            v3 = vtok.rearrange("(c p) n -> p c n", p=P)
            for u in range(4):
                zo_unit(u * 256, ACT.Gelu_apprx_tanh,
                        lambda c0, n, b: (v3[:, 2 * n:2 * n + 2, c0:c0 + 256], zo[b][:, :].rearrange("p (c n) -> p c n", c=2)))
                if u == 2:
                    act.wait_ge(sem["tab_dve"], 5)
                    act.activation(te[:, :, :], te[:, :, :], ACT.Exp).then_inc(sem["tab_act"], p.counted("tab_act"))
                    act.activation(tab[:, :, :, 3, :], PM[:, 2, 0:NALL * R32].rearrange("p (c d h) -> p c d h", d=2, h=HEADS),
                                   ACT.Exp).then_inc(sem["tab_act"], p.counted("tab_act"))
            for d in range(2):
                for s in range(NCX):
                    p.skip(f"step_full{s}")
                    p.skip("scal_ready")
                with p.loop(NCH // 2, {"step_full0": 4 - d, "step_full1": 4 - d, "scal_ready": 2, "y_done": 4, "E_ready": 2,
                                       "seg_ready": 2, "seg1_ready": 2, "D_exp": 4}) as i:
                    for s in range(2):
                        act.wait_ge(sem[f"step_full{s}"], p.after(f"step_full{s}", 4 - d))
                        act.wait_ge(sem["y_done"], p.so_far("y_done", -2))
                        act.activation(Eb[s][:, :, :], Abc[s][:, :, :], ACT.Exp).then_inc(
                            sem["E_ready"], p.counted("E_ready"))
                        act.wait_ge(sem["scal_ready"], p.after("scal_ready"))
                        act.wait_ge(sem["y_done"], p.so_far("y_done", -1))
                        for h in range(8):
                            ins = act.activation(Wb[:, h, :], Abc[s][:, h, :], ACT.Relu, bias=scal[s][:, 0, h:h + 1], scale=-1.0)
                        ins.then_inc(sem["seg_ready"], p.counted("seg_ready"))
                        act.wait_ge(sem["seg_ready"], p.so_far("seg_ready"))
                        v = Wb[:, 0:8, :]
                        act.activation(v, v, ACT.Exp, scale=-1.0).then_inc(sem["D_exp"], p.counted("D_exp"))
                        act.wait_ge(sem["seg1_ready"], p.after("seg1_ready"))
                        v = Wb[:, 8:16, :]
                        act.activation(v, v, ACT.Exp).then_inc(sem["D_exp"], p.counted("D_exp"))
                        p.skip("y_done", 2)
            act.wait_ge(sem["fin_dve"], 2 + NCH)
            norm_act(p, act, y_parts(), D // 2)

            act.wait_ge(sem["u_lo"], p.so_far("u_lo"))
            for q in range(2):
                act.dma_start(uf[q][:, :].rearrange("p (g k) -> p g k", k=P),
                                     a["sg_w"][0, 4 * q:4 * q + 4].rearrange("g q k -> q g k")).then_inc(
                                         sem["sg_loaded"], p.counted("sg_loaded"))
                act.dma_start((sacc, rs[0])[q][0:1, :], a["sg_b"][0, 4 * q:4 * q + 4].rearrange("g q -> (g q)").unsqueeze(0)).then_inc(
                    sem["sg_loaded"], p.counted("sg_loaded"))
            act.dma_start(lnrow[:, :], a["sg_ln_g"].rearrange("a d -> (a d)").partition_broadcast(P)).then_inc(
                sem["sg_loaded"], p.counted("sg_loaded"))
            act.dma_start(vln[:, :, :], v3).then_inc(sem["v_loaded"], p.counted("v_loaded"))
            at(p, "out")
            p.skip("group_done", 16)
            act.wait_ge(sem["v_dve"], 3 * NCH)
            act.activation(rstd[:, :, :], mv[:, :, 1:2], ACT.Ln, bias=EPS).then_inc(sem["v_act"], p.counted("v_act"))
            act.wait_ge(sem["v_act"], p.so_far("v_act"))
            act.activation(rstd[:, :, :], rstd[:, :, :], ACT.Exp, scale=-0.5).then_inc(sem["v_act"], p.counted("v_act"))
            act.wait_ge(sem["v_dve"], 5 * NCH)
            act.dma_start(lnrow[:, :], a["sg_ln_b"].rearrange("a d -> (a d)").partition_broadcast(P)).then_inc(
                sem["sg_loaded"], p.counted("sg_loaded"))
            at(p, "sg")
            p.skip("read_by_dve", 2)
            act.wait_ge(sem["read_by_dve"], p.so_far("read_by_dve"))
            for g in range(KT):
                for s in range(2):
                    if g:
                        act.wait_ge(sem["sg_lo"], 2 * (g - 1) + s + 1)
                    act.dma_start(gu[s][:, :], guT[g * P:(g + 1) * P, s * HALF:(s + 1) * HALF]).then_inc(sem[f"gu_full{s}"], 16)
                for s in range(2):
                    act.wait_ge(sem["read_by_dve"], p.after("read_by_dve"))
                    act.activation(yh2[:, g, s * HALF:(s + 1) * HALF], tm[s][:, :], ACT.Copy).then_inc(
                        sem["sg_hi"], p.counted("sg_hi"))

            def mlp(l):
                at(p, f"mlp{l}")
                norm_act(p, act, h_parts(2 if l == 0 else 4, l, 24, range(2), vh, vl), D, behind=behind_projection, mods=5)
                with p.loop(8, {"group_done": 24, "read_by_act": 8, "relu_sq": 8}) as i:
                    for m in range(8):
                        act.wait_ge(sem["relu_sq"], p.so_far("relu_sq", -1))
                        p.skip("relu_sq")
                        group(lambda b: act.activation(sq[m % 2][:, :], PG[:, b, :], ACT.Relu))
                    p.skip("group_done", 16)
                act.wait_ge(sem["read_by_act"], p.so_far("read_by_act"))

            mlp(0)
            at(p, "pw1")
            norm_act(p, act, h_parts(3, 1, 0, range(2), vh, vl), D, behind=behind_mlp, mods=9)
            def products(k, taps):
                act.wait_ge(sem["glu_done"], 2 * k + 2)
                for t in taps:
                    tap = CW - POOL_TAPS + t
                    if t == 0:
                        if k:
                            act.wait_ge(sem["dw_done"], k)
                    elif k * (POOL_TAPS - 1) + t - 2 > 0:
                        act.wait_ge(sem["prod_added"], k * (POOL_TAPS - 1) + t - 2)
                    dst = prod[t % 2] if t else pacc
                    act.activation(dst[:, :], apad[k % 2][:, tap:tap + TOK], ACT.Copy, scale=col("w_dw", tap * KT + k)).then_inc(
                        sem["prod_ready"], p.counted("prod_ready"))

            for k in range(KT + 1):
                for s in range(2):
                    if k:
                        products(k - 1, range(5 * s, 5 + (POOL_TAPS - 5) * s))
                    if k == KT:
                        continue
                    m = 2 * k + s
                    if m >= 1:
                        act.wait_ge(sem["glu_done"], m)
                    group(lambda b: act.activation(tm[0][:, :], PG[:, b, :], ACT.Identity, bias=col("b_pw1", k)))
                    group(lambda b: act.activation(tm[1][:, :], PG[:, b, :], ACT.Sigmoid, bias=col("b_pw1", KT + k)))
            for s in range(2):
                act.wait_ge(sem["ln_dve"], KT * (s + 1))
                norm_act(p, act, c_parts(s), D, ACT.Silu)
            mlp(1)
            act.wait_ge(sem["tok_turned"], 1)
            act.dma_start(fg[:, :], a["final_norm_g"].partition_broadcast(P)).then_inc(
                sem["fg_loaded"], p.counted("fg_loaded"))
            for c in range(NCH):
                act.wait_ge(sem["tok_turned"], c + 1)
                if c:
                    act.wait_ge(sem["out_act"], p.so_far("out_act"))
                act.activation(fs[:, :], tok(c), ACT.Square, accum_out=fm[:, c, :]).then_inc(
                    sem["out_act"], p.counted("out_act"))
                if c % 4 == 3:
                    v = fm[:, c - 3:c + 1, :]
                    act.wait_ge(sem["out_act"], p.so_far("out_act"))
                    act.activation(v, v, ACT.Ln, bias=EPS, scale=1.0 / D).then_inc(sem["out_act"], p.counted("out_act"))
                    act.wait_ge(sem["out_act"], p.so_far("out_act"))
                    act.activation(v, v, ACT.Exp, scale=-0.5).then_inc(sem["out_act"], p.counted("out_act"))

        @block.vector
        def _(dve):
            p = Program(dve, names, mirrored)
            p.bank = 0

            def group(fn):
                b = p.bank
                p.bank = (b + 1) % 4
                dve.wait_ge(sem["group_done"], p.after("group_done"))
                return fn(b).then_inc(sem["read_by_dve"], p.counted("read_by_dve"))

            def add_ada(l, t0, n, nj=1):
                src = PM[:, 3, 2 * t0:2 * (t0 + n)].rearrange("p (t j) -> p t j", j=2)[:, :, 0:nj]
                b = col("ada_b", l * 48 + t0, n).unsqueeze(2).to_broadcast([P, n, nj])
                dve.tensor_tensor(mod[:, l, t0:t0 + n, 0:nj], src, b, ALU.add).then_inc(
                    sem["mod_ready"], p.counted("mod_ready"))
                dve.wait_ge(sem["mod_ready"], p.so_far("mod_ready"))

            def later_ada(q):
                s = q % 2
                dve.wait_ge(sem[f"ada_full{s}"], p.after(f"ada_full{s}"))
                v = adaw[s][:, :].rearrange("p (k c) -> p k c", c=P)
                dve.tensor_tensor(v, v, csil[:, 0:KT].unsqueeze(2).to_broadcast([P, KT, P]), ALU.mult).then_inc(
                    sem["ada_step"], p.counted("ada_step"))
                for n in (4, 2, 1):
                    dve.wait_ge(sem["ada_step"], p.so_far("ada_step"))
                    name = "ada_step" if n > 1 else "ada_added"
                    dve.tensor_tensor(v[:, 0:n], v[:, 0:n], v[:, n:2 * n], ALU.add).then_inc(sem[name], p.counted(name))

            def gain(idx, l, t0, j, g):
                dve.scalar_tensor_tensor(out=gsc[:, idx, :], in0=mod[:, l, t0:t0 + KT, j], scalar=1.0, in1=g,
                                                op0=ALU.add, op1=ALU.mult).then_inc(sem["mod_ready"], p.counted("mod_ready"))

            dve.wait_ge(sem["par_ready"], 2)
            for s in range(2):
                dve.wait_ge(sem[f"raw_empty{s}"], 1 + N_ADA0 // 2)
            add_ada(0, 0, 16, 2)
            gain(0, 0, 8, 0, col("mix_g", 0, KT))
            gain(1, 0, 8, 1, col("mix_g", 0, KT))
            dve.wait_ge(sem["rec_loaded"], 64)
            for q in range(2):
                v = slice(q * HD, (q + 1) * HD)
                dve.tensor_copy(dsk[v, :], d_bc[v, q:HEADS:2]).then_inc(sem["skip_ready"], p.counted("skip_ready"))
            norm_dve(p, dve, h_parts(0, 0, 0, range(3), uh, ul))

            at(p, "xbc")
            for q in range(2):
                dve.memset(xp[q][:, :], 0.0).then_inc(sem["pads_ready"], p.counted("pads_ready"))

            def copy_turned(tt):
                dve.wait_ge(sem["xt_turned"], tt + 1)
                if tt:
                    dve.wait_ge(sem["xt_stored"], 16 * tt)
                dve.tensor_copy(xtk[:, :, :].rearrange("p c t -> p (c t)"),
                                       PM[:, 0:3, :].rearrange("p b n -> p (b n)")[:, 0:ALL]).then_inc(
                                           sem["xt_copied"], p.counted("xt_copied"))

            for tt in range(XBT):
                p.skip("read_by_act", 3)
                dve.wait_ge(sem["read_by_act"], p.so_far("read_by_act"))
                n = PADW - 4
                if tt:
                    dve.wait_ge(sem["xs_ready"], 2 * tt)
                dve.tensor_scalar(cv[:, 0:n], xp[tt % 2][:, 0:n], col("conv_w", tt), col("conv_b", tt), ALU.mult, ALU.add).then_inc(
                    sem["conv_step"], p.counted("conv_step"))
                for tap in range(1, CONV):
                    dve.wait_ge(sem["conv_step"], p.so_far("conv_step"))
                    dve.scalar_tensor_tensor(out=cv[:, 0:n], in0=xp[tt % 2][:, tap:tap + n],
                                                    scalar=col("conv_w", tap * XBT + tt), in1=cv[:, 0:n], op0=ALU.mult,
                                                    op1=ALU.add).then_inc(
                                                        sem["conv_done" if tap == CONV - 1 else "conv_step"], p.counted("conv_done" if tap == CONV - 1 else "conv_step"))
                if tt:
                    copy_turned(tt - 1)
            copy_turned(XBT - 1)

            with p.loop(2, {"ada_full0": 4, "ada_full1": 4, "ada_step": 24, "ada_added": 8}) as i:
                for q in range(8):
                    later_ada(q)
            dve.wait_ge(sem["row_act"], 4)

            def row(ins):
                ins.then_inc(sem["row_dve"], p.counted("row_dve"))
                dve.wait_ge(sem["row_dve"], p.so_far("row_dve"))

            row(dve.tensor_scalar(rwq[:, :], rwe[:, :], 2.0, None, ALU.add))
            row(dve.reciprocal(rwq[:, :], rwq[:, :]))
            later_ada(0)
            row(dve.tensor_tensor(rwe[:, :], rwe[:, :], rwq[:, :], ALU.mult))
            row(dve.tensor_tensor(rwq[:, :], rwe[:, :], rwe[:, :], ALU.mult))
            later_ada(1)
            row(dve.tensor_scalar(rwp[:, :], rwq[:, :], 1.0 / 13, None, ALU.mult))
            for q, n in enumerate((11, 9, 7, 5, 3)):
                row(dve.scalar_tensor_tensor(out=rwp[:, :], in0=rwp[:, :], scalar=1.0 / n, in1=rwq[:, :], op0=ALU.add, op1=ALU.mult))
                later_ada(2 + q)
            row(dve.scalar_tensor_tensor(out=rwp[:, :], in0=rwp[:, :], scalar=1.0, in1=rwe[:, :], op0=ALU.add, op1=ALU.mult))
            later_ada(7)
            row(dve.tensor_scalar(rwx[:, :], rwx[:, :], 0.0, None, ALU.max))
            later_ada(8)
            row(dve.scalar_tensor_tensor(out=rwdt[:, :], in0=rwp[:, :], scalar=2.0, in1=rwx[:, :], op0=ALU.mult, op1=ALU.add))
            later_ada(9)
            row(dve.tensor_scalar(rwp[:, :], rwdt[:, :], alog[:, 0:1], -1.0, ALU.mult, ALU.mult))
            row(dve.tensor_scalar(a_bc[:, :], a_bc[:, :], -1.0, None, ALU.mult))
            later_ada(10)
            for c in range(NALL):
                v = slice(c * P, (c + 1) * P)
                if c % 2 == 1:
                    later_ada(11 + c // 2)
                dve.tensor_tensor_scan(rwx[:, v], ones[0:R32, :], rwp[:, v], 0.0, ALU.mult, ALU.add).then_inc(
                    sem["row_dve"], p.counted("row_dve"))
                dve.tensor_tensor_scan(rwe[:, v][:, ::-1], ones[0:R32, :], rwp[:, v][:, ::-1], 0.0, ALU.mult, ALU.add).then_inc(
                    sem["row_dve"], p.counted("row_dve"))

            for s in range(2):
                dve.wait_ge(sem[f"ada_empty{s}"], ADA_FREED[0])
            add_ada(0, 16, 32)
            gain(2, 0, 32, 0, col("mlp_g", 0, KT))

            dve.wait_ge(sem["tab_turned"], 1)
            view = lambda b: PM[:, b, 0:NALL * R32].rearrange("p (c d h) -> p c d h", d=2, h=HEADS)
            te4 = te[:, :, :].rearrange("p c (d h) -> p c d h", h=HEADS)
            dve.tensor_copy(tab[:, :, :, 0, :], view(0)).then_inc(sem["tab_dve"], p.counted("tab_dve"))
            dve.tensor_copy(tab[:, :, :, 1, :], view(1)).then_inc(sem["tab_dve"], p.counted("tab_dve"))
            dve.wait_ge(sem["tab_dve"], p.so_far("tab_dve"))
            dve.tensor_tensor(dAt[:, :, :], PM[:, 1, 0:NALL * R32].rearrange("p (c h) -> p c h", h=R32),
                                     a_bc[:, :].unsqueeze(1).to_broadcast([P, NALL, R32]), ALU.mult).then_inc(
                                         sem["tab_dve"], p.counted("tab_dve"))
            dve.wait_ge(sem["tot_done"], p.after("tot_done"))
            dve.tensor_tensor(te4, view(2), tab[:, :, :, 0, :], ALU.subtract).then_inc(sem["tab_dve"], p.counted("tab_dve"))
            dve.wait_ge(sem["tab_dve"], p.so_far("tab_dve"))
            dve.tensor_scalar(te[:, :, :], te[:, :, :], 0.0, None, ALU.min).then_inc(sem["tab_dve"], p.counted("tab_dve"))
            dve.wait_ge(sem["tab_act"], p.after("tab_act", 2))
            dve.tensor_tensor(tab[:, :, :, 2, :], te4, tab[:, :, :, 1, :], ALU.mult).then_inc(
                sem["tab_dve"], p.counted("tab_dve"))
            dve.wait_ge(sem["tab_dve"], p.so_far("tab_dve"))

            wide = lambda t: t[:, :].rearrange("p (h q) -> p h q", q=HD)

            def scalars(s, c, d):
                src = tab[:, c:c + 1, d, :, :] if isinstance(c, int) else tab[:, bass.ds(c, 1), d, :, :]
                dve.wait_ge(sem["step_done"], p.so_far("step_done"))
                dve.wait_ge(sem["par_ready"], 2)
                dve.tensor_copy(scal[s][:, :, :].unsqueeze(1), src).then_inc(sem["scal_ready"], p.counted("scal_ready"))
                dve.wait_ge(sem["scal_ready"], p.so_far("scal_ready"))

            def prepare(s, c, d):
                dve.wait_ge(sem[f"step_full{s}"], p.after(f"step_full{s}", 4 - d))
                scalars(s, c, d)
                for g in range(2):
                    dve.tensor_tensor(wide(xd[s][g]), xtb[s][:, g * 512:(g + 1) * 512].rearrange("p (h q) -> p h q", q=HD),
                                      scal[s][:, 1, g * 8:(g + 1) * 8].unsqueeze(2).to_broadcast([P, 8, HD]),
                                      ALU.mult).then_inc(sem["xdt_ready"], p.counted("xdt_ready"))

            def weights(s, mask):
                for h in range(8, HEADS):
                    ins = dve.tensor_scalar(Wb[:, h, :], Abc[s][:, h, :], scal[s][:, 0, h:h + 1], 0.0, ALU.subtract, ALU.min)
                ins.then_inc(sem["seg1_ready"], p.counted("seg1_ready"))
                dve.wait_ge(sem["scores_done"], p.after("scores_done"))
                dve.tensor_tensor(sm[:, :, :], PM[:, 0, 0:2 * P].rearrange("p (g t) -> p g t", t=P),
                                  mask[:, :].unsqueeze(1).to_broadcast([P, 2, P]), ALU.mult).then_inc(
                                      sem["sm_ready"], p.counted("sm_ready"))
                dve.wait_ge(sem["sm_ready"], p.so_far("sm_ready"))
                for g in range(2):
                    v = Wb[:, g * 8:(g + 1) * 8, :]
                    dve.wait_ge(sem["D_exp"], p.after("D_exp"))
                    dve.tensor_tensor(v, v, sm[:, g:g + 1, :].to_broadcast([P, 8, P]), ALU.mult).then_inc(
                        sem["W_ready"], p.counted("W_ready"))

            def next_state(s, first, lat=True):
                if not first:
                    dve.tensor_tensor(wide(st[1 - s]), wide(st[s]), scal[s][:, 3, :].unsqueeze(2).to_broadcast([P, HEADS, HD]),
                                      ALU.mult).then_inc(sem["state_mul"], p.counted("state_mul"))
                for g in range(2):
                    v = st[1 - s][:, g * 512:(g + 1) * 512]
                    if lat and g == 1:
                        dve.wait_ge(sem["CE_ready"], p.after("CE_ready", 2))
                    dve.wait_ge(sem["S_done"], p.after("S_done"))
                    if first:
                        dve.tensor_copy(v, PG[:, 2 * s + g, :]).then_inc(sem["state_ready"], p.counted("state_ready"))
                    else:
                        dve.wait_ge(sem["state_mul"], p.so_far("state_mul"))
                        dve.tensor_tensor(v, v, PG[:, 2 * s + g, :], ALU.add).then_inc(
                            sem["state_ready"], p.counted("state_ready"))

            def add_y(s, c, d):
                for g, read in enumerate(("y_added", "step_done")):
                    v = yT[:, 4 * g:4 * g + 4, c * P:(c + 1) * P] if isinstance(c, int) else yT[:, 4 * g:4 * g + 4, bass.ds(c * P, P)]
                    dve.wait_ge(sem["y_done"], p.after("y_done"))
                    y = PM[:, 2 + g, :].rearrange("p (t q) -> p t q", q=P)
                    if d == 0:
                        for t in range(4):
                            k = 4 * g + t
                            ins = dve.scalar_tensor_tensor(out=v[:, t, :], in0=prod[s][:, k * P:(k + 1) * P], scalar=dsk[:, k:k + 1],
                                                           in1=y[:, t, :], op0=ALU.mult, op1=ALU.add)
                        ins.then_inc(sem[read], p.counted(read))
                    else:
                        dve.tensor_tensor(v, v, y, ALU.add).then_inc(sem[read], p.counted(read))

            def finish(s, c):
                toks = slice(c * P, (c + 1) * P) if isinstance(c, int) else bass.ds(c * P, P)
                dve.wait_ge(sem[f"z_full{s}"], p.after(f"z_full{s}"))
                dve.wait_ge(sem["step_done"], p.so_far("step_done"))
                v = yT[:, :, toks]
                dve.tensor_tensor(v, v, prod[s][:, :].rearrange("p (k t) -> p k t", t=P), ALU.mult).then_inc(
                    sem["fin_dve"], p.counted("fin_dve"))

            dve.wait_ge(sem["skip_ready"], p.so_far("skip_ready"))
            for d in range(2):
                mask = maskF if d == 0 else maskB
                chunk = lambda n: n if d == 0 else n * -1 + (NCH - 1)
                for s in range(NCX):
                    c = NCH + (s if d == 0 else NCX - 1 - s)
                    dve.wait_ge(sem[f"step_full{s}"], p.after(f"step_full{s}"))
                    scalars(s, c, d)
                    next_state(s, s == 0, lat=False)
                    dve.wait_ge(sem["state_ready"], p.so_far("state_ready"))
                    dve.tensor_copy(scal[s][:, 0:1, 0:1], scal[s][:, 0:1, 0:1]).then_inc(
                        sem["step_done"], p.counted("step_done"))
                prepare(0, chunk(0), d)

                def step(s, n, last=False, fin=True):
                    weights(s, mask)
                    next_state(s, False)
                    if not last:
                        prepare(1 - s, chunk(n + 1), d)
                    if d == 1 and fin:
                        finish(1 - s, chunk(n + -1))
                    add_y(s, chunk(n), d)

                if d == 1:
                    step(0, 0, fin=False)
                    step(1, 1)
                with p.loop(NCH // 2 - 1 - d, {"step_full0": 4 - d, "step_full1": 4 - d, "scal_ready": 2, "xdt_ready": 4, "D_exp": 4,
                                               "CE_ready": 4, "seg1_ready": 2, "scores_done": 2, "sm_ready": 2, "W_ready": 4, "state_mul": 2, "S_done": 4,
                                               "state_ready": 4, "y_done": 4, "y_added": 2, "step_done": 2,
                                               "fin_dve": 2 * d, "z_full0": d, "z_full1": d}) as i:
                    for s in range(2):
                        step(s, i * 2 + (s + 2 * d))
                step(0, NCH - 2)
                step(1, NCH - 1, last=True)
            finish(1, 0)
            dve.wait_ge(sem["fin_dve"], p.so_far("fin_dve"))
            norm_dve(p, dve, y_parts())

            def add_to_h(k, s, l, t0, b):
                o = s * HALF
                return dve.scalar_tensor_tensor(out=hT[:, k, o:o + HALF], in0=PG[:, b, :], scalar=mod[:, l, t0 + k, 0:1],
                                                in1=hT[:, k, o:o + HALF], op0=ALU.mult, op1=ALU.add)

            def out_proj(l, t0, between=lambda u, n: None):
                for u in range(4):
                    for s in range(2):
                        for t in range(2):
                            group(lambda b: add_to_h(2 * u + t, s, l, t0, b))
                            between(u, 2 * s + t)

            def v_stats(c):
                if c == 0:
                    dve.wait_ge(sem["v_loaded"], 16)
                for q in range(2):
                    if c or q:
                        dve.wait_ge(sem["v_dve"], p.so_far("v_dve"))
                    dve.bn_stats(bst[:, q, :], vln[:, c, q * 512:(q + 1) * 512]).then_inc(sem["v_dve"], p.counted("v_dve"))
                dve.wait_ge(sem["v_dve"], p.so_far("v_dve"))
                dve.bn_aggr(mv[:, c, :], bst[:, :, :]).then_inc(sem["v_dve"], p.counted("v_dve"))

            def v_scale(c):
                if c == 0:
                    dve.wait_ge(sem["v_act"], 2)
                    dve.wait_ge(sem["sg_loaded"], 80)
                dve.tensor_scalar(vln[:, c, :], vln[:, c, :], mv[:, c, 0:1], rstd[:, c, 0:1], ALU.subtract, ALU.mult).then_inc(
                    sem["v_dve"], p.counted("v_dve"))
                dve.wait_ge(sem["v_dve"], p.so_far("v_dve"))
                dve.tensor_tensor(vln[:, c, :], vln[:, c, :], lnrow[:, :], ALU.mult).then_inc(
                    sem["v_dve"], p.counted("v_dve"))

            def v_shift(c):
                if c == 0:
                    dve.wait_ge(sem["sg_loaded"], 96)
                    dve.wait_ge(sem["v_dve"], p.so_far("v_dve"))
                dve.tensor_tensor(vln[:, c, :], vln[:, c, :], lnrow[:, :], ALU.add).then_inc(
                    sem["v_ready"], p.counted("v_ready"))

            def v_norm(u, n):
                for c in (2 * n, 2 * n + 1):
                    if u:
                        (v_stats, v_scale, v_shift)[u - 1](c)

            at(p, "out")
            out_proj(0, 16, between=v_norm)
            at(p, "sg")
            for q in range(2):
                group(lambda b: dve.tensor_copy(sgwT[:, 4 * q:4 * q + 4, :].rearrange("p g k -> p (g k)"), PG[:, b, :]))
            for g in range(KT):
                for s in range(2):
                    dve.wait_ge(sem[f"gu_full{s}"], p.after(f"gu_full{s}"))
                    group(lambda b: dve.tensor_tensor(tm[s][:, :], PG[:, b, :], gu[s][:, :], ALU.mult))
                    dve.wait_ge(sem["sg_hi"], p.after("sg_hi"))
                    dve.tensor_tensor(yl2[:, g, s * HALF:(s + 1) * HALF], tm[s][:, :],
                                             yh2[:, g, s * HALF:(s + 1) * HALF].bitcast(F32), ALU.subtract).then_inc(
                                                 sem["sg_lo"], p.counted("sg_lo"))
            out_proj(0, 16)
            dve.wait_ge(sem["read_by_dve"], p.so_far("read_by_dve"))

            def mlp(l):
                norm_dve(p, dve, h_parts(2 if l == 0 else 4, l, 24, range(2), vh, vl))
                dve.wait_ge(sem["u_lo"], p.so_far("u_lo"))
                at(p, f"mlp{l}")
                with p.loop(8, {"group_done": 24, "read_by_act": 8, "read_by_dve": 16, "relu_sq": 8, "hid_hi": 8, "hid_lo": 8,
                                **({"ada_full0": 3, "ada_full1": 3, "ada_step": 18, "ada_added": 6} if l == 0 else {})}) as i:
                    for m in range(8):
                        if l == 0 and m >= 2:
                            later_ada(m - 2)
                        t, o = (m // 4) * 2 + m % 2, (m // 2 % 2) * HALF
                        dve.wait_ge(sem["read_by_act"], p.after("read_by_act"))
                        if m:
                            dve.wait_ge(sem["hid_lo"], p.so_far("hid_lo"))
                        dve.tensor_tensor(uf[0][:, :], sq[m % 2][:, :], sq[m % 2][:, :], ALU.mult).then_inc(
                            sem["relu_sq"], p.counted("relu_sq"))
                        dve.wait_ge(sem["relu_sq"], p.so_far("relu_sq"))
                        hi, lo = hh[:, t, o:o + HALF], hl[:, t, o:o + HALF]
                        dve.tensor_copy(hi, uf[0][:, :]).then_inc(sem["hid_hi"], p.counted("hid_hi"))
                        dve.wait_ge(sem["hid_hi"], p.so_far("hid_hi"))
                        dve.tensor_tensor(lo, uf[0][:, :], hi.bitcast(F32), ALU.subtract).then_inc(
                            sem["hid_lo"], p.counted("hid_lo"))
                    p.skip("group_done", 8)
                    for j in range(2):
                        for s in range(2):
                            for t in range(4):
                                group(lambda b: add_to_h(4 * j + t, s, l, 40, b))
                dve.wait_ge(sem["read_by_dve"], p.so_far("read_by_dve"))

            mlp(0)
            for s in range(2):
                dve.wait_ge(sem[f"ada_empty{s}"], ADA_FREED[1])
            add_ada(1, 0, 48)
            gain(3, 1, 8, 0, col("mix_g", KT, KT))
            gain(4, 1, 32, 0, col("mlp_g", KT, KT))
            dve.tensor_tensor(gb[:, :], mod[:, 1, 16:24, 0], col("b_pw2", 0, KT), ALU.mult).then_inc(
                sem["mod_ready"], p.counted("mod_ready"))
            dve.memset(apad[0][:, :], 0.0).then_inc(sem["mod_ready"], p.counted("mod_ready"))
            dve.memset(apad[1][:, :], 0.0).then_inc(sem["mod_ready"], p.counted("mod_ready"))
            norm_dve(p, dve, h_parts(3, 1, 0, range(2), vh, vl))
            at(p, "pw1")
            for k in range(KT):
                for s in range(2):
                    dve.wait_ge(sem["read_by_act"], p.after("read_by_act", 2))
                    o = CW // 2 + s * HALF
                    dve.tensor_tensor(apad[k % 2][:, o:o + HALF], tm[0][:, :], tm[1][:, :], ALU.mult).then_inc(
                        sem["glu_done"], p.counted("glu_done"))
                dve.wait_ge(sem["glu_done"], p.so_far("glu_done"))
                dve.tensor_scalar(cT[:, k, :], apad[k % 2][:, 0:TOK], col("w_dw", k), col("b_dw", k), ALU.mult, ALU.add).then_inc(
                    sem["dw_step"], p.counted("dw_step"))
                for tap in range(1, CW - POOL_TAPS):
                    dve.wait_ge(sem["dw_step"], p.so_far("dw_step"))
                    dve.scalar_tensor_tensor(out=cT[:, k, :], in0=apad[k % 2][:, tap:tap + TOK],
                                                    scalar=col("w_dw", tap * KT + k), in1=cT[:, k, :], op0=ALU.mult,
                                                    op1=ALU.add).then_inc(sem["dw_step"], p.counted("dw_step"))
                dve.wait_ge(sem["dw_step"], p.so_far("dw_step"))
                dve.wait_ge(sem["prod_added"], (POOL_TAPS - 1) * (k + 1))
                dve.tensor_tensor(cT[:, k, :], cT[:, k, :], pacc[:, :], ALU.add).then_inc(
                    sem["dw_done"], p.counted("dw_done"))
            dve.wait_ge(sem["mean_done"], p.after("mean_done"))
            for s in range(2):
                o = s * HALF
                src = lambda k: cT[:, k, o:o + HALF]
                for k in range(KT):
                    dve.scalar_tensor_tensor(out=src(k), in0=PM[:, 1 + s, :], scalar=-1.0 / D, in1=src(k), op0=ALU.mult,
                                                    op1=ALU.add).then_inc(sem["ln_dve"], p.counted("ln_dve"))
                norm_dve(p, dve, c_parts(s))
            for k in range(KT):
                dve.tensor_scalar(hT[:, k, :], hT[:, k, :], gb[:, k:k + 1], None, ALU.add).then_inc(
                    sem["bias_added"], p.counted("bias_added"))
            dve.wait_ge(sem["bias_added"], p.so_far("bias_added"))
            at(p, "pw2")
            out_proj(1, 16)
            dve.wait_ge(sem["read_by_dve"], p.so_far("read_by_dve"))
            mlp(1)
            dve.wait_ge(sem["fg_loaded"], 16)
            for c in range(NCH):
                dve.wait_ge(sem["out_act"], 6 * (c // 4 + 1))
                if c >= 4:
                    dve.wait_ge(sem[f"out_stored{c % 4}"], 16 * (c // 4))
                dve.scalar_tensor_tensor(out=fo[c % 4][:, :], in0=tok(c),
                                         scalar=fm[:, c, 0:1], in1=fg[:, :], op0=ALU.mult,
                                         op1=ALU.mult).then_inc(sem["out_dve"], p.counted("out_dve"))


_INS = ["x", "c", "ctx", "c_ctx", "ada_w", "ada_b", "norm_mix_g", "norm_mlp_g", "mlp_w1", "mlp_w2",
        "hy_w_in", "ssd_conv_w", "ssd_conv_b", "ssd_dt_bias", "ssd_a_log", "ssd_d", "ssd_norm_g",
        "sg_ln_g", "sg_ln_b", "sg_w", "sg_b", "hy_w_out", "cf_w_pw1", "cf_b_pw1", "cf_w_dw", "cf_b_dw",
        "cf_ln_g", "cf_ln_b", "cf_w_pw2", "cf_b_pw2", "final_norm_g"]


def kernel(**inputs):
    import numpy as _np
    import concourse.bacc as _bacc
    from concourse import mybir as _mybir
    from concourse.bass_utils import run_bass_kernel_spmd as _run

    nc = _bacc.Bacc("TRN2", target_bir_lowering=False, num_devices=1)
    arrays, aps = {}, {}
    for name in _INS:
        v = _np.ascontiguousarray(inputs[name])
        arrays[f"in_{name}"] = v
        aps[name] = nc.dram_tensor(f"in_{name}", v.shape, _mybir.dt.from_np(v.dtype), kind="ExternalInput").ap()
    out = nc.dram_tensor("out_0", (1, TOK, D), _mybir.dt.float32, kind="ExternalOutput").ap()
    build(nc, aps, out)
    r = _run(nc, [arrays], core_ids=[0])
    return r.results[0]["out_0"]
```
